# Optimizing a Trainium2 kernel written in Bass

```python
import jax, jax.numpy as jnp
from jax import lax
import numpy as np

D_MODEL = 1024
BATCH = 1
SEQ = 256
DEPTH = 1

CHUNK = 64
N_MEM = 256
EPS = 1e-6
ROPE_THETA = 10000.0
RET_HEADS = 4
RET_DK = 64
RET_DV = 128
SWA_HEADS = 4
SWA_KV_HEADS = 2
SWA_DH = 64
SWA_WINDOW = 128
SWA_WIN_CHUNKS = SWA_WINDOW // CHUNK
MEM_HEADS = 4
MEM_DH = 64
N_EXPERTS = 32
TOP_K = 4
D_EXPERT = D_MODEL
SWIGLU_LIMIT = 7.0
SWIGLU_ALPHA = 1.702
MOE_BLOCK = 256

RET_QK_W = RET_HEADS * RET_DK
RET_V_W = RET_HEADS * RET_DV
SWA_Q_W = SWA_HEADS * SWA_DH
SWA_KV_W = SWA_KV_HEADS * SWA_DH
MEM_Q_W = MEM_HEADS * MEM_DH
MEM_KV_W = 2 * MEM_HEADS * MEM_DH
MIX_WIDTH = RET_V_W + SWA_Q_W + MEM_Q_W
IN_SPLITS = (RET_QK_W, RET_QK_W, RET_V_W, RET_V_W, SWA_Q_W, SWA_KV_W, SWA_KV_W, MEM_Q_W)
IN_WIDTH = RET_QK_W * 2 + RET_V_W * 2 + SWA_Q_W + SWA_KV_W * 2 + MEM_Q_W

kernel_name = "hybrid_retention_swa_memory_moe_block"

def rms_norm(x, g):
    xf = x.astype(jnp.float32)
    y = xf * lax.rsqrt(jnp.mean(xf * xf, axis=-1, keepdims=True) + EPS)
    return (y * g.astype(jnp.float32)).astype(x.dtype)

def rope_tables(positions, dim):
    inv = ROPE_THETA ** (-jnp.arange(0, dim, 2, dtype=jnp.float32) / dim)
    ang = positions.astype(jnp.float32)[..., None] * inv
    return jnp.cos(ang), jnp.sin(ang)

def apply_rope(x, cos, sin):
    x1, x2 = jnp.split(x.astype(jnp.float32), 2, axis=-1)
    c = cos[:, :, None, :]
    s = sin[:, :, None, :]
    return jnp.concatenate([x1 * c - x2 * s, x2 * c + x1 * s], axis=-1).astype(x.dtype)

def retention(q, k, v, g, positions):
    B, S = q.shape[0], q.shape[1]
    nc = S // CHUNK
    f32 = jnp.float32
    cos, sin = rope_tables(positions, RET_DK)
    q = apply_rope(q, cos, sin).astype(f32)
    k = apply_rope(k, cos, sin).astype(f32) * (RET_DK ** -0.5)
    log_gamma = jnp.log1p(-(2.0 ** (-5.0 - jnp.arange(RET_HEADS, dtype=f32))))
    idx = jnp.arange(CHUNK, dtype=f32)
    intra = jnp.exp(log_gamma[:, None, None] * jnp.abs(idx[:, None] - idx[None, :]))
    q_dec = jnp.exp(log_gamma[:, None] * (idx + 1.0)[None, :]).T
    k_dec = jnp.exp(log_gamma[:, None] * (CHUNK - 1.0 - idx)[None, :]).T
    chunk_dec = jnp.exp(log_gamma * CHUNK)
    qc = q.reshape(B, nc, CHUNK, RET_HEADS, RET_DK)
    kc = k.reshape(B, nc, CHUNK, RET_HEADS, RET_DK)
    vc = v.astype(f32).reshape(B, nc, CHUNK, RET_HEADS, RET_DV)
    scores = jnp.einsum('bnihd,bnjhd->bnhij', qc, kc) * intra
    o_intra = jnp.einsum('bnhij,bnjhe->bnihe', scores, vc)
    kv = jnp.einsum('bnjhd,bnjhe->bnhde', kc * k_dec[None, None, :, :, None], vc)

    def step(state, kv_n):
        return state * chunk_dec[None, :, None, None] + kv_n, state

    _, prev = lax.scan(step, jnp.zeros((B, RET_HEADS, RET_DK, RET_DV), f32), jnp.moveaxis(kv, 1, 0))
    prev = jnp.moveaxis(prev, 0, 1)
    o_inter = jnp.einsum('bnihd,bnhde->bnihe', qc * q_dec[None, None, :, :, None], prev)
    o = (o_intra + o_inter).reshape(B, S, RET_HEADS, RET_DV)
    o = o * lax.rsqrt(jnp.mean(o * o, axis=-1, keepdims=True) + EPS)
    o = jax.nn.silu(g.astype(f32)) * o
    return o.reshape(B, S, RET_V_W).astype(v.dtype)

def sliding_window_attention(q, k, v, q_gain, k_gain, sinks, positions):
    B, S = q.shape[0], q.shape[1]
    nc = S // CHUNK
    grp = SWA_HEADS // SWA_KV_HEADS
    f32 = jnp.float32
    cos, sin = rope_tables(positions, SWA_DH)
    q = apply_rope(rms_norm(q, q_gain), cos, sin)
    k = apply_rope(rms_norm(k, k_gain), cos, sin)
    qc = q.astype(f32).reshape(B, nc, CHUNK, SWA_KV_HEADS, grp, SWA_DH)
    kc = k.astype(f32).reshape(B, nc, CHUNK, SWA_KV_HEADS, SWA_DH)
    vc = v.astype(f32).reshape(B, nc, CHUNK, SWA_KV_HEADS, SWA_DH)
    pad = SWA_WIN_CHUNKS - 1
    pw = ((0, 0), (pad, 0), (0, 0), (0, 0), (0, 0))
    kp = jnp.pad(kc, pw)
    vp = jnp.pad(vc, pw)
    kb = jnp.concatenate([kp[:, w:w + nc] for w in range(SWA_WIN_CHUNKS)], axis=2)
    vb = jnp.concatenate([vp[:, w:w + nc] for w in range(SWA_WIN_CHUNKS)], axis=2)
    logits = jnp.einsum('bnihgd,bnjhd->bnhgij', qc, kb) * (SWA_DH ** -0.5)
    key_chunk = (jnp.arange(nc)[:, None] - pad
                 + (jnp.arange(SWA_WIN_CHUNKS * CHUNK) // CHUNK)[None, :])
    valid = key_chunk >= 0
    logits = jnp.where(valid[None, :, None, None, None, :], logits, -jnp.inf)
    sink = sinks.astype(f32).reshape(SWA_KV_HEADS, grp)[None, None, :, :, None, None]
    m = jnp.maximum(jnp.max(logits, axis=-1, keepdims=True), sink)
    p = jnp.exp(logits - m)
    attn = p / (jnp.sum(p, axis=-1, keepdims=True) + jnp.exp(sink - m))
    o = jnp.einsum('bnhgij,bnjhd->bnihgd', attn, vb)
    return o.reshape(B, S, SWA_Q_W).astype(v.dtype)

def memory_attention(q, mk, mv, q_gain, k_gain):
    B, S = q.shape[0], q.shape[1]
    f32 = jnp.float32
    qn = rms_norm(q, q_gain).astype(f32)
    kn = rms_norm(mk, k_gain).astype(f32)
    logits = jnp.einsum('bshd,bmhd->bhsm', qn, kn) * (MEM_DH ** -0.5)
    attn = jax.nn.softmax(logits, axis=-1)
    o = jnp.einsum('bhsm,bmhd->bshd', attn, mv.astype(f32))
    return o.reshape(B, S, MEM_Q_W).astype(mv.dtype)

def moe_ffn(h, w_router, b_router, w_up, b_up, w_down, b_down):
    B, S, D = h.shape
    T = B * S
    TK = T * TOP_K
    ht = h.reshape(T, D)
    logits = (ht @ w_router + b_router).astype(jnp.float32)
    top_val, top_idx = lax.top_k(logits, TOP_K)
    gates = jax.nn.softmax(top_val, axis=-1)
    flat_e = top_idx.reshape(TK).astype(jnp.int32)
    flat_t = jnp.arange(TK, dtype=jnp.int32) // TOP_K
    flat_g = gates.reshape(TK)
    order = jnp.argsort(flat_e)
    se = flat_e[order]
    counts = jnp.zeros((N_EXPERTS,), jnp.int32).at[flat_e].add(1)
    starts = jnp.cumsum(counts) - counts
    padded = ((counts + MOE_BLOCK - 1) // MOE_BLOCK) * MOE_BLOCK
    pad_ends = jnp.cumsum(padded)
    pad_starts = pad_ends - padded
    dest = pad_starts[se] + (jnp.arange(TK, dtype=jnp.int32) - starts[se])
    n_rows = ((TK + MOE_BLOCK - 1) // MOE_BLOCK) * MOE_BLOCK + N_EXPERTS * MOE_BLOCK
    n_blocks = n_rows // MOE_BLOCK
    row_tok = jnp.full((n_rows,), T, jnp.int32).at[dest].set(flat_t[order])
    row_gate = jnp.zeros((n_rows,), jnp.float32).at[dest].set(flat_g[order])
    block_e = jnp.minimum(
        jnp.searchsorted(pad_ends, jnp.arange(n_blocks, dtype=jnp.int32) * MOE_BLOCK, side='right'),
        N_EXPERTS - 1).astype(jnp.int32)
    h_pad = jnp.concatenate([ht, jnp.zeros((1, D), ht.dtype)], axis=0)

    def expert_block(args):
        e, tok, gate = args
        xb = h_pad[tok]
        hu = xb @ w_up[e] + b_up[e]
        x_glu, x_lin = jnp.split(hu, 2, axis=-1)
        x_glu = jnp.minimum(x_glu, SWIGLU_LIMIT)
        x_lin = jnp.clip(x_lin, -SWIGLU_LIMIT, SWIGLU_LIMIT)
        act = x_glu * jax.nn.sigmoid(SWIGLU_ALPHA * x_glu) * (x_lin + 1.0)
        y = act @ w_down[e] + b_down[e]
        return y * gate[:, None].astype(y.dtype)

    y = lax.map(expert_block, (block_e, row_tok.reshape(n_blocks, MOE_BLOCK),
                               row_gate.reshape(n_blocks, MOE_BLOCK)))
    out = jax.ops.segment_sum(y.reshape(n_rows, D), row_tok, num_segments=T + 1)[:T]
    return out.reshape(B, S, D).astype(h.dtype)

def setup_inputs(seed: int = 0) -> dict:
    key = jax.random.key(seed)
    ks = jax.random.split(key, 24)
    f32 = jnp.float32
    nrm = lambda k, shape, s: jax.random.normal(k, shape, f32) * s
    gain = lambda k, shape: 1.0 + 0.02 * jax.random.normal(k, shape, f32)
    x = jax.random.normal(ks[0], (BATCH, SEQ, D_MODEL), f32)
    mem = jax.random.normal(ks[1], (BATCH, N_MEM, D_MODEL), f32)
    offsets = jax.random.randint(ks[2], (BATCH, 1), 0, 64, dtype=jnp.int32) * CHUNK
    positions = (offsets + jnp.arange(SEQ, dtype=jnp.int32)[None, :]).astype(jnp.int32)
    return {
        "x": x,
        "mem": mem,
        "positions": positions,
        "g_mix": gain(ks[3], (DEPTH, D_MODEL)),
        "g_mem": gain(ks[4], (DEPTH, D_MODEL)),
        "w_in": nrm(ks[5], (DEPTH, D_MODEL, IN_WIDTH), D_MODEL ** -0.5),
        "w_mem_kv": nrm(ks[6], (DEPTH, D_MODEL, MEM_KV_W), D_MODEL ** -0.5),
        "swa_q_gain": gain(ks[7], (DEPTH, SWA_DH)),
        "swa_k_gain": gain(ks[8], (DEPTH, SWA_DH)),
        "swa_sinks": nrm(ks[9], (DEPTH, SWA_HEADS), 0.5),
        "mem_q_gain": gain(ks[10], (DEPTH, MEM_DH)),
        "mem_k_gain": gain(ks[11], (DEPTH, MEM_DH)),
        "w_out": nrm(ks[12], (DEPTH, MIX_WIDTH, D_MODEL), MIX_WIDTH ** -0.5),
        "g_ffn": gain(ks[13], (DEPTH, D_MODEL)),
        "w_router": nrm(ks[14], (DEPTH, D_MODEL, N_EXPERTS), D_MODEL ** -0.5),
        "b_router": nrm(ks[15], (DEPTH, N_EXPERTS), 0.01),
        "w_up": nrm(ks[16], (DEPTH, N_EXPERTS, D_MODEL, 2 * D_EXPERT), D_MODEL ** -0.5),
        "b_up": nrm(ks[17], (DEPTH, N_EXPERTS, 2 * D_EXPERT), 0.01),
        "w_down": nrm(ks[18], (DEPTH, N_EXPERTS, D_EXPERT, D_MODEL), D_EXPERT ** -0.5),
        "b_down": nrm(ks[19], (DEPTH, N_EXPERTS, D_MODEL), 0.01),
    }

def reference(x, mem, positions, g_mix, g_mem, w_in, w_mem_kv, swa_q_gain, swa_k_gain, swa_sinks,
              mem_q_gain, mem_k_gain, w_out, g_ffn, w_router, b_router, w_up, b_up, w_down, b_down):
    B, S = x.shape[0], x.shape[1]
    split_at = []
    acc = 0
    for w in IN_SPLITS[:-1]:
        acc += w
        split_at.append(acc)
    for l in range(DEPTH):
        h = rms_norm(x, g_mix[l])
        proj = h @ w_in[l]
        rq, rk, rv, rg, sq, sk, sv, mq = jnp.split(proj, split_at, axis=-1)
        mkv = rms_norm(mem, g_mem[l]) @ w_mem_kv[l]
        mk, mv = jnp.split(mkv, 2, axis=-1)
        n_mem = mem.shape[1]
        o_ret = retention(rq.reshape(B, S, RET_HEADS, RET_DK), rk.reshape(B, S, RET_HEADS, RET_DK),
                          rv.reshape(B, S, RET_HEADS, RET_DV), rg.reshape(B, S, RET_HEADS, RET_DV),
                          positions)
        o_swa = sliding_window_attention(sq.reshape(B, S, SWA_HEADS, SWA_DH),
                                         sk.reshape(B, S, SWA_KV_HEADS, SWA_DH),
                                         sv.reshape(B, S, SWA_KV_HEADS, SWA_DH),
                                         swa_q_gain[l], swa_k_gain[l], swa_sinks[l], positions)
        o_mem = memory_attention(mq.reshape(B, S, MEM_HEADS, MEM_DH),
                                 mk.reshape(B, n_mem, MEM_HEADS, MEM_DH),
                                 mv.reshape(B, n_mem, MEM_HEADS, MEM_DH),
                                 mem_q_gain[l], mem_k_gain[l])
        x = x + jnp.concatenate([o_ret, o_swa, o_mem], axis=-1) @ w_out[l]
        x = x + moe_ffn(rms_norm(x, g_ffn[l]), w_router[l], b_router[l], w_up[l], b_up[l],
                        w_down[l], b_down[l])
    return x


_drawn_inputs = setup_inputs


def setup_inputs(seed=0):
    import zlib

    import numpy as np

    out = dict(_drawn_inputs(seed))
    spreads = {}
    factors = {'g_mem': 7.977,
     'swa_q_gain': 19.191,
     'swa_k_gain': 27.685,
     'swa_sinks': 8.0,
     'mem_q_gain': 6.196,
     'mem_k_gain': 5.577,
     'b_up': 36.727,
     'b_down': 42.49,
     'g_ffn': 4.505,
     'b_router': 7.242}
    for name, (base, spread) in spreads.items():
        noise = np.random.default_rng([zlib.crc32(name.encode()), seed]).standard_normal(out[name].shape)
        drawn = base * np.exp(spread * noise) if base else spread * noise
        out[name] = __import__('jax').numpy.asarray(drawn.astype(out[name].dtype))
    for name, factor in factors.items():
        out[name] = (out[name] * factor).astype(out[name].dtype)
    return out
```

```python
from contextlib import ExitStack

import numpy as np

import concourse.bass as bass
from concourse import mybir

P = 128
CHUNK = 64
EPS = 1e-6
ROPE_THETA = 10000.0
RET_HEADS, RET_DV = 4, 128
SWA_HEADS, SWA_KV_HEADS = 4, 2
MEM_HEADS = 4
DH = 64
TOP_K = 4
LIMIT = 7.0
ALPHA = 1.702
SCALE = DH ** -0.5
MASKED = -1e30
FAR = 1e9

SLOTS = 64
RING = 6
SLOT_COLS = 4096

F32 = mybir.dt.float32
I32 = mybir.dt.int32
U32 = mybir.dt.uint32
ALU = mybir.AluOpType
ACT = mybir.ActivationFunctionType
AX_X = mybir.AxisListType.X

TWO_PI_HI = 6.28125
TWO_PI_MID = float(np.float32(np.round((2 * np.pi - TWO_PI_HI) * 2.0 ** 20) / 2.0 ** 20))
TWO_PI_LO = float(np.float32(2 * np.pi - TWO_PI_HI - TWO_PI_MID))
ROUND = 12582912.0
PI = float(np.float32(np.pi)) - 2.0 ** -22

CONST_WIDTHS = {"ident": P, "dist": 3 * P, "band": 3 * P, "inv": DH // 2, "iota": SLOTS,
                "before": P, "ones": P, "half": P, "row": 18}
CONST_AT = {}
CONST_COLS = 0
for _name, _width in CONST_WIDTHS.items():
    CONST_AT[_name] = (CONST_COLS, CONST_COLS + _width)
    CONST_COLS += _width

ROW_WIDTHS = {"swa_q": DH, "swa_k": DH, "mem_q": DH, "mem_k": DH, "sinks": SWA_HEADS, "b_router": 32}
ROW_AT = {}
ROW_COLS = 0
for _name, _width in ROW_WIDTHS.items():
    ROW_AT[_name] = (ROW_COLS, ROW_COLS + _width)
    ROW_COLS += _width


def shape_constants(n_experts):
    c = np.zeros((P, CONST_COLS), np.float32)

    def put(name, a):
        lo, hi = CONST_AT[name]
        c[:a.shape[0], lo:hi] = a

    p = np.arange(P)
    put("ident", np.eye(P))
    dist, band = [], []
    for key0, frame0, frames in ((0, 0, 2 * P), (P, P, P)):
        m, n = key0 + p[:, None], frame0 + np.arange(frames)[None, :]
        dist.append(np.where(m // CHUNK <= n // CHUNK, np.abs(n - m), FAR))
    put("dist", np.concatenate(dist, 1))
    for frame0, keys in ((0, P), (P, 2 * P)):
        n, m = frame0 + p[:, None], np.arange(keys)[None, :]
        ahead = n // CHUNK - m // CHUNK
        band.append(np.where((ahead >= 0) & (ahead <= 1), 0.0, MASKED))
    put("band", np.concatenate(band, 1))
    inv = np.float32(ROPE_THETA) ** (-np.arange(0, DH, 2, dtype=np.float32) / np.float32(DH))
    put("inv", np.broadcast_to(inv.astype(np.float32), (P, DH // 2)))
    put("iota", np.broadcast_to(np.arange(SLOTS), (P, SLOTS)))
    put("before", p[:, None] < p[None, :])
    put("ones", np.ones((P, P)))
    put("half", np.broadcast_to(p // SLOTS, (P, P)))
    pair = np.arange(18) % (n_experts // 2)
    put("row", p[:, None] - 2.0 * pair[None, :])
    return c


def layer_kernel(nc, x, mem, positions, g_mix, g_mem, w_in, w_mem_kv, swa_q_gain, swa_k_gain, swa_sinks,
                 mem_q_gain, mem_k_gain, w_out, g_ffn, w_router, b_router, w_up, b_up, w_down, b_down,
                 constants, out):
    _, S, D = x.shape
    E = w_router.shape[2]
    F = w_down.shape[2]
    TILES = S // P
    KD = D // P
    KF = F // P
    PAIRS = E // 2
    BLOCKS = S // SLOTS
    N = 512
    RET_BANKS = (5, 6, 7, 0)
    H2_BANKS = (0, 1, 2, 7)
    assert (S, D, F, E) == (256, 1024, 1024, 32) and mem.shape[1] == S

    MIX_CHUNKS = 8
    UP_CHUNKS = KD
    DOWN_CHUNKS = KF // 2
    PAIR_CHUNKS = UP_CHUNKS + DOWN_CHUNKS
    assert PAIR_CHUNKS % RING == 0
    PAIR_LAPS = PAIR_CHUNKS // RING

    with ExitStack() as ctx:
        def sb(name, shape, dt=F32):
            return ctx.enter_context(nc.sbuf_tensor(name, shape, dt))

        def sem(name):
            return ctx.enter_context(nc.semaphore(name))

        psum = ctx.enter_context(nc.psum_tensor("psum", [P, 8, N], F32))

        ring = sb("ring", [P, RING, SLOT_COLS])
        xy = sb("xy", [P, TILES, D])
        const = sb("const", [P, CONST_COLS])
        norm_rows = sb("norm_rows", [3 * KD, P])
        norm_gain = sb("norm_gain", [P, 3 * KD])
        param_row = sb("param_row", [1, ROW_COLS])
        param = sb("param", [P, ROW_COLS])
        wr = sb("wr", [P, KD, E])
        small = sb("small", [P, 256])
        pos_i = sb("pos_i", [P, TILES], I32)
        top_i = sb("top_i", [P, TILES, 8], U32)
        count_i = sb("count_i", [1, 1], I32)

        KIB = 256
        work = sb("work", [P, 88 * KIB])
        at = [0]

        def carve(cols):
            at[0] += cols
            assert at[0] <= 88 * KIB
            return work[:, at[0] - cols:at[0]]

        xn = carve(8 * KIB).rearrange("p (t d) -> p t d", t=TILES)
        hT = carve(8 * KIB).rearrange("p (k n) -> p k n", k=KD)
        mix_start = at[0]
        memT = carve(8 * KIB).rearrange("p (k n) -> p k n", k=KD)
        catT = carve(8 * KIB).rearrange("p (k n) -> p k n", k=KD)
        rqk = carve(4 * KIB).rearrange("p (t n) -> p t n", t=TILES)
        rv = carve(4 * KIB).rearrange("p (t n) -> p t n", t=TILES)
        rg = carve(4 * KIB).rearrange("p (t n) -> p t n", t=TILES)
        sqk = carve(3 * KIB).rearrange("p (t n) -> p t n", t=TILES)
        sv = carve(1 * KIB).rearrange("p (t n) -> p t n", t=TILES)
        mq = carve(2 * KIB).rearrange("p (t n) -> p t n", t=TILES)
        mk = carve(2 * KIB).rearrange("p (t n) -> p t n", t=TILES)
        mv = carve(2 * KIB).rearrange("p (t n) -> p t n", t=TILES)
        sqT = carve(2 * KIB).rearrange("p (g n) -> p g n", g=2)
        mqT = carve(2 * KIB).rearrange("p (g n) -> p g n", g=2)
        mkT = carve(2 * KIB).rearrange("p (g n) -> p g n", g=2)
        decay = carve(6 * KIB).rearrange("p (h n) -> p h n", h=RET_HEADS)
        swaP = carve(6 * KIB).rearrange("p (h n) -> p h n", h=SWA_HEADS)
        memP = carve(8 * KIB).rearrange("p (h t n) -> p h t n", h=MEM_HEADS, t=TILES)
        tmpA = carve(4 * KIB)
        tmpB = carve(4 * KIB)
        retP = xn.rearrange("p t d -> p (t d)")[:, 0:1536].rearrange("p (h n) -> p h n", h=RET_HEADS)
        rope_r = xn.rearrange("p t d -> p (t d)")[:, 0:1024].rearrange("p (t n) -> p t n", t=TILES)
        rkT = xn.rearrange("p t d -> p (t d)")[:, 1536:2048].rearrange("p (g n) -> p g n", g=2)
        rqT = hT.rearrange("p k n -> p (k n)")[:, 1536:2048].rearrange("p (g n) -> p g n", g=2)
        skT = tmpB[:, 768:1024]
        rope_s = swaP.rearrange("p h n -> p (h n)")[:, 0:768].rearrange("p (t n) -> p t n", t=TILES)
        swaPT = hT.rearrange("p k n -> p (k n)")[:, 0:1536].rearrange("p (h n) -> p h n", h=SWA_HEADS)
        memPT = memT.rearrange("p (h b) n -> p h b n", b=2)

        at[0] = mix_start
        XT = carve(4 * KIB).rearrange("p (k s) -> p k s", k=KD)
        actT = carve(4 * KIB).rearrange("p (k s) -> p k s", k=KF)
        glu = carve(4 * KIB)
        lin = carve(4 * KIB)
        sig = carve(4 * KIB)
        act_out = carve(4 * KIB)
        Y = carve(4 * KIB)
        sel = carve(1 * KIB).rearrange("p (t s) -> p t s", t=TILES)
        gated = carve(1 * KIB).rearrange("p (t s) -> p t s", t=TILES)
        back = carve(1 * KIB).rearrange("p (t n) -> p t n", t=TILES)
        whose = carve(KIB // 2)
        place = carve(TILES * (BLOCKS * E + 2)).rearrange("p (t c) -> p t c", t=TILES)
        bup_rows = carve(8 * KIB)
        logits = carve(TILES * E).rearrange("p (t e) -> p t e", t=TILES)
        chosen = carve(TILES * E).rearrange("p (t e) -> p t e", t=TILES)
        gates = carve(TILES * E).rearrange("p (t e) -> p t e", t=TILES)
        hits = carve(TILES * TOP_K * E).rearrange("p (t j e) -> p t j e", t=TILES, j=TOP_K)
        hitg = carve(TILES * TOP_K * E).rearrange("p (t j e) -> p t j e", t=TILES, j=TOP_K)

        used = [0]

        def cols(n):
            used[0] += n
            return small[:, used[0] - n:used[0]]

        ss_mem, rs_mem = cols(TILES), cols(TILES)
        ss_x, rs_x = cols(TILES), cols(TILES)
        ss_mk, rs_mk = cols(8), cols(8)
        ss_mq, rs_mq = cols(8), cols(8)
        ss_s, rs_s = cols(12), cols(12)
        ss_ret, rs_ret = cols(8), cols(8)
        ss_ffn, rs_ffn = cols(TILES), cols(TILES)
        mem_max, mem_neg, mem_sum, mem_inv = cols(8), cols(8), cols(8), cols(8)
        swa_max, swa_neg, swa_sum, swa_sink, swa_inv = cols(8), cols(8), cols(8), cols(8), cols(8)
        minus_half = cols(16)
        posf = cols(TILES)
        top_v = cols(16).rearrange("p (t j) -> p t j", t=TILES)
        top_x = cols(8).rearrange("p (t j) -> p t j", t=TILES)
        top_neg, top_sum, top_inv = cols(TILES), cols(TILES), cols(TILES)
        top_g = cols(8).rearrange("p (t j) -> p t j", t=TILES)
        count_f = cols(1)
        angle = sb("angle", [P, 4, TILES, DH // 2])
        turns = sb("turns", [P, 2, TILES, DH // 2])
        cos2 = sb("cos2", [P, TILES, DH])
        sin2 = sb("sin2", [P, TILES, DH])
        swa_gain = sb("swa_gain", [P, 6, DH])

        def constant(name, rows=P):
            lo, hi = CONST_AT[name]
            return const[0:rows, lo:hi]

        def parameter(name):
            lo, hi = ROW_AT[name]
            return param[:, lo:hi]

        ident = constant("ident")

        const_in, x_in, mem_in = sem("const_in"), sem("x_in"), sem("mem_in")
        pos_in, params_in, router_in = sem("pos_in"), sem("params_in"), sem("router_in")
        bup_in, bdown_in, out_written = sem("bup_in"), sem("bdown_in"), sem("out_written")
        landed = [sem(f"landed{i}") for i in range(RING)]
        slot_used = sem("slot_used")
        dve_step, pool_step = sem("dve_step"), sem("pool_step")
        squares = {n: sem(f"squares_{n}") for n in ("mem", "x", "mk", "mq", "swa", "ret", "ffn")}
        sums = {n: sem(f"sums_{n}") for n in ("mk", "mq", "swa", "ret")}
        rstd = {n: sem(f"rstd_{n}") for n in ("mem", "x", "mk", "mq", "swa", "ret", "ffn")}
        params_spread, params_ready = sem("params_spread"), sem("params_ready")
        angles_ready, trig_ready, decay_ready = sem("angles_ready"), sem("trig_ready"), sem("decay_ready")
        memn_ready, xn_ready = sem("memn_ready"), sem("xn_ready")
        mem_turned, memT_ready = sem("mem_turned"), sem("memT_ready")
        x_turned, hT_ready = sem("x_turned"), sem("hT_ready")
        mkv_done, mv_ready, mk_ready = sem("mkv_done"), sem("mv_ready"), sem("mk_ready")
        mq_done, mq_ready = sem("mq_done"), sem("mq_ready")
        swa_done, swa_qk_ready, sv_ready = sem("swa_done"), sem("swa_qk_ready"), sem("sv_ready")
        rqk_done, rqk_ready = sem("rqk_done"), sem("rqk_ready")
        rv_done, rv_ready = sem("rv_done"), sem("rv_ready")
        rg_done, rg_exp, rg_ready = sem("rg_done"), sem("rg_exp"), sem("rg_ready")
        turnedA, turnsA_ready = sem("turnedA"), sem("turnsA_ready")
        turnedB, turnsB_ready = sem("turnedB"), sem("turnsB_ready")
        mem_scored, mem_max_ready, mem_exp, memP_ready = (
            sem("mem_scored"), sem("mem_max_ready"), sem("mem_exp"), sem("memP_ready"))
        swa_scored, swa_max_ready, swa_exp, swaP_ready = (
            sem("swa_scored"), sem("swa_max_ready"), sem("swa_exp"), sem("swaP_ready"))
        ret_scored, retP_ready = sem("ret_scored"), sem("retP_ready")
        memP_turned, memPT_ready = sem("memP_turned"), sem("memPT_ready")
        swaP_turned, swaPT_ready = sem("swaP_turned"), sem("swaPT_ready")
        mem_read, swa_read, ret_read = sem("mem_read"), sem("swa_read"), sem("ret_read")
        cat_mem, cat_swa, ret_gated, ret_turned, cat_ret = (
            sem("cat_mem"), sem("cat_swa"), sem("ret_gated"), sem("ret_turned"), sem("cat_ret"))
        mixed, x2_ready, xn2_ready = sem("mixed"), sem("x2_ready"), sem("xn2_ready")
        h2_turned, h2T_ready, routed, top_ready, top_exp = (
            sem("h2_turned"), sem("h2T_ready"), sem("routed"), sem("top_ready"), sem("top_exp"))
        chosen_ready, gates_ready, placed, count_ready = (
            sem("chosen_ready"), sem("gates_ready"), sem("placed"), sem("count_ready"))
        gates_turned = sem("gates_turned")
        sel_ready, gated_ready, whose_ready = sem("sel_ready"), sem("gated_ready"), sem("whose_ready")
        biased, gathered, xt_ready = sem("biased"), sem("gathered"), sem("xt_ready")
        glu_ready, lin1_ready, sig_ready, act_ready = sem("glu_ready"), sem("lin1_ready"), sem("sig_ready"), sem("act_ready")
        up_read = sem("up_read")
        gated_turned, back_ready = sem("gated_turned"), sem("back_ready")
        act_turned, actT_ready = sem("act_turned"), sem("actT_ready")
        y_ready, combined, y_added = sem("y_ready"), sem("combined"), sem("y_added")

        w_mem_sb = ring[:, 0, :].rearrange("p (k n) -> p k n", k=KD)
        w_main_sb = [ring[:, 1 + k // 2, (k % 2) * 2048:(k % 2 + 1) * 2048] for k in range(KD)]
        w_mq_sb = ring[:, 5, 0:2048].rearrange("p (k n) -> p k n", k=KD)
        mem_sb = ring[:, 5, 2048:4096].rearrange("p (t d) -> p t d", t=TILES)
        w_out_sb = [ring[:, (6 + k // 4) % RING, (k % 4) * D:(k % 4 + 1) * D] for k in range(KD)]

        def up_slot(j):
            s = (MIX_CHUNKS + j) % RING
            return ring[:, s, :].rearrange("p (e n) -> p e n", e=2)

        def down_slot(j):
            s = (MIX_CHUNKS + UP_CHUNKS + j) % RING
            return ring[:, s, :].rearrange("p (e k n) -> p e k n", e=2, k=2)

        def chunk_landed(eng, q, j):
            g = MIX_CHUNKS + j
            eng.wait_ge(landed[g % RING], q * (16 * PAIR_LAPS) + 16 * (g // RING + 1))

        def chunks_used(q, j):
            return q * PAIR_CHUNKS + (MIX_CHUNKS + j)

        block = ctx.enter_context(nc.Block())

        def overflowing(eng):
            eng.wait_ge(count_ready, 1)
            return eng.value_load(count_i[0:1, 0:1], min_val=0, max_val=S) > SLOTS

        def further_blocks(eng, pair):
            with eng.Fori(1, BLOCKS) as b:
                with eng.Fori(0, PAIRS) as p:
                    pair(b * PAIRS + p, p)

        @block.sync
        def _(sp):
            for t in range(TILES):
                sp.dma_start(mem_sb[:, t], mem[0, t * P:(t + 1) * P, :]).then_inc(mem_in, 16)
            for t in range(TILES):
                sp.dma_start(xy[:, t], x[0, t * P:(t + 1) * P, :]).then_inc(x_in, 16)
            sp.dma_start(w_mem_sb, w_mem_kv[0].rearrange("(k p) n -> p k n", p=P)).then_inc(landed[0], 16)
            sp.dma_start(w_mq_sb, w_in[0, :, 2048:2304].rearrange("(k p) n -> p k n", p=P)).then_inc(landed[5], 16)
            for s in range(4):
                sp.dma_start(ring[:, 1 + s, :].rearrange("p (k n) -> p k n", k=2),
                             w_in[0, 2 * s * P:(2 * s + 2) * P, 0:2048].rearrange("(k p) n -> p k n", p=P)
                             ).then_inc(landed[1 + s], 16)
            for s in range(2):
                sp.wait_ge(slot_used, s + 1)
                sp.dma_start(ring[:, s, :].rearrange("p (k n) -> p k n", k=4),
                             w_out[0, 4 * s * P:(4 * s + 4) * P, :].rearrange("(k p) n -> p k n", p=P)
                             ).then_inc(landed[s], 16)

            def pair(q, p):
                for j in range(PAIR_CHUNKS):
                    g = MIX_CHUNKS + j
                    sp.wait_ge(slot_used, q * PAIR_CHUNKS + (g - RING + 1))
                    if j < UP_CHUNKS:
                        src = w_up[0, bass.ds(2 * p, 2), j * P:(j + 1) * P, :].rearrange("e r n -> r e n")
                    else:
                        i = j - UP_CHUNKS
                        src = w_down[0, bass.ds(2 * p, 2), 2 * i * P:(2 * i + 2) * P, :].rearrange(
                            "e (r k) n -> r e (k n)", k=2)
                    sp.dma_start(ring[:, g % RING, :].rearrange("r (e n) -> r e n", e=2), src
                                 ).then_inc(landed[g % RING], 16)

            def store_result(q_end):
                for t in range(TILES):
                    for n in range(2):
                        sp.wait_ge(y_added, 4 * q_end + 2 * t + n + 1)
                        sp.dma_start(out[0, t * P:(t + 1) * P, n * N:(n + 1) * N], xy[:, t, n * N:(n + 1) * N]
                                     ).then_inc(out_written, 16)

            with sp.Fori(0, PAIRS) as q:
                pair(q, q)
            with sp.If(overflowing(sp)):
                further_blocks(sp, pair)
                store_result(BLOCKS * PAIRS)
            with sp.Else():
                store_result(PAIRS)
            sp.wait_ge(out_written, 16 * 4)

        @block.gpsimd
        def _(pool):
            count = [0]

            def step(ins):
                count[0] += 1
                ins.then_inc(pool_step, 1)
                pool.wait_ge(pool_step, count[0])

            step(nc.gpsimd.memset(minus_half, -0.5))

            def root(name, summed, done, ss, rs, width):
                n = ss.shape[1]
                pool.wait_ge(summed, done)
                step(nc.gpsimd.tensor_scalar(ss, ss, 1.0 / width, EPS, ALU.mult, ALU.add))
                nc.gpsimd.tensor_tensor(rs, ss, minus_half[:, 0:n], ALU.pow).then_inc(rstd[name], 1)

            root("mem", squares["mem"], TILES, ss_mem, rs_mem, D)
            root("x", squares["x"], TILES, ss_x, rs_x, D)
            root("mk", sums["mk"], 1, ss_mk, rs_mk, DH)
            root("mq", sums["mq"], 1, ss_mq, rs_mq, DH)
            root("swa", sums["swa"], 1, ss_s, rs_s, DH)
            for t in range(TILES):
                root("ret", sums["ret"], t + 1, ss_ret[:, 4 * t:4 * t + 4], rs_ret[:, 4 * t:4 * t + 4], RET_DV)
            for t in range(TILES):
                root("ffn", squares["ffn"], t + 1, ss_ffn[:, t:t + 1], rs_ffn[:, t:t + 1], D)

        @block.scalar
        def _(act):
            act.dma_start(const[:], constants).then_inc(const_in, 16)
            act.dma_start(pos_i[:], positions[0].rearrange("(t p) -> p t", p=P), allow_slow_non_contiguous=True).then_inc(pos_in, 16)
            for i, g in enumerate((g_mix, g_mem, g_ffn)):
                act.dma_start(norm_rows[i * KD:(i + 1) * KD, :], g[0].rearrange("(k p) -> k p", p=P)
                              ).then_inc(params_in, 16)
            for name, a in (("swa_q", swa_q_gain), ("swa_k", swa_k_gain), ("mem_q", mem_q_gain),
                            ("mem_k", mem_k_gain), ("sinks", swa_sinks), ("b_router", b_router)):
                lo, hi = ROW_AT[name]
                act.dma_start(param_row[:, lo:hi], a).then_inc(params_in, 16)
            act.dma_start(wr[:], w_router[0].rearrange("(k p) e -> p k e", p=P)).then_inc(router_in, 16)

            for name, src, ss, arrived, other in (("mem", mem_sb, ss_mem, mem_in, tmpA), ("x", xy, ss_x, x_in, tmpB)):
                act.wait_ge(arrived, 16 * TILES)
                for t in range(TILES):
                    if t > 0:
                        act.wait_ge(squares[name], t)
                    nc.scalar.activation(other, src[:, t], ACT.Square, accum_out=ss[:, t:t + 1]
                                         ).then_inc(squares[name], 1)
            act.wait_ge(angles_ready, 1)
            nc.scalar.activation(angle[:, 2:4], angle[:, 0:2], ACT.Sin).then_inc(trig_ready, 1)
            act.wait_ge(params_ready, 2)
            for k in range(KD):
                if k % 2 == 0:
                    act.wait_ge(mem_turned, k // 2 + 1)
                nc.scalar.activation(memT[:, k], psum[:, k // 2, (k % 2) * 256:(k % 2 + 1) * 256], ACT.Copy,
                                     scale=norm_gain[:, KD + k:KD + k + 1]).then_inc(memT_ready, 1)
            for h in range(RET_HEADS):
                nc.scalar.activation(decay[:, h], constant("dist"), ACT.Exp,
                                     scale=float(np.log1p(-(2.0 ** (-5.0 - h))))).then_inc(decay_ready, 1)
            for t in range(TILES):
                act.wait_ge(mkv_done, t + 1)
                nc.scalar.activation(tmpA[:, t * 256:(t + 1) * 256], psum[:, t, 0:256], ACT.Square
                                     ).then_inc(squares["mk"], 1)
                nc.scalar.activation(mv[:, t], psum[:, t, 256:512], ACT.Copy).then_inc(mv_ready, 1)
            act.wait_ge(mq_done, 2)
            nc.scalar.activation(tmpA[:, 512:1024], psum[:, 2], ACT.Square).then_inc(squares["mq"], 1)
            for t in range(TILES):
                act.wait_ge(swa_done, t + 1)
                nc.scalar.activation(tmpB[:, t * 384:(t + 1) * 384], psum[:, 3 + t, 0:384], ACT.Square
                                     ).then_inc(squares["swa"], 1)
                nc.scalar.activation(sv[:, t], psum[:, 3 + t, 384:512], ACT.Copy).then_inc(sv_ready, 1)
            for t in range(TILES):
                act.wait_ge(rv_done, t + 1)
                nc.scalar.activation(rv[:, t], psum[:, 7 if t == 0 else 0], ACT.Copy).then_inc(rv_ready, 1)
            for n, (dst, b) in enumerate(((mkT, 1), (mqT, 2), (sqT, 3))):
                act.wait_ge(turnedA, n + 1)
                nc.scalar.activation(dst, psum[:, b].rearrange("p (g n) -> p g n", g=2), ACT.Copy
                                     ).then_inc(turnsA_ready, 1)
            act.wait_ge(turnedA, 4)
            nc.scalar.activation(skT, psum[:, 4, 0:256], ACT.Copy).then_inc(turnsA_ready, 1)

            def gate_exp(t):
                act.wait_ge(rg_done, t + 1)
                nc.scalar.activation(rg[:, t], psum[:, 5 + t], ACT.Exp, scale=-1.0).then_inc(rg_exp, 1)

            gate_exp(0)
            for h in range(MEM_HEADS):
                act.wait_ge(mem_max_ready, h + 1)
                for t in range(TILES):
                    c = 2 * h + t
                    nc.scalar.activation(memP[:, h, t], psum[:, 1 + h, t * 256:(t + 1) * 256], ACT.Exp, scale=SCALE,
                                         bias=mem_neg[:, c:c + 1], accum_out=mem_sum[:, c:c + 1]).then_inc(mem_exp, 1)
            gate_exp(1)
            for n, (dst, b) in enumerate(((rqT, 7), (rkT, 0))):
                act.wait_ge(turnedB, n + 1)
                nc.scalar.activation(dst, psum[:, b].rearrange("p (g n) -> p g n", g=2), ACT.Copy
                                     ).then_inc(turnsB_ready, 1)
            for h in range(SWA_HEADS):
                act.wait_ge(swa_max_ready, h + 1)
                for t, (lo, hi) in enumerate(((0, P), (P, 3 * P))):
                    c = 2 * h + t
                    nc.scalar.activation(swaP[:, h, lo:hi], swaP[:, h, lo:hi], ACT.Exp, bias=swa_neg[:, c:c + 1],
                                         accum_out=swa_sum[:, c:c + 1]).then_inc(swa_exp, 1)
                    nc.scalar.activation(swa_sink[:, c:c + 1], parameter("sinks")[:, h:h + 1], ACT.Exp,
                                         bias=swa_neg[:, c:c + 1]).then_inc(swa_exp, 1)
            for h in range(MEM_HEADS):
                act.wait_ge(memP_turned, h + 1)
                nc.scalar.activation(memPT[:, h], psum[:, 1 + h].rearrange("p (b n) -> p b n", b=2), ACT.Copy
                                     ).then_inc(memPT_ready, 1)
            for h in range(SWA_HEADS):
                act.wait_ge(swaP_turned, h + 1)
                nc.scalar.activation(swaPT[:, h], psum[:, 1 + h, 0:3 * P], ACT.Copy).then_inc(swaPT_ready, 1)
            for t in range(TILES):
                act.wait_ge(ret_read, t + 1)
                nc.scalar.activation(tmpA[:, t * N:(t + 1) * N], psum[:, 7 if t == 0 else 0], ACT.Square
                                     ).then_inc(squares["ret"], 1)
            act.wait_ge(mem_read, 1)
            act.dma_start(bup_rows[0:E, :], b_up[0]).then_inc(bup_in, 16)
            nc.scalar.activation(catT[:, 6:8], psum[:, 5].rearrange("p (g n) -> p g n", g=2), ACT.Copy
                                 ).then_inc(cat_mem, 1)
            act.wait_ge(swa_read, 1)
            nc.scalar.activation(catT[:, 4:6], psum[:, 6].rearrange("p (g n) -> p g n", g=2), ACT.Copy
                                 ).then_inc(cat_swa, 1)
            for t in range(TILES):
                act.wait_ge(ret_turned, t + 1)
                nc.scalar.activation(catT[:, 0:4, t * P:(t + 1) * P], psum[:, 1 + t].rearrange("p (h n) -> p h n", h=4),
                                     ACT.Copy).then_inc(cat_ret, 1)
            act.wait_ge(y_ready, 2)
            act.dma_start(Y[0:E, :], b_down[0]).then_inc(bdown_in, 16)
            for t in range(TILES):
                act.wait_ge(x2_ready, 2 * t + 2)
                if t > 0:
                    act.wait_ge(squares["ffn"], t)
                nc.scalar.activation(tmpA, xy[:, t], ACT.Square, accum_out=ss_ffn[:, t:t + 1]
                                     ).then_inc(squares["ffn"], 1)
            for t in range(TILES):
                act.wait_ge(top_ready, t + 1)
                nc.scalar.activation(top_g[:, t], top_v[:, t, 0:TOP_K], ACT.Exp, bias=top_neg[:, t:t + 1],
                                     accum_out=top_sum[:, t:t + 1]).then_inc(top_exp, 1)
            act.wait_ge(gates_turned, 1)
            nc.scalar.activation(back[0:E], psum[0:E, 4, 0:256].rearrange("p (t n) -> p t n", t=TILES), ACT.Copy
                                 ).then_inc(back_ready, 1)

            def pair(q, p):
                act.wait_ge(glu_ready, q + 1)
                nc.scalar.activation(sig, glu, ACT.Sigmoid, scale=ALPHA).then_inc(sig_ready, 1)
                act.wait_ge(gated_turned, q + 1)
                nc.scalar.activation(back, psum[:, 4, 0:256].rearrange("p (t n) -> p t n", t=TILES), ACT.Copy
                                     ).then_inc(back_ready, 1)
                for i in range(2):
                    act.wait_ge(act_turned, 2 * q + (i + 1))
                    nc.scalar.activation(actT[:, 4 * i:4 * i + 4], psum[:, 6 + i].rearrange("p (k s) -> p k s", k=4),
                                         ACT.Copy).then_inc(actT_ready, 1)
                act.wait_ge(slot_used, chunks_used(q, PAIR_CHUNKS))
                for n in range(2):
                    nc.scalar.activation(Y[:, n * N:(n + 1) * N], psum[:, 4 + n], ACT.Copy).then_inc(y_ready, 1)

            with act.Fori(0, PAIRS) as q:
                pair(q, q)
            with act.If(overflowing(act)):
                further_blocks(act, pair)

        @block.vector
        def _(dve):
            V = nc.vector
            count = [0]

            def step(ins):
                count[0] += 1
                ins.then_inc(dve_step, 1)
                dve.wait_ge(dve_step, count[0])

            dve.wait_ge(const_in, 16)
            dve.wait_ge(pos_in, 16)
            step(V.tensor_copy(posf, pos_i[:]))
            for t in range(TILES):
                step(V.tensor_scalar(angle[:, 0, t], constant("inv"), posf[:, t:t + 1], None, ALU.mult))
            step(V.tensor_scalar(turns[:, 0], angle[:, 0], float(1 / (2 * np.pi)), ROUND, ALU.mult, ALU.add))
            step(V.tensor_scalar(turns[:, 1], angle[:, 0], float(1 / (2 * np.pi)), 0.25, ALU.mult, ALU.add))
            step(V.tensor_scalar(turns[:, 1], turns[:, 1], ROUND, None, ALU.add))
            step(V.tensor_scalar(turns[:], turns[:], ROUND, None, ALU.subtract))
            step(V.tensor_copy(angle[:, 1], angle[:, 0]))
            for part in (TWO_PI_HI, TWO_PI_MID, TWO_PI_LO):
                step(V.scalar_tensor_tensor(out=angle[:, 0:2], in0=turns[:], scalar=-part, in1=angle[:, 0:2],
                                            op0=ALU.mult, op1=ALU.add))
            step(V.tensor_scalar(angle[:, 1], angle[:, 1], float(np.pi / 2), None, ALU.add))
            V.tensor_scalar(angle[:, 0:2], angle[:, 0:2], PI, -PI, ALU.min, ALU.max).then_inc(angles_ready, 1)

            dve.wait_ge(params_spread, 2)
            V.tensor_copy(norm_gain[:], psum[:, 7, 0:3 * KD]).then_inc(params_ready, 1)
            V.tensor_copy(param[:], psum[:, 7, 64:64 + ROW_COLS]).then_inc(params_ready, 1)
            dve.wait_ge(rstd["mem"], 1)
            for t in range(TILES):
                V.tensor_scalar(mem_sb[:, t], mem_sb[:, t], rs_mem[:, t:t + 1], None, ALU.mult).then_inc(memn_ready, 1)
            dve.wait_ge(rstd["x"], 1)
            for t in range(TILES):
                V.tensor_scalar(xn[:, t], xy[:, t], rs_x[:, t:t + 1], None, ALU.mult).then_inc(xn_ready, 1)

            def turned_gain(dst, src, gain0, k0, kn, n):
                g = norm_gain[:, gain0 + k0:gain0 + k0 + kn].unsqueeze(2).to_broadcast([P, kn, n])
                return V.tensor_tensor(dst, src.rearrange("p (k n) -> p k n", k=kn), g, ALU.mult)

            dve.wait_ge(params_ready, 2)
            for i in range(4):
                dve.wait_ge(x_turned, i + 1)
                turned_gain(hT[:, 2 * i:2 * i + 2], psum[:, 4 + i], 0, 2 * i, 2, 256).then_inc(hT_ready, 1)

            dve.wait_ge(trig_ready, 1)
            V.tensor_copy(cos2[:, :, 0:32], angle[:, 3])
            V.tensor_copy(cos2[:, :, 32:64], angle[:, 3])
            V.tensor_scalar(sin2[:, :, 0:32], angle[:, 2], -1.0, None, ALU.mult)
            V.tensor_copy(sin2[:, :, 32:64], angle[:, 2])
            V.tensor_copy(swa_gain[:, 0:4], parameter("swa_q").unsqueeze(1).to_broadcast([P, 4, DH]))
            step(V.tensor_copy(swa_gain[:, 4:6], parameter("swa_k").unsqueeze(1).to_broadcast([P, 2, DH])))

            def heads(a, n):
                return a.rearrange("p (h d) -> p h d", h=n)

            def per_head(a, n, width=DH):
                return a.unsqueeze(2).to_broadcast([P, n, width])

            def over_heads(a, n):
                return a.unsqueeze(1).to_broadcast([P, n, a.shape[1]])

            def head_sums(name, src, ss, done, n):
                dve.wait_ge(squares[name], done)
                V.tensor_reduce(ss, heads(src, n), AX_X, ALU.add).then_inc(sums[name], 1)

            head_sums("mk", tmpA[:, 0:512], ss_mk, 2, 8)
            dve.wait_ge(rstd["mk"], 1)
            dve.wait_ge(mv_ready, 2)
            for t in range(TILES):
                step(V.tensor_tensor(heads(mk[:, t], 4), heads(psum[:, t, 0:256], 4),
                                     per_head(rs_mk[:, 4 * t:4 * t + 4], 4), ALU.mult))
                V.tensor_tensor(heads(mk[:, t], 4), heads(mk[:, t], 4), over_heads(parameter("mem_k"), 4), ALU.mult
                                ).then_inc(mk_ready, 1)
            head_sums("mq", tmpA[:, 512:1024], ss_mq, 1, 8)
            dve.wait_ge(rstd["mq"], 1)
            for t in range(TILES):
                step(V.tensor_tensor(heads(mq[:, t], 4), heads(psum[:, 2, t * 256:(t + 1) * 256], 4),
                                     per_head(rs_mq[:, 4 * t:4 * t + 4], 4), ALU.mult))
                V.tensor_tensor(heads(mq[:, t], 4), heads(mq[:, t], 4), over_heads(parameter("mem_q"), 4), ALU.mult
                                ).then_inc(mq_ready, 1)

            def rotate(dst, src, swapped, t, n):
                src, dst, swapped = heads(src, n), heads(dst, n), heads(swapped, n)
                for lo, hi in ((0, 32), (32, 64)):
                    last = V.tensor_tensor(swapped[:, :, lo:hi], src[:, :, 32 - lo:64 - lo],
                                           over_heads(sin2[:, t, lo:hi], n), ALU.mult)
                step(last)
                step(V.tensor_tensor(dst, src, over_heads(cos2[:, t], n), ALU.mult))
                return V.tensor_tensor(dst, dst, swapped, ALU.add)

            head_sums("swa", tmpB[:, 0:768], ss_s, 2, 12)
            dve.wait_ge(rstd["swa"], 1)
            dve.wait_ge(sv_ready, 2)
            for t in range(TILES):
                rs = rs_s[:, 6 * t:6 * t + 6]
                V.tensor_tensor(sqk[:, t, 0:256].rearrange("p (b a d) -> p a b d", a=2, b=2),
                                psum[:, 3 + t, 0:256].rearrange("p (a b d) -> p a b d", a=2, b=2),
                                rs[:, 0:4].rearrange("p (a b) -> p a b", a=2).unsqueeze(3).to_broadcast([P, 2, 2, DH]),
                                ALU.mult)
                step(V.tensor_tensor(heads(sqk[:, t, 256:384], 2), heads(psum[:, 3 + t, 256:384], 2),
                                     per_head(rs[:, 4:6], 2), ALU.mult))
                step(V.tensor_tensor(heads(sqk[:, t], 6), heads(sqk[:, t], 6), swa_gain[:], ALU.mult))
                rotate(sqk[:, t], sqk[:, t], rope_s[:, t], t, 6).then_inc(swa_qk_ready, 1)
            for t in range(TILES):
                dve.wait_ge(rqk_done, t + 1)
                rotate(rqk[:, t], psum[:, 5 + t], rope_r[:, t], t, 8).then_inc(rqk_ready, 1)

            def gate(t):
                dve.wait_ge(rg_exp, t + 1)
                step(V.tensor_scalar(rg[:, t], rg[:, t], 1.0, None, ALU.add))
                step(V.reciprocal(rg[:, t], rg[:, t]))
                V.tensor_tensor(rg[:, t], rg[:, t], psum[:, 5 + t], ALU.mult).then_inc(rg_ready, 1)

            gate(0)
            for h in range(MEM_HEADS):
                dve.wait_ge(mem_scored, h + 1)
                step(V.tensor_reduce(mem_max[:, 2 * h:2 * h + 2], psum[:, 1 + h].rearrange("p (t n) -> p t n", t=2),
                                     AX_X, ALU.max))
                V.tensor_scalar(mem_neg[:, 2 * h:2 * h + 2], mem_max[:, 2 * h:2 * h + 2], -SCALE, None, ALU.mult
                                ).then_inc(mem_max_ready, 1)
            for h in range(MEM_HEADS):
                dve.wait_ge(mem_exp, 2 * h + 2)
                step(V.reciprocal(mem_inv[:, 2 * h:2 * h + 2], mem_sum[:, 2 * h:2 * h + 2]))
                for t in range(TILES):
                    V.tensor_scalar(memP[:, h, t], memP[:, h, t], mem_inv[:, 2 * h + t:2 * h + t + 1], None, ALU.mult
                                    ).then_inc(memP_ready, 1)
            gate(1)
            for h in range(SWA_HEADS):
                dve.wait_ge(swa_scored, h + 1)
                step(V.scalar_tensor_tensor(out=swaP[:, h], in0=psum[:, 1 + h, 0:3 * P], scalar=SCALE,
                                            in1=constant("band"), op0=ALU.mult, op1=ALU.add))
                V.tensor_reduce(swa_max[:, 2 * h:2 * h + 1], swaP[:, h, 0:P], AX_X, ALU.max)
                step(V.tensor_reduce(swa_max[:, 2 * h + 1:2 * h + 2], swaP[:, h, P:3 * P], AX_X, ALU.max))
                V.tensor_scalar(swa_neg[:, 2 * h:2 * h + 2], swa_max[:, 2 * h:2 * h + 2],
                                parameter("sinks")[:, h:h + 1], -1.0, ALU.max, ALU.mult).then_inc(swa_max_ready, 1)
            dve.wait_ge(decay_ready, RET_HEADS)
            for h in range(RET_HEADS):
                dve.wait_ge(ret_scored, h + 1)
                V.scalar_tensor_tensor(out=retP[:, h], in0=psum[:, RET_BANKS[h], 0:3 * P], scalar=SCALE,
                                       in1=decay[:, h], op0=ALU.mult, op1=ALU.mult).then_inc(retP_ready, 1)
            for h in range(SWA_HEADS):
                dve.wait_ge(swa_exp, 4 * h + 4)
                step(V.tensor_tensor(swa_inv[:, 2 * h:2 * h + 2], swa_sum[:, 2 * h:2 * h + 2],
                                     swa_sink[:, 2 * h:2 * h + 2], ALU.add))
                step(V.reciprocal(swa_inv[:, 2 * h:2 * h + 2], swa_inv[:, 2 * h:2 * h + 2]))
                for t, (lo, hi) in enumerate(((0, P), (P, 3 * P))):
                    V.tensor_scalar(swaP[:, h, lo:hi], swaP[:, h, lo:hi], swa_inv[:, 2 * h + t:2 * h + t + 1], None,
                                    ALU.mult).then_inc(swaP_ready, 1)
            for t in range(TILES):
                head_sums("ret", tmpA[:, t * N:(t + 1) * N], ss_ret[:, 4 * t:4 * t + 4], t + 1, 4)
            for t in range(TILES):
                dve.wait_ge(rstd["ret"], t + 1)
                o = tmpB[:, t * N:(t + 1) * N]
                step(V.tensor_tensor(heads(o, 4), heads(psum[:, 7 if t == 0 else 0], 4),
                                     per_head(rs_ret[:, 4 * t:4 * t + 4], 4, RET_DV), ALU.mult))
                V.tensor_tensor(o, o, rg[:, t], ALU.mult).then_inc(ret_gated, 1)
            dve.wait_ge(cat_ret, 2)
            V.memset(back, 0.0)
            V.memset(place, -FAR)
            V.memset(Y, 0.0).then_inc(y_ready, 2)
            for t in range(TILES):
                for n in range(2):
                    dve.wait_ge(mixed, 2 * t + n + 1)
                    part = xy[:, t, n * N:(n + 1) * N]
                    V.tensor_tensor(part, psum[:, 3 + 2 * t + n], part, ALU.add).then_inc(x2_ready, 1)
            for t in range(TILES):
                dve.wait_ge(rstd["ffn"], t + 1)
                V.tensor_scalar(xn[:, t], xy[:, t], rs_ffn[:, t:t + 1], None, ALU.mult).then_inc(xn2_ready, 1)
            for t in range(TILES):
                for i in range(2):
                    dve.wait_ge(h2_turned, 2 * t + i + 1)
                    turned_gain(hT[:, 4 * i:4 * i + 4, t * P:(t + 1) * P], psum[:, H2_BANKS[2 * t + i]], 2 * KD, 4 * i, 4,
                                P).then_inc(h2T_ready, 1)
            for t in range(TILES):
                dve.wait_ge(routed, t + 1)
                step(V.tensor_tensor(logits[:, t], psum[:, 3 + 2 * t, 0:E], parameter("b_router"), ALU.add))
                step(V.max(top_v[:, t], logits[:, t]))
                V.tensor_scalar(top_neg[:, t:t + 1], top_v[:, t, 0:1], -1.0, None, ALU.mult).then_inc(top_ready, 1)
                step(V.max_index(top_i[:, t], top_v[:, t], logits[:, t]))
                step(V.tensor_copy(top_x[:, t], top_i[:, t, 0:TOP_K]))
                step(V.tensor_tensor(hits[:, t], constant("iota")[:, 0:E].unsqueeze(1).to_broadcast([P, TOP_K, E]),
                                     top_x[:, t].unsqueeze(2).to_broadcast([P, TOP_K, E]), ALU.is_equal))
                V.tensor_reduce(chosen[:, t], hits[:, t].rearrange("p j e -> p e j"), AX_X, ALU.add
                                ).then_inc(chosen_ready, 1)
            for t in range(TILES):
                dve.wait_ge(top_exp, t + 1)
                step(V.reciprocal(top_inv[:, t:t + 1], top_sum[:, t:t + 1]))
                step(V.tensor_scalar(top_g[:, t], top_g[:, t], top_inv[:, t:t + 1], None, ALU.mult))
                step(V.tensor_tensor(hitg[:, t], hits[:, t], top_g[:, t].unsqueeze(2).to_broadcast([P, TOP_K, E]),
                                     ALU.mult))
                V.tensor_reduce(gates[:, t], hitg[:, t].rearrange("p j e -> p e j"), AX_X, ALU.add
                                ).then_inc(gates_ready, 1)
            dve.wait_ge(placed, 1)
            step(V.scalar_tensor_tensor(out=logits[:], in0=psum[:, 5, 64:128].rearrange("p (t e) -> p t e", t=TILES),
                                        scalar=1.0, in1=chosen[:], op0=ALU.add, op1=ALU.mult))
            for b in range(BLOCKS):
                last = V.tensor_scalar(place[:, :, b * E:(b + 1) * E], logits[:], -1.0 - b * SLOTS, None, ALU.add)
            step(last)

            def build_sel(q):
                for t in range(TILES):
                    for e in range(2):
                        last = V.tensor_scalar(sel[:, t, e * SLOTS:(e + 1) * SLOTS], constant("iota"),
                                               place[:, t, bass.ds(2 * q + e, 1)], None, ALU.is_equal)
                last.then_inc(sel_ready, 1)

            def build_gated(q, p):
                for t in range(TILES):
                    for e in range(2):
                        last = V.tensor_scalar(gated[:, t, e * SLOTS:(e + 1) * SLOTS], constant("iota"),
                                               place[:, t, bass.ds(2 * q + e, 1)], gates[:, t, bass.ds(2 * p + e, 1)],
                                               ALU.is_equal, ALU.mult)
                last.then_inc(gated_ready, 1)

            def build_whose(p):
                V.tensor_scalar(whose[0:E, :], constant("half", E), constant("row", E)[:, bass.ds(p, 1)], None,
                                ALU.is_equal).then_inc(whose_ready, 1)

            def take_gathered(q, i):
                dve.wait_ge(gathered, 2 * q + (i + 1))
                turned_gain(XT[:, 4 * i:4 * i + 4], psum[:, 6 + i], 2 * KD, 4 * i, 4, P).then_inc(xt_ready, 1)

            def add_combined(q, c):
                t, n = c // 2, c % 2
                dve.wait_ge(combined, 4 * q + (c + 1))
                part = xy[:, t, n * N:(n + 1) * N]
                V.tensor_tensor(part, psum[:, 6 + n], part, ALU.add).then_inc(y_added, 1)

            build_sel(0)
            build_whose(0)
            V.tensor_reduce(count_f, psum[:, 5, 128:160], AX_X, ALU.max).then_inc(up_read, 1)
            dve.wait_ge(up_read, 1)
            V.tensor_copy(count_i[:], count_f[0:1]).then_inc(count_ready, 1)
            for i in range(2):
                take_gathered(0, i)

            def pair(q, p):
                dve.wait_ge(gathered, 2 * q + 2)
                build_sel(q + 1)
                dve.wait_ge(back_ready, q + 1)
                build_gated(q, p)
                dve.wait_ge(biased, q + 1)
                build_whose(p + 1)
                dve.wait_ge(slot_used, chunks_used(q, UP_CHUNKS))
                V.tensor_scalar(glu, psum[:, 0:2].rearrange("p b n -> p (b n)"), LIMIT, None, ALU.min
                                ).then_inc(glu_ready, 1)
                V.tensor_scalar(lin, psum[:, 2:4].rearrange("p b n -> p (b n)"), LIMIT, -LIMIT, ALU.min, ALU.max
                                ).then_inc(up_read, 1)
                for i in range(2):
                    take_gathered(q + 1, i)
                dve.wait_ge(glu_ready, q + 1)
                dve.wait_ge(up_read, q + 2)
                V.scalar_tensor_tensor(out=lin, in0=lin, scalar=1.0, in1=glu, op0=ALU.add, op1=ALU.mult
                                       ).then_inc(lin1_ready, 1)
                dve.wait_ge(lin1_ready, q + 1)
                dve.wait_ge(sig_ready, q + 1)
                V.tensor_tensor(act_out, lin, sig, ALU.mult).then_inc(act_ready, 1)
                for c in range(4):
                    add_combined(q, c)

            with dve.Fori(0, PAIRS) as q:
                pair(q, q)
            with dve.If(overflowing(dve)):
                further_blocks(dve, pair)
                for c in range(4):
                    add_combined(BLOCKS * PAIRS, c)
            with dve.Else():
                for c in range(4):
                    add_combined(PAIRS, c)

        @block.tensor
        def _(pe):
            def turn(dst, src):
                n = src.shape[0]
                return pe.transpose(dst, src, ident[0:n, 0:n])

            pe.wait_ge(const_in, 16)
            pe.wait_ge(params_in, 16 * 9)
            turn(psum[:, 7, 0:3 * KD], norm_rows[:]).then_inc(params_spread, 1)
            pe.matmul(psum[:, 7, 64:64 + ROW_COLS], constant("ones", 1), param_row[:], start=True, stop=True
                      ).then_inc(params_spread, 1)

            def turn_rows(src, bank0, ready, done):
                for t in range(TILES):
                    pe.wait_ge(ready, t + 1)
                    for k in range(KD):
                        c = (k % 2) * 256 + t * P
                        mm = turn(psum[:, bank0 + k // 2, c:c + P], src[:, t, k * P:(k + 1) * P])
                        if t == TILES - 1 and k % 2 == 1:
                            mm.then_inc(done, 1)

            turn_rows(mem_sb, 0, memn_ready, mem_turned)
            pe.wait_ge(params_ready, 2)
            turn_rows(xn, 4, xn_ready, x_turned)

            pe.wait_ge(memT_ready, KD)
            pe.wait_ge(landed[0], 16)
            for t in range(TILES):
                for k in range(KD):
                    mm = pe.matmul(psum[:, t], memT[:, k, t * P:(t + 1) * P], w_mem_sb[:, k],
                                   start=k == 0, stop=k == KD - 1)
                mm.then_inc(mkv_done, 1)

            pe.wait_ge(hT_ready, 4)
            pe.wait_ge(landed[5], 16)
            for t in range(TILES):
                for k in range(KD):
                    mm = pe.matmul(psum[:, 2, t * 256:(t + 1) * 256], hT[:, k, t * P:(t + 1) * P], w_mq_sb[:, k],
                                   start=k == 0, stop=k == KD - 1)
                    if t == 0 and k == 0:
                        mm.then_inc(slot_used, 1)
                mm.then_inc(mq_done, 1)
            for k in range(KD):
                pe.wait_ge(landed[1 + k // 2], 16)
                for t in range(TILES):
                    mm = pe.matmul(psum[:, 3 + t], hT[:, k, t * P:(t + 1) * P], w_main_sb[k][:, 3 * N:4 * N],
                                   start=k == 0, stop=k == KD - 1)
                    if k == KD - 1:
                        mm.then_inc(swa_done, 1)

            def project(n, t, b, done):
                for k in range(KD):
                    mm = pe.matmul(psum[:, b], hT[:, k, t * P:(t + 1) * P], w_main_sb[k][:, n * N:(n + 1) * N],
                                   start=k == 0, stop=k == KD - 1)
                mm.then_inc(done, 1)

            project(0, 0, 5, rqk_done)
            project(0, 1, 6, rqk_done)
            project(1, 0, 7, rv_done)
            pe.wait_ge(mk_ready, 1)
            pe.wait_ge(mv_ready, 1)
            project(1, 1, 0, rv_done)

            def turn_heads(src, b, groups, done):
                for g in range(groups):
                    for t in range(TILES):
                        c = g * 256 + t * P
                        mm = turn(psum[:, b, c:c + P], src(t, g))
                mm.then_inc(done, 1)

            pe.wait_ge(mk_ready, 2)
            pe.wait_ge(mv_ready, 2)
            turn_heads(lambda t, g: mk[:, t, g * P:(g + 1) * P], 1, 2, turnedA)
            pe.wait_ge(mq_ready, 2)
            turn_heads(lambda t, g: mq[:, t, g * P:(g + 1) * P], 2, 2, turnedA)
            pe.wait_ge(swa_qk_ready, 2)
            pe.wait_ge(sv_ready, 2)
            turn_heads(lambda t, g: sqk[:, t, g * P:(g + 1) * P], 3, 2, turnedA)
            turn_heads(lambda t, g: sqk[:, t, 256:384], 4, 1, turnedA)
            pe.wait_ge(rqk_ready, 1)
            project(2, 0, 5, rg_done)
            pe.wait_ge(turnsA_ready, 4)
            for h in range(MEM_HEADS):
                r = DH * (h % 2)
                for t in range(TILES):
                    mm = pe.matmul(psum[:, 1 + h, t * 256:(t + 1) * 256], mqT[r:r + DH, h // 2, t * P:(t + 1) * P],
                                   mkT[r:r + DH, h // 2, :], start=True, stop=True)
                mm.then_inc(mem_scored, 1)
            pe.wait_ge(rqk_ready, 2)
            project(2, 1, 6, rg_done)
            pe.wait_ge(rv_ready, 2)
            turn(psum[:, 7, 0:P], rqk[:, 0, 0:P]).then_inc(slot_used, 5)
            turn_heads(lambda t, g: rqk[:, t, g * P:(g + 1) * P], 7, 2, turnedB)
            turn_heads(lambda t, g: rqk[:, t, (2 + g) * P:(3 + g) * P], 0, 2, turnedB)
            for h in range(SWA_HEADS):
                pe.wait_ge(mem_exp, 2 * h + 2)
                r = DH * (h // 2)
                for t in range(TILES):
                    mm = pe.matmul(psum[:, 1 + h, t * P:(2 * t + 1) * P], sqT[r:r + DH, h % 2, t * P:(t + 1) * P],
                                   skT[r:r + DH, 0:(t + 1) * P], start=True, stop=True)
                mm.then_inc(swa_scored, 1)
            pe.wait_ge(turnsB_ready, 2)
            pe.wait_ge(rg_ready, 2)
            for h in range(RET_HEADS):
                r = DH * (h % 2)
                pe.matmul(psum[:, RET_BANKS[h], 0:256], rkT[r:r + DH, h // 2, 0:P], rqT[r:r + DH, h // 2, :],
                          start=True, stop=True)
                pe.matmul(psum[:, RET_BANKS[h], 256:384], rkT[r:r + DH, h // 2, P:2 * P], rqT[r:r + DH, h // 2, P:2 * P],
                          start=True, stop=True).then_inc(ret_scored, 1)
            for h in range(MEM_HEADS):
                pe.wait_ge(memP_ready, 2 * h + 2)
                pe.wait_ge(swa_max_ready, h + 1)
                for b in range(2):
                    for t in range(TILES):
                        c = b * 256 + t * P
                        mm = turn(psum[:, 1 + h, c:c + P], memP[:, h, t, b * P:(b + 1) * P])
                mm.then_inc(memP_turned, 1)
            pe.wait_ge(rv_ready, 2)
            pe.wait_ge(retP_ready, 4)
            for h in range(RET_HEADS):
                mm = pe.matmul(psum[:, 7, h * P:(h + 1) * P], retP[:, h, 0:P], rv[:, 0, h * P:(h + 1) * P],
                               start=True, stop=True)
            mm.then_inc(ret_read, 1)
            for h in range(RET_HEADS):
                pe.matmul(psum[:, 0, h * P:(h + 1) * P], retP[:, h, P:2 * P], rv[:, 0, h * P:(h + 1) * P],
                          start=True, stop=False)
                mm = pe.matmul(psum[:, 0, h * P:(h + 1) * P], retP[:, h, 2 * P:3 * P], rv[:, 1, h * P:(h + 1) * P],
                               start=False, stop=True)
            mm.then_inc(ret_read, 1)
            for g in range(2):
                pe.wait_ge(memPT_ready, 2 * g + 2)
                for b in range(2):
                    for r in range(2):
                        h = 2 * g + r
                        mm = pe.matmul(psum[r * DH:(r + 1) * DH, 5, g * 256:(g + 1) * 256], mv[:, b, h * DH:(h + 1) * DH],
                                       memPT[:, h, b], start=b == 0, stop=b == 1)
            mm.then_inc(mem_read, 1)
            for h in range(SWA_HEADS):
                pe.wait_ge(swaP_ready, 2 * h + 2)
                pe.wait_ge(memPT_ready, h + 1)
                for c in range(3):
                    mm = turn(psum[:, 1 + h, c * P:(c + 1) * P], swaP[:, h, c * P:(c + 1) * P])
                mm.then_inc(swaP_turned, 1)
            for g in range(2):
                pe.wait_ge(swaPT_ready, 2 * g + 2)
                for c, (t, b) in enumerate(((0, 0), (1, 0), (1, 1))):
                    for r in range(2):
                        h = 2 * g + r
                        at = g * 256 + t * P
                        mm = pe.matmul(psum[r * DH:(r + 1) * DH, 6, at:at + P], sv[:, b, g * DH:(g + 1) * DH],
                                       swaPT[:, h, c * P:(c + 1) * P], start=b == 0, stop=b == t)
            mm.then_inc(swa_read, 1)
            for t in range(TILES):
                pe.wait_ge(ret_gated, t + 1)
                for h in range(RET_HEADS):
                    c = t * N + h * P
                    mm = turn(psum[:, 1 + t, h * P:(h + 1) * P], tmpB[:, c:c + P])
                mm.then_inc(ret_turned, 1)
            pe.wait_ge(swaPT_ready, 4)
            pe.wait_ge(cat_mem, 1)
            pe.wait_ge(cat_swa, 1)
            pe.wait_ge(landed[0], 32)
            pe.wait_ge(landed[1], 32)
            for t in range(TILES):
                for n in range(2):
                    for i, k in enumerate((4, 5, 6, 7, 0, 1, 2, 3)):
                        if i == 4:
                            pe.wait_ge(cat_ret, t + 1)
                        mm = pe.matmul(psum[:, 3 + 2 * t + n], catT[:, k, t * P:(t + 1) * P],
                                       w_out_sb[k][:, n * N:(n + 1) * N], start=i == 0, stop=i == KD - 1)
                    mm.then_inc(mixed, 1)
            turn(psum[:, 1, 0:P], ident).then_inc(slot_used, 2)

            for t in range(TILES):
                pe.wait_ge(xn2_ready, t + 1)
                for k in range(KD):
                    c = (k % 4) * P
                    mm = turn(psum[:, H2_BANKS[2 * t + k // 4], c:c + P], xn[:, t, k * P:(k + 1) * P])
                    if k % 4 == 3:
                        mm.then_inc(h2_turned, 1)
            pe.wait_ge(router_in, 16)
            for t in range(TILES):
                pe.wait_ge(h2T_ready, 2 * t + 2)
                for k in range(KD):
                    mm = pe.matmul(psum[:, 3 + 2 * t, 0:E], hT[:, k, t * P:(t + 1) * P], wr[:, k],
                                   start=k == 0, stop=k == KD - 1)
                mm.then_inc(routed, 1)
            pe.wait_ge(chosen_ready, 2)
            pe.matmul(psum[:, 5, 64:96], constant("before"), chosen[:, 0], start=True, stop=True)
            pe.matmul(psum[:, 5, 96:128], constant("ones"), chosen[:, 0], start=True, stop=False)
            pe.matmul(psum[:, 5, 96:128], constant("before"), chosen[:, 1], start=False, stop=True)
            pe.matmul(psum[:, 5, 128:160], constant("ones"), chosen[:, 0], start=True, stop=False)
            pe.matmul(psum[:, 5, 128:160], constant("ones"), chosen[:, 1], start=False, stop=True).then_inc(placed, 1)
            for t in range(TILES):
                pe.wait_ge(gates_ready, t + 1)
                mm = turn(psum[0:E, 4, t * P:(t + 1) * P], gates[:, t])
            mm.then_inc(gates_turned, 1)

            def gather(q):
                pe.wait_ge(sel_ready, q + 1)
                for k in range(KD):
                    c = (k % 4) * P
                    for t in range(TILES):
                        mm = pe.matmul(psum[:, 6 + k // 4, c:c + P], xn[:, t, k * P:(k + 1) * P], sel[:, t],
                                       start=t == 0, stop=t == TILES - 1)
                    if k % 4 == 3:
                        mm.then_inc(gathered, 1)

            def combine(q, c):
                t, n = c // 2, c % 2
                pe.matmul(psum[:, 6 + n], back[:, t], Y[:, n * N:(n + 1) * N], start=True, stop=True
                          ).then_inc(combined, 1)

            gather(0)
            pe.wait_ge(bdown_in, 16)
            pe.wait_ge(bup_in, 16)
            pe.wait_ge(count_ready, 1)

            def pair(q, p):
                pe.wait_ge(whose_ready, q + 1)
                pe.wait_ge(up_read, q + 1)
                for n in range(4):
                    mm = pe.matmul(psum[:, n], whose[0:E, :], bup_rows[0:E, n * N:(n + 1) * N], start=True, stop=False,
                                   skip_group_check=True)
                mm.then_inc(biased, 1)
                pe.wait_ge(xt_ready, 2 * q + 2)
                for j in range(UP_CHUNKS):
                    chunk_landed(pe, q, j)
                    for n in range(4):
                        for e in range(2):
                            r = e * SLOTS
                            mm = pe.matmul(psum[r:r + SLOTS, n], XT[:, j, r:r + SLOTS], up_slot(j)[:, e, n * N:(n + 1) * N],
                                           start=False, stop=j == KD - 1, skip_group_check=True)
                    mm.then_inc(slot_used, 1)
                pe.wait_ge(y_ready, 2 * q + 2)
                gather(q + 1)
                pe.wait_ge(back_ready, q + 1)
                pe.wait_ge(xt_ready, 2 * q + 3)
                combine(q, 0)
                pe.wait_ge(xt_ready, 2 * q + 4)
                combine(q, 1)
                pe.wait_ge(y_added, 4 * q + 1)
                combine(q, 2)
                pe.wait_ge(y_added, 4 * q + 2)
                combine(q, 3)
                pe.wait_ge(gated_ready, q + 1)
                for t in range(TILES):
                    mm = turn(psum[:, 4, t * P:(t + 1) * P], gated[:, t])
                mm.then_inc(gated_turned, 1)
                pe.wait_ge(act_ready, q + 1)
                for i in range(2):
                    pe.wait_ge(y_added, 4 * q + (3 + i))
                    for k in range(4):
                        j = 4 * i + k
                        first = 256 * (j // 2) + j % 2
                        mm = turn(psum[:, 6 + i, k * P:(k + 1) * P], act_out[:, first:first + 255:2])
                    mm.then_inc(act_turned, 1)
                pe.wait_ge(actT_ready, 2 * q + 2)
                pe.wait_ge(back_ready, q + 2)
                for i in range(DOWN_CHUNKS):
                    chunk_landed(pe, q, UP_CHUNKS + i)
                    for k in range(2):
                        for n in range(2):
                            for e in range(2):
                                r = e * SLOTS
                                mm = pe.matmul(psum[r:r + SLOTS, 4 + n], actT[:, 2 * i + k, r:r + SLOTS],
                                               down_slot(i)[:, e, k, n * N:(n + 1) * N],
                                               start=i == 0 and k == 0, stop=i == DOWN_CHUNKS - 1 and k == 1)
                    mm.then_inc(slot_used, 1)

            def last_share(q_end):
                pe.wait_ge(back_ready, q_end + 1)
                pe.wait_ge(y_ready, 2 * q_end + 2)
                for c in range(4):
                    if c >= 2:
                        pe.wait_ge(y_added, 4 * q_end + c - 1)
                    combine(q_end, c)

            with pe.Fori(0, PAIRS) as q:
                pair(q, q)
            with pe.If(overflowing(pe)):
                further_blocks(pe, pair)
                last_share(BLOCKS * PAIRS)
            with pe.Else():
                last_share(PAIRS)


_INPUTS = ["x", "mem", "positions", "g_mix", "g_mem", "w_in", "w_mem_kv", "swa_q_gain", "swa_k_gain", "swa_sinks",
           "mem_q_gain", "mem_k_gain", "w_out", "g_ffn", "w_router", "b_router", "w_up", "b_up", "w_down", "b_down"]


def kernel(**inputs):
    import concourse.bacc as bacc
    from concourse.bass_utils import run_bass_kernel_spmd

    nc = bacc.Bacc("TRN2", target_bir_lowering=False, num_devices=1)
    arrays = {name: np.ascontiguousarray(inputs[name]) for name in _INPUTS}
    arrays["constants"] = shape_constants(arrays["w_router"].shape[2])
    args = [nc.dram_tensor(f"in_{name}", a.shape, mybir.dt.from_np(a.dtype), kind="ExternalInput").ap()
            for name, a in arrays.items()]
    out = nc.dram_tensor("out_0", arrays["x"].shape, F32, kind="ExternalOutput").ap()
    layer_kernel(nc, *args, out)
    result = run_bass_kernel_spmd(nc, [{f"in_{name}": a for name, a in arrays.items()}], core_ids=[0])
    return result.results[0]["out_0"]
```

```python
from contextlib import ExitStack

import numpy as np

import concourse.bass as bass
from concourse import mybir

P = 128
CHUNK = 64
EPS = 1e-6
ROPE_THETA = 10000.0
RET_HEADS, RET_DV = 4, 128
SWA_HEADS, SWA_KV_HEADS = 4, 2
MEM_HEADS = 4
DH = 64
TOP_K = 4
LIMIT = 7.0
ALPHA = 1.702
SCALE = DH ** -0.5
MASKED = -1e30
FAR = 1e9

SLOTS = 64
RING = 6
SLOT_COLS = 4096

F32 = mybir.dt.float32
I32 = mybir.dt.int32
U32 = mybir.dt.uint32
ALU = mybir.AluOpType
ACT = mybir.ActivationFunctionType
AX_X = mybir.AxisListType.X

TWO_PI_HI = 6.28125
TWO_PI_MID = float(np.float32(np.round((2 * np.pi - TWO_PI_HI) * 2.0 ** 20) / 2.0 ** 20))
TWO_PI_LO = float(np.float32(2 * np.pi - TWO_PI_HI - TWO_PI_MID))
ROUND = 12582912.0
PI = float(np.float32(np.pi)) - 2.0 ** -22

CONST_WIDTHS = {"ident": P, "ones": P, "inv": DH // 2,
                "dist": 3 * P, "band": 3 * P, "iota": SLOTS, "before": P, "half": P, "row": 18}
CONST_FIRST = 2 * P + DH // 2
CONST_AT = {}
CONST_COLS = 0
for _name, _width in CONST_WIDTHS.items():
    CONST_AT[_name] = (CONST_COLS, CONST_COLS + _width)
    CONST_COLS += _width

ROW_WIDTHS = {"swa_q": DH, "swa_k": DH, "mem_q": DH, "mem_k": DH, "sinks": SWA_HEADS, "b_router": 32}
ROW_AT = {}
ROW_COLS = 0
for _name, _width in ROW_WIDTHS.items():
    ROW_AT[_name] = (ROW_COLS, ROW_COLS + _width)
    ROW_COLS += _width


def shape_constants(n_experts):
    c = np.zeros((P, CONST_COLS), np.float32)

    def put(name, a):
        lo, hi = CONST_AT[name]
        c[:a.shape[0], lo:hi] = a

    p = np.arange(P)
    put("ident", np.eye(P))
    dist, band = [], []
    for key0, frame0, frames in ((0, 0, 2 * P), (P, P, P)):
        m, n = key0 + p[:, None], frame0 + np.arange(frames)[None, :]
        dist.append(np.where(m // CHUNK <= n // CHUNK, np.abs(n - m), FAR))
    put("dist", np.concatenate(dist, 1))
    for frame0, keys in ((0, P), (P, 2 * P)):
        n, m = frame0 + p[:, None], np.arange(keys)[None, :]
        ahead = n // CHUNK - m // CHUNK
        band.append(np.where((ahead >= 0) & (ahead <= 1), 0.0, MASKED))
    put("band", np.concatenate(band, 1))
    inv = np.float32(ROPE_THETA) ** (-np.arange(0, DH, 2, dtype=np.float32) / np.float32(DH))
    put("inv", np.broadcast_to(inv.astype(np.float32), (P, DH // 2)))
    put("iota", np.broadcast_to(np.arange(SLOTS), (P, SLOTS)))
    put("before", p[:, None] < p[None, :])
    put("ones", np.ones((P, P)))
    put("half", np.broadcast_to(p // SLOTS, (P, P)))
    pair = np.arange(18) % (n_experts // 2)
    put("row", p[:, None] - 2.0 * pair[None, :])
    return c


def layer_kernel(nc, x, mem, positions, norm_gains, w_in, w_mem_kv, small_params, w_out, w_router, w_up, b_up,
                 w_down, b_down, constants, out):
    _, S, D = x.shape
    E = w_router.shape[2]
    F = w_down.shape[2]
    TILES = S // P
    KD = D // P
    KF = F // P
    PAIRS = E // 2
    BLOCKS = S // SLOTS
    N = 512
    MQ_BANKS = RV_BANKS = RET_O_BANKS = (2, 7)
    MEMT_BANKS = MIXED_BANKS = (0, 1, 3, 4)
    HEAD_BANKS = (5, 6, 0, 1)
    RET_BANKS = (3, 4, 2, 7)
    H2_BANKS = (2, 7, 5, 6)
    ROUTE_BANKS = (2, 5)
    LAST_BANKS = (0, 1, 2, 3)
    assert (S, D, F, E) == (256, 1024, 1024, 32) and mem.shape[1] == S

    MIX_CHUNKS = 8
    UP_CHUNKS = KD
    DOWN_CHUNKS = KF // 2
    PAIR_CHUNKS = UP_CHUNKS + DOWN_CHUNKS
    assert PAIR_CHUNKS % RING == 0
    PAIR_LAPS = PAIR_CHUNKS // RING
    EXTRA = 2
    BASE = MIX_CHUNKS - EXTRA

    with ExitStack() as ctx:
        def sb(name, shape, dt=F32):
            return ctx.enter_context(nc.sbuf_tensor(name, shape, dt))

        def sem(name):
            return ctx.enter_context(nc.semaphore(name))

        psum = ctx.enter_context(nc.psum_tensor("psum", [P, 8, N], F32))

        ring = sb("ring", [P, RING, SLOT_COLS])
        xy = sb("xy", [P, TILES, D])
        const = sb("const", [P, CONST_COLS])
        norm_rows = sb("norm_rows", [3 * KD, P])
        norm_gain = sb("norm_gain", [P, 3 * KD])
        param_row = sb("param_row", [1, ROW_COLS])
        param = sb("param", [P, ROW_COLS])
        wr = sb("wr", [P, KD, E])
        small = sb("small", [P, 256])
        pos_i = sb("pos_i", [P, TILES], I32)
        top_i = sb("top_i", [P, TILES, 8], U32)
        count_i = sb("count_i", [1, 1], I32)

        KIB = 256
        WORK_KIB = 88
        work = sb("work", [P, WORK_KIB * KIB])
        at = [0]

        def carve(cols):
            at[0] += cols
            assert at[0] <= WORK_KIB * KIB
            return work[:, at[0] - cols:at[0]]

        xn = carve(8 * KIB).rearrange("p (t d) -> p t d", t=TILES)
        hT = carve(8 * KIB).rearrange("p (k n) -> p k n", k=KD)
        mix_start = at[0]
        memT = carve(8 * KIB).rearrange("p (k n) -> p k n", k=KD)
        catT = carve(8 * KIB).rearrange("p (k n) -> p k n", k=KD)
        rqk = carve(4 * KIB).rearrange("p (t n) -> p t n", t=TILES)
        rv = carve(4 * KIB).rearrange("p (t n) -> p t n", t=TILES)
        rg = carve(4 * KIB).rearrange("p (t n) -> p t n", t=TILES)
        sqk = carve(3 * KIB).rearrange("p (t n) -> p t n", t=TILES)
        sv = carve(1 * KIB).rearrange("p (t n) -> p t n", t=TILES)
        mq = carve(2 * KIB).rearrange("p (t n) -> p t n", t=TILES)
        mk = carve(2 * KIB).rearrange("p (t n) -> p t n", t=TILES)
        mv = carve(2 * KIB).rearrange("p (t n) -> p t n", t=TILES)
        sqT = carve(2 * KIB).rearrange("p (g n) -> p g n", g=2)
        extra_start = at[0]
        mqT = carve(2 * KIB).rearrange("p (g n) -> p g n", g=2)
        mkT = carve(2 * KIB).rearrange("p (g n) -> p g n", g=2)
        decay = carve(6 * KIB).rearrange("p (h n) -> p h n", h=RET_HEADS)
        swaP = carve(6 * KIB).rearrange("p (h n) -> p h n", h=SWA_HEADS)
        memP = carve(8 * KIB).rearrange("p (h t n) -> p h t n", h=MEM_HEADS, t=TILES)
        tmpA = carve(4 * KIB)
        tmpB = carve(4 * KIB)
        retP = xn.rearrange("p t d -> p (t d)")[:, 0:1536].rearrange("p (h n) -> p h n", h=RET_HEADS)
        rope_r = xn.rearrange("p t d -> p (t d)")[:, 0:1024].rearrange("p (t n) -> p t n", t=TILES)
        rkT = xn.rearrange("p t d -> p (t d)")[:, 1536:2048].rearrange("p (g n) -> p g n", g=2)
        rqT = hT.rearrange("p k n -> p (k n)")[:, 1536:2048].rearrange("p (g n) -> p g n", g=2)
        skT = tmpB[:, 768:1024]
        rope_s = swaP.rearrange("p h n -> p (h n)")[:, 0:768].rearrange("p (t n) -> p t n", t=TILES)
        swaPT = hT.rearrange("p k n -> p (k n)")[:, 0:1536].rearrange("p (h n) -> p h n", h=SWA_HEADS)
        memPT = memT.rearrange("p (h b) n -> p h b n", b=2)

        at[0] = mix_start
        XT = carve(4 * KIB).rearrange("p (k s) -> p k s", k=KD)
        actT = carve(4 * KIB).rearrange("p (k s) -> p k s", k=KF)
        glu = carve(4 * KIB)
        lin = carve(4 * KIB)
        sig = carve(4 * KIB)
        Y = carve(4 * KIB)
        sel = carve(1 * KIB).rearrange("p (t s) -> p t s", t=TILES)
        gated = carve(1 * KIB).rearrange("p (t s) -> p t s", t=TILES)
        back = carve(1 * KIB).rearrange("p (t n) -> p t n", t=TILES)
        whose = carve(KIB // 2)
        place = carve(TILES * (BLOCKS * E + 2)).rearrange("p (t c) -> p t c", t=TILES)
        bup_rows = carve(8 * KIB)
        gates = carve(TILES * E).rearrange("p (t e) -> p t e", t=TILES)
        assert at[0] <= extra_start
        extra = work[:, extra_start:extra_start + EXTRA * SLOT_COLS].rearrange("p (s n) -> p s n", s=EXTRA)
        logits = glu[:, 0:TILES * E].rearrange("p (t e) -> p t e", t=TILES)
        chosen = glu[:, 64:64 + TILES * E].rearrange("p (t e) -> p t e", t=TILES)
        hits = lin[:, 0:256].rearrange("p (t j e) -> p t j e", t=TILES, j=TOP_K)
        hitg = lin[:, 256:512].rearrange("p (t j e) -> p t j e", t=TILES, j=TOP_K)

        used = [0]

        def cols(n):
            used[0] += n
            return small[:, used[0] - n:used[0]]

        ss_mem, rs_mem = cols(TILES), cols(TILES)
        ss_x, rs_x, neg_rs_x = cols(TILES), cols(TILES), cols(TILES)
        ss_mk, rs_mk = cols(8), cols(8)
        ss_mq, rs_mq = cols(8), cols(8)
        ss_s, rs_s = cols(12), cols(12)
        ss_ret, rs_ret = cols(8), cols(8)
        ss_ffn, rs_ffn = cols(TILES), cols(TILES)
        mem_max, mem_neg, mem_sum, mem_inv = cols(8), cols(8), cols(8), cols(8)
        swa_max, swa_neg, swa_sum, swa_sink, swa_inv = cols(8), cols(8), cols(8), cols(8), cols(8)
        minus_half = cols(16)
        posf = cols(TILES)
        top_v = cols(16).rearrange("p (t j) -> p t j", t=TILES)
        top_x = cols(8).rearrange("p (t j) -> p t j", t=TILES)
        top_neg, top_sum, top_inv = cols(TILES), cols(TILES), cols(TILES)
        top_g = cols(8).rearrange("p (t j) -> p t j", t=TILES)
        count_f = cols(1)
        angle = sb("angle", [P, 4, TILES, DH // 2])
        turns = sb("turns", [P, 2, TILES, DH // 2])
        cos2 = sb("cos2", [P, TILES, DH])
        sin2 = sb("sin2", [P, TILES, DH])
        cosr = sb("cosr", [P, TILES, DH])
        sinr = sb("sinr", [P, TILES, DH])
        swa_gain = sb("swa_gain", [P, 6, DH])

        def constant(name, rows=P):
            lo, hi = CONST_AT[name]
            return const[0:rows, lo:hi]

        def parameter(name):
            lo, hi = ROW_AT[name]
            return param[:, lo:hi]

        ident = constant("ident")

        const_in, tables_in, x_in, mem_in = (
            sem("const_in"), sem("tables_in"), [sem("x_in0"), sem("x_in1")], [sem("mem_in0"), sem("mem_in1")])
        pos_in, params_in, router_in = sem("pos_in"), sem("params_in"), sem("router_in")
        bup_in, bdown_in, out_written = sem("bup_in"), sem("bdown_in"), sem("out_written")
        extra_in = [sem(f"extra_in{i}") for i in range(EXTRA)]
        landed = [sem(f"landed{i}") for i in range(RING)]
        slot_used = sem("slot_used")
        dve_step, pool_step = sem("dve_step"), sem("pool_step")
        squares = {n: sem(f"squares_{n}") for n in ("mem", "x", "mk", "mq", "swa", "ret", "ffn")}
        sums = {n: sem(f"sums_{n}") for n in ("mk", "mq", "swa", "ret")}
        rstd = {n: sem(f"rstd_{n}") for n in ("mem", "x", "mk", "mq", "swa", "ret", "ffn")}
        params_spread, params_ready = sem("params_spread"), sem("params_ready")
        angles_ready, trig_ready, decay_ready = sem("angles_ready"), sem("trig_ready"), sem("decay_ready")
        rotation_ready = sem("rotation_ready")
        mem_turned, memT_ready = sem("mem_turned"), sem("memT_ready")
        x_turned, hT_ready = sem("x_turned"), sem("hT_ready")
        mkv_done, mv_ready, mk_ready = sem("mkv_done"), sem("mv_ready"), sem("mk_ready")
        mq_done, mq_ready = sem("mq_done"), sem("mq_ready")
        swa_done, swa_qk_ready, sv_ready = sem("swa_done"), sem("swa_qk_ready"), sem("sv_ready")
        rqk_done, rqk_ready = sem("rqk_done"), sem("rqk_ready")
        rv_done, rv_ready = sem("rv_done"), sem("rv_ready")
        rg_done, rg_exp, rg_ready = sem("rg_done"), sem("rg_exp"), sem("rg_ready")
        turnedA, turnsA_ready = sem("turnedA"), sem("turnsA_ready")
        turnedB, turnsB_ready = sem("turnedB"), sem("turnsB_ready")
        mem_scored, mem_max_ready, mem_exp, memP_ready = (
            sem("mem_scored"), sem("mem_max_ready"), sem("mem_exp"), sem("memP_ready"))
        swa_scored, swa_max_ready, swa_exp, swaP_ready = (
            sem("swa_scored"), sem("swa_max_ready"), sem("swa_exp"), sem("swaP_ready"))
        ret_scored, retP_ready = sem("ret_scored"), sem("retP_ready")
        memP_turned, memPT_ready = sem("memP_turned"), sem("memPT_ready")
        swaP_turned, swaPT_ready = sem("swaP_turned"), sem("swaPT_ready")
        mem_read, swa_read, ret_read = sem("mem_read"), sem("swa_read"), sem("ret_read")
        cat_mem, cat_swa, ret_gated, ret_turned, cat_ret = (
            sem("cat_mem"), sem("cat_swa"), sem("ret_gated"), sem("ret_turned"), sem("cat_ret"))
        mixed, x2_ready, xn2_ready = sem("mixed"), sem("x2_ready"), sem("xn2_ready")
        h2_turned, h2T_ready, routed, top_ready, top_exp = (
            sem("h2_turned"), sem("h2T_ready"), sem("routed"), sem("top_ready"), sem("top_exp"))
        chosen_ready, gates_ready, placed, count_ready = (
            sem("chosen_ready"), sem("gates_ready"), sem("placed"), sem("count_ready"))
        gates_turned = sem("gates_turned")
        sel_ready, gated_ready, whose_ready = sem("sel_ready"), sem("gated_ready"), sem("whose_ready")
        biased, gathered, xt_ready = sem("biased"), sem("gathered"), sem("xt_ready")
        glu_ready, lin1_ready, sig_ready, act_ready = sem("glu_ready"), sem("lin1_ready"), sem("sig_ready"), sem("act_ready")
        up_read = sem("up_read")
        gated_turned, back_ready = sem("gated_turned"), sem("back_ready")
        act_turned, actT_ready = sem("act_turned"), sem("actT_ready")
        down_half, y_ready, combined, y_added = sem("down_half"), sem("y_ready"), sem("combined"), sem("y_added")

        w_mem_sb = ring[:, 0, :].rearrange("p (k n) -> p k n", k=KD)
        w_main_sb = [ring[:, 1 + k // 2, (k % 2) * 2048:(k % 2 + 1) * 2048] for k in range(KD)]
        w_mq_sb = ring[:, 5, 0:2048].rearrange("p (k n) -> p k n", k=KD)
        mem_sb = ring[:, 5, 2048:4096].rearrange("p (t d) -> p t d", t=TILES)
        w_out_sb = [ring[:, (6 + k // 4) % RING, (k % 4) * D:(k % 4 + 1) * D] for k in range(KD)]

        def up_slot(j):
            s = (BASE + j) % RING
            return ring[:, s, :].rearrange("p (e n) -> p e n", e=2)

        def down_slot(j):
            s = (BASE + UP_CHUNKS + j) % RING
            return ring[:, s, :].rearrange("p (e k n) -> p e k n", e=2, k=2)

        def chunk_landed(eng, q, j):
            g = BASE + j
            eng.wait_ge(landed[g % RING], q * (16 * PAIR_LAPS) + 16 * (g // RING + 1))

        def chunks_used(q, j):
            return q * PAIR_CHUNKS + (BASE + j)

        block = ctx.enter_context(nc.Block())

        def overflowing(eng):
            eng.wait_ge(count_ready, 1)
            return eng.value_load(count_i[0:1, 0:1], min_val=0, max_val=S) > SLOTS

        def further_blocks(eng, pair):
            with eng.Fori(1, BLOCKS) as b:
                with eng.Fori(0, PAIRS) as p:
                    pair(b * PAIRS + p, p)

        @block.sync
        def _(sp):
            sp.dma_start(const[:, 0:CONST_FIRST], constants[:, 0:CONST_FIRST]).then_inc(const_in, 16)
            for t in range(TILES):
                sp.dma_start(xy[:, t], x[0, t * P:(t + 1) * P, :]).then_inc(x_in[t], 16)
            sp.dma_start(w_mq_sb, w_in[0, :, 2048:2304].rearrange("(k p) n -> p k n", p=P)).then_inc(landed[5], 16)
            for t in range(TILES):
                sp.dma_start(mem_sb[:, t], mem[0, t * P:(t + 1) * P, :]).then_inc(mem_in[t], 16)
            sp.dma_start(w_mem_sb, w_mem_kv[0].rearrange("(k p) n -> p k n", p=P)).then_inc(landed[0], 16)
            sp.dma_start(const[:, CONST_FIRST:], constants[:, CONST_FIRST:]).then_inc(tables_in, 16)
            for s in range(4):
                sp.dma_start(ring[:, 1 + s, :].rearrange("p (k n) -> p k n", k=2),
                             w_in[0, 2 * s * P:(2 * s + 2) * P, 0:2048].rearrange("(k p) n -> p k n", p=P)
                             ).then_inc(landed[1 + s], 16)
            sp.dma_start(wr[:], w_router[0].rearrange("(k p) e -> p k e", p=P)).then_inc(router_in, 16)
            for s in range(2):
                sp.wait_ge(slot_used, s + 1)
                sp.dma_start(ring[:, s, :].rearrange("p (k n) -> p k n", k=4),
                             w_out[0, 4 * s * P:(4 * s + 4) * P, :].rearrange("(k p) n -> p k n", p=P)
                             ).then_inc(landed[s], 16)

            def load(dst, p, j):
                if j < UP_CHUNKS:
                    src = w_up[0, bass.ds(2 * p, 2), j * P:(j + 1) * P, :].rearrange("e r n -> r e n")
                else:
                    i = j - UP_CHUNKS
                    src = w_down[0, bass.ds(2 * p, 2), 2 * i * P:(2 * i + 2) * P, :].rearrange(
                        "e (r k) n -> r e (k n)", k=2)
                return sp.dma_start(dst.rearrange("r (e n) -> r e n", e=2), src)

            def pair(q, p, first=0):
                for j in range(first, PAIR_CHUNKS):
                    g = BASE + j
                    sp.wait_ge(slot_used, q * PAIR_CHUNKS + (g - RING + 1))
                    load(ring[:, g % RING, :], p, j).then_inc(landed[g % RING], 16)
                    if first and j == first + 3:
                        sp.wait_ge(ret_turned, TILES)
                        for i in range(EXTRA):
                            load(extra[:, i], p, i).then_inc(extra_in[i], 16)

            def store_result(q_end):
                for n in range(2):
                    for t in range(TILES):
                        sp.wait_ge(y_added, 4 * q_end + 2 * n + t + 1)
                        sp.dma_start(out[0, t * P:(t + 1) * P, n * N:(n + 1) * N], xy[:, t, n * N:(n + 1) * N]
                                     ).then_inc(out_written, 16)

            pair(0, 0, EXTRA)
            with sp.Fori(1, PAIRS) as q:
                pair(q, q)
            with sp.If(overflowing(sp)):
                further_blocks(sp, pair)
                store_result(BLOCKS * PAIRS)
            with sp.Else():
                store_result(PAIRS)
            sp.wait_ge(out_written, 16 * 4)

        @block.gpsimd
        def _(pool):
            count = [0]

            def step(ins):
                count[0] += 1
                ins.then_inc(pool_step, 1)
                pool.wait_ge(pool_step, count[0])

            step(nc.gpsimd.memset(minus_half, -0.5))

            def root(name, summed, done, ss, rs, width):
                n = ss.shape[1]
                pool.wait_ge(summed, done)
                step(nc.gpsimd.tensor_scalar(ss, ss, 1.0 / width, EPS, ALU.mult, ALU.add))
                nc.gpsimd.tensor_tensor(rs, ss, minus_half[:, 0:n], ALU.pow).then_inc(rstd[name], 1)

            root("x", squares["x"], TILES, ss_x, rs_x, D)
            root("mem", squares["mem"], TILES, ss_mem, rs_mem, D)
            root("mq", sums["mq"], 1, ss_mq, rs_mq, DH)
            root("mk", sums["mk"], 1, ss_mk, rs_mk, DH)
            root("swa", sums["swa"], 1, ss_s, rs_s, DH)
            for t in range(TILES):
                root("ret", sums["ret"], t + 1, ss_ret[:, 4 * t:4 * t + 4], rs_ret[:, 4 * t:4 * t + 4], RET_DV)
            for t in range(TILES):
                root("ffn", squares["ffn"], t + 1, ss_ffn[:, t:t + 1], rs_ffn[:, t:t + 1], D)

        @block.scalar
        def _(act):
            act.dma_start(norm_rows[:], norm_gains).then_inc(params_in, 16)
            act.dma_start(param_row[:], small_params).then_inc(params_in, 16)
            act.dma_start(pos_i[:], positions).then_inc(pos_in, 16)

            def row_squares(name, src, ss, arrived, other):
                for t in range(TILES):
                    act.wait_ge(arrived[t], 16)
                    if t > 0:
                        act.wait_ge(squares[name], t)
                    nc.scalar.activation(other, src[:, t], ACT.Square, accum_out=ss[:, t:t + 1]
                                         ).then_inc(squares[name], 1)

            row_squares("x", xy, ss_x, x_in, tmpB)
            row_squares("mem", mem_sb, ss_mem, mem_in, tmpA)
            act.wait_ge(params_ready, 2)
            for k in range(KD):
                if k % 2 == 0:
                    act.wait_ge(mem_turned, k // 2 + 1)
                nc.scalar.activation(memT[:, k], psum[:, MEMT_BANKS[k // 2], (k % 2) * 256:(k % 2 + 1) * 256], ACT.Copy,
                                     scale=norm_gain[:, KD + k:KD + k + 1]).then_inc(memT_ready, 1)
            act.wait_ge(rstd["x"], 1)
            act.wait_ge(squares["mem"], TILES)
            for t in range(TILES):
                act.wait_ge(mq_done, t + 1)
                nc.scalar.activation(tmpA[:, 512 + t * 256:768 + t * 256], psum[:, MQ_BANKS[t], 0:256], ACT.Square,
                                     scale=rs_x[:, t:t + 1]).then_inc(squares["mq"], 1)
            act.wait_ge(angles_ready, 1)
            nc.scalar.activation(angle[:, 2:4], angle[:, 0:2], ACT.Sin).then_inc(trig_ready, 1)
            act.wait_ge(tables_in, 16)
            for h in range(RET_HEADS):
                nc.scalar.activation(decay[:, h], constant("dist"), ACT.Exp,
                                     scale=float(np.log1p(-(2.0 ** (-5.0 - h))))).then_inc(decay_ready, 1)
            act.wait_ge(rstd["mem"], 1)
            for t in range(TILES):
                act.wait_ge(mkv_done, t + 1)
                nc.scalar.activation(tmpA[:, t * 256:(t + 1) * 256], psum[:, 5 + t, 0:256], ACT.Square,
                                     scale=rs_mem[:, t:t + 1]).then_inc(squares["mk"], 1)
                nc.scalar.activation(mv[:, t], psum[:, 5 + t, 256:512], ACT.Copy, scale=rs_mem[:, t:t + 1]
                                     ).then_inc(mv_ready, 1)
            for t in range(TILES):
                act.wait_ge(swa_done, t + 1)
                nc.scalar.activation(tmpB[:, t * 384:(t + 1) * 384], psum[:, t, 0:384], ACT.Square,
                                     scale=rs_x[:, t:t + 1]).then_inc(squares["swa"], 1)
                nc.scalar.activation(sv[:, t], psum[:, t, 384:512], ACT.Copy, scale=rs_x[:, t:t + 1]
                                     ).then_inc(sv_ready, 1)
            for t in range(TILES):
                act.wait_ge(rv_done, t + 1)
                nc.scalar.activation(rv[:, t], psum[:, RV_BANKS[t]], ACT.Copy, scale=rs_x[:, t:t + 1]
                                     ).then_inc(rv_ready, 1)
            for n, (dst, b) in enumerate(((mkT, 5), (mqT, 6), (sqT, 0))):
                act.wait_ge(turnedA, n + 1)
                nc.scalar.activation(dst, psum[:, b].rearrange("p (g n) -> p g n", g=2), ACT.Copy
                                     ).then_inc(turnsA_ready, 1)
            act.wait_ge(turnedA, 4)
            nc.scalar.activation(skT, psum[:, 1, 0:256], ACT.Copy).then_inc(turnsA_ready, 1)

            def gate_exp(t):
                act.wait_ge(rg_done, t + 1)
                nc.scalar.activation(rg[:, t], psum[:, 3 + t], ACT.Exp, scale=neg_rs_x[:, t:t + 1]).then_inc(rg_exp, 1)

            act.wait_ge(rotation_ready, 1)
            gate_exp(0)
            for h in range(MEM_HEADS):
                act.wait_ge(mem_max_ready, h + 1)
                for t in range(TILES):
                    c = 2 * h + t
                    nc.scalar.activation(memP[:, h, t], psum[:, HEAD_BANKS[h], t * 256:(t + 1) * 256], ACT.Exp, scale=SCALE,
                                         bias=mem_neg[:, c:c + 1], accum_out=mem_sum[:, c:c + 1]).then_inc(mem_exp, 1)
            gate_exp(1)
            for n, (dst, b) in enumerate(((rqT, 2), (rkT, 7))):
                act.wait_ge(turnedB, n + 1)
                nc.scalar.activation(dst, psum[:, b].rearrange("p (g n) -> p g n", g=2), ACT.Copy
                                     ).then_inc(turnsB_ready, 1)
            for h in range(SWA_HEADS):
                act.wait_ge(swa_max_ready, h + 1)
                for t, (lo, hi) in enumerate(((0, P), (P, 3 * P))):
                    c = 2 * h + t
                    nc.scalar.activation(swaP[:, h, lo:hi], swaP[:, h, lo:hi], ACT.Exp, bias=swa_neg[:, c:c + 1],
                                         accum_out=swa_sum[:, c:c + 1]).then_inc(swa_exp, 1)
                    nc.scalar.activation(swa_sink[:, c:c + 1], parameter("sinks")[:, h:h + 1], ACT.Exp,
                                         bias=swa_neg[:, c:c + 1]).then_inc(swa_exp, 1)
            for h in range(MEM_HEADS):
                act.wait_ge(memP_turned, h + 1)
                nc.scalar.activation(memPT[:, h], psum[:, HEAD_BANKS[h]].rearrange("p (b n) -> p b n", b=2), ACT.Copy
                                     ).then_inc(memPT_ready, 1)
            for h in range(SWA_HEADS):
                act.wait_ge(swaP_turned, h + 1)
                nc.scalar.activation(swaPT[:, h], psum[:, HEAD_BANKS[h], 0:3 * P], ACT.Copy).then_inc(swaPT_ready, 1)
            for t in range(TILES):
                act.wait_ge(ret_read, t + 1)
                nc.scalar.activation(tmpA[:, t * N:(t + 1) * N], psum[:, RET_O_BANKS[t]], ACT.Square
                                     ).then_inc(squares["ret"], 1)
            act.wait_ge(mem_read, 1)
            nc.scalar.activation(catT[:, 6:8], psum[:, 3].rearrange("p (g n) -> p g n", g=2), ACT.Copy
                                 ).then_inc(cat_mem, 1)
            act.wait_ge(swa_read, 1)
            act.dma_start(bup_rows[0:E, :], b_up[0]).then_inc(bup_in, 16)
            nc.scalar.activation(catT[:, 4:6], psum[:, 4].rearrange("p (g n) -> p g n", g=2), ACT.Copy
                                 ).then_inc(cat_swa, 1)
            for t in range(TILES):
                act.wait_ge(ret_turned, t + 1)
                nc.scalar.activation(catT[:, 0:4, t * P:(t + 1) * P], psum[:, 5 + t].rearrange("p (h n) -> p h n", h=4),
                                     ACT.Copy).then_inc(cat_ret, 1)
            act.wait_ge(y_ready, 2)
            act.dma_start(Y[0:E, :], b_down[0]).then_inc(bdown_in, 16)
            for t in range(TILES):
                act.wait_ge(x2_ready, 2 * t + 2)
                nc.scalar.activation(rqk.rearrange("p t n -> p (t n)"), xy[:, t], ACT.Square,
                                     accum_out=ss_ffn[:, t:t + 1]).then_inc(squares["ffn"], 1)
                act.wait_ge(rstd["ffn"], t + 1)
                nc.scalar.activation(xn[:, t], xy[:, t], ACT.Copy, scale=rs_ffn[:, t:t + 1]).then_inc(xn2_ready, 1)
                act.wait_ge(top_ready, t + 1)
                nc.scalar.activation(top_g[:, t], top_v[:, t, 0:TOP_K], ACT.Exp, bias=top_neg[:, t:t + 1],
                                     accum_out=top_sum[:, t:t + 1]).then_inc(top_exp, 1)
            act.wait_ge(gates_turned, 1)
            nc.scalar.activation(back[0:E], psum[0:E, 4, 0:256].rearrange("p (t n) -> p t n", t=TILES), ACT.Copy
                                 ).then_inc(back_ready, 1)

            def pair(q, p):
                act.wait_ge(glu_ready, q + 1)
                nc.scalar.activation(sig, glu, ACT.Sigmoid, scale=ALPHA).then_inc(sig_ready, 1)
                act.wait_ge(gated_turned, q + 1)
                nc.scalar.activation(back, psum[:, 4, 0:256].rearrange("p (t n) -> p t n", t=TILES), ACT.Copy
                                     ).then_inc(back_ready, 1)
                for i in range(2):
                    act.wait_ge(act_turned, 2 * q + (i + 1))
                    nc.scalar.activation(actT[:, 4 * i:4 * i + 4], psum[:, 6 + i].rearrange("p (k s) -> p k s", k=4),
                                         ACT.Copy).then_inc(actT_ready, 1)
                for n in range(2):
                    if n == 0:
                        act.wait_ge(down_half, q + 1)
                    else:
                        act.wait_ge(slot_used, chunks_used(q, PAIR_CHUNKS))
                    nc.scalar.activation(Y[:, n * N:(n + 1) * N], psum[:, 4 + n], ACT.Copy).then_inc(y_ready, 1)

            with act.Fori(0, PAIRS) as q:
                pair(q, q)
            with act.If(overflowing(act)):
                further_blocks(act, pair)

        @block.vector
        def _(dve):
            V = nc.vector
            count = [0]

            def step(ins):
                count[0] += 1
                ins.then_inc(dve_step, 1)
                dve.wait_ge(dve_step, count[0])

            dve.wait_ge(params_spread, 2)
            V.tensor_copy(norm_gain[:], psum[:, 7, 0:3 * KD]).then_inc(params_ready, 1)
            V.tensor_copy(param[:], psum[:, 7, 64:64 + ROW_COLS]).then_inc(params_ready, 1)

            def turned_gain(dst, src, gain0, k0, kn, n):
                g = norm_gain[:, gain0 + k0:gain0 + k0 + kn].unsqueeze(2).to_broadcast([P, kn, n])
                return V.tensor_tensor(dst, src.rearrange("p (k n) -> p k n", k=kn), g, ALU.mult)

            dve.wait_ge(params_ready, 2)
            for i in range(4):
                dve.wait_ge(x_turned, i + 1)
                turned_gain(hT[:, 2 * i:2 * i + 2], psum[:, 3 + i], 0, 2 * i, 2, 256).then_inc(hT_ready, 1)

            dve.wait_ge(pos_in, 16)
            step(V.tensor_copy(posf, pos_i[:]))
            for t in range(TILES):
                step(V.tensor_scalar(angle[:, 0, t], constant("inv"), posf[:, t:t + 1], None, ALU.mult))
            step(V.tensor_scalar(turns[:, 0], angle[:, 0], float(1 / (2 * np.pi)), ROUND, ALU.mult, ALU.add))
            step(V.tensor_scalar(turns[:, 1], angle[:, 0], float(1 / (2 * np.pi)), 0.25, ALU.mult, ALU.add))
            step(V.tensor_scalar(turns[:, 1], turns[:, 1], ROUND, None, ALU.add))
            step(V.tensor_scalar(turns[:], turns[:], ROUND, None, ALU.subtract))
            step(V.tensor_copy(angle[:, 1], angle[:, 0]))
            for part in (TWO_PI_HI, TWO_PI_MID, TWO_PI_LO):
                step(V.scalar_tensor_tensor(out=angle[:, 0:2], in0=turns[:], scalar=-part, in1=angle[:, 0:2],
                                            op0=ALU.mult, op1=ALU.add))
            step(V.tensor_scalar(angle[:, 1], angle[:, 1], float(np.pi / 2), None, ALU.add))
            V.tensor_scalar(angle[:, 0:2], angle[:, 0:2], PI, -PI, ALU.min, ALU.max).then_inc(angles_ready, 1)

            dve.wait_ge(trig_ready, 1)
            V.tensor_copy(cos2[:, :, 0:32], angle[:, 3])
            V.tensor_copy(cos2[:, :, 32:64], angle[:, 3])
            V.tensor_scalar(sin2[:, :, 0:32], angle[:, 2], -1.0, None, ALU.mult)
            V.tensor_copy(sin2[:, :, 32:64], angle[:, 2])
            V.tensor_copy(swa_gain[:, 0:4], parameter("swa_q").unsqueeze(1).to_broadcast([P, 4, DH]))
            step(V.tensor_copy(swa_gain[:, 4:6], parameter("swa_k").unsqueeze(1).to_broadcast([P, 2, DH])))
            dve.wait_ge(rstd["x"], 1)
            for t in range(TILES):
                V.tensor_scalar(cosr[:, t], cos2[:, t], rs_x[:, t:t + 1], None, ALU.mult)
                V.tensor_scalar(sinr[:, t], sin2[:, t], rs_x[:, t:t + 1], None, ALU.mult)
            V.tensor_scalar(neg_rs_x, rs_x, -1.0, None, ALU.mult).then_inc(rotation_ready, 1)

            def heads(a, n):
                return a.rearrange("p (h d) -> p h d", h=n)

            def per_head(a, n, width=DH):
                return a.unsqueeze(2).to_broadcast([P, n, width])

            def over_heads(a, n):
                return a.unsqueeze(1).to_broadcast([P, n, a.shape[1]])

            def head_sums(name, src, ss, done, n):
                dve.wait_ge(squares[name], done)
                V.tensor_reduce(ss, heads(src, n), AX_X, ALU.add).then_inc(sums[name], 1)

            def normed(dst, src, rs, row_rs, n):
                step(V.tensor_scalar(rs, rs, row_rs, None, ALU.mult))
                return V.tensor_tensor(heads(dst, n), heads(src, n), per_head(rs, n), ALU.mult)

            head_sums("mq", tmpA[:, 512:1024], ss_mq, 2, 8)
            dve.wait_ge(rstd["mq"], 1)
            for t in range(TILES):
                step(normed(mq[:, t], psum[:, MQ_BANKS[t], 0:256], rs_mq[:, 4 * t:4 * t + 4], rs_x[:, t:t + 1], 4))
                V.tensor_tensor(heads(mq[:, t], 4), heads(mq[:, t], 4), over_heads(parameter("mem_q"), 4), ALU.mult
                                ).then_inc(mq_ready, 1)
            head_sums("mk", tmpA[:, 0:512], ss_mk, 2, 8)
            dve.wait_ge(rstd["mk"], 1)
            dve.wait_ge(mv_ready, 2)
            for t in range(TILES):
                step(normed(mk[:, t], psum[:, 5 + t, 0:256], rs_mk[:, 4 * t:4 * t + 4], rs_mem[:, t:t + 1], 4))
                V.tensor_tensor(heads(mk[:, t], 4), heads(mk[:, t], 4), over_heads(parameter("mem_k"), 4), ALU.mult
                                ).then_inc(mk_ready, 1)

            def rotate(dst, src, swapped, cos, sin, n):
                src, dst, swapped = heads(src, n), heads(dst, n), heads(swapped, n)
                for lo, hi in ((0, 32), (32, 64)):
                    last = V.tensor_tensor(swapped[:, :, lo:hi], src[:, :, 32 - lo:64 - lo],
                                           over_heads(sin[:, lo:hi], n), ALU.mult)
                step(last)
                step(V.tensor_tensor(dst, src, over_heads(cos, n), ALU.mult))
                return V.tensor_tensor(dst, dst, swapped, ALU.add)

            head_sums("swa", tmpB[:, 0:768], ss_s, 2, 12)
            dve.wait_ge(rstd["swa"], 1)
            dve.wait_ge(sv_ready, 2)
            for t in range(TILES):
                rs = rs_s[:, 6 * t:6 * t + 6]
                step(V.tensor_scalar(rs, rs, rs_x[:, t:t + 1], None, ALU.mult))
                V.tensor_tensor(sqk[:, t, 0:256].rearrange("p (b a d) -> p a b d", a=2, b=2),
                                psum[:, t, 0:256].rearrange("p (a b d) -> p a b d", a=2, b=2),
                                rs[:, 0:4].rearrange("p (a b) -> p a b", a=2).unsqueeze(3).to_broadcast([P, 2, 2, DH]),
                                ALU.mult)
                step(V.tensor_tensor(heads(sqk[:, t, 256:384], 2), heads(psum[:, t, 256:384], 2),
                                     per_head(rs[:, 4:6], 2), ALU.mult))
                step(V.tensor_tensor(heads(sqk[:, t], 6), heads(sqk[:, t], 6), swa_gain[:], ALU.mult))
                rotate(sqk[:, t], sqk[:, t], rope_s[:, t], cos2[:, t], sin2[:, t], 6).then_inc(swa_qk_ready, 1)
            dve.wait_ge(rotation_ready, 1)
            for t in range(TILES):
                dve.wait_ge(rqk_done, t + 1)
                rotate(rqk[:, t], psum[:, 3 + t], rope_r[:, t], cosr[:, t], sinr[:, t], 8).then_inc(rqk_ready, 1)

            def gate(t):
                dve.wait_ge(rg_exp, t + 1)
                step(V.tensor_scalar(rg[:, t], rg[:, t], 1.0, None, ALU.add))
                step(V.reciprocal(rg[:, t], rg[:, t]))
                V.scalar_tensor_tensor(out=rg[:, t], in0=psum[:, 3 + t], scalar=rs_x[:, t:t + 1], in1=rg[:, t],
                                       op0=ALU.mult, op1=ALU.mult).then_inc(rg_ready, 1)

            gate(0)
            for h in range(MEM_HEADS):
                dve.wait_ge(mem_scored, h + 1)
                step(V.tensor_reduce(mem_max[:, 2 * h:2 * h + 2], psum[:, HEAD_BANKS[h]].rearrange("p (t n) -> p t n", t=2),
                                     AX_X, ALU.max))
                V.tensor_scalar(mem_neg[:, 2 * h:2 * h + 2], mem_max[:, 2 * h:2 * h + 2], -SCALE, None, ALU.mult
                                ).then_inc(mem_max_ready, 1)
            for h in range(MEM_HEADS):
                dve.wait_ge(mem_exp, 2 * h + 2)
                step(V.reciprocal(mem_inv[:, 2 * h:2 * h + 2], mem_sum[:, 2 * h:2 * h + 2]))
                for t in range(TILES):
                    V.tensor_scalar(memP[:, h, t], memP[:, h, t], mem_inv[:, 2 * h + t:2 * h + t + 1], None, ALU.mult
                                    ).then_inc(memP_ready, 1)
            gate(1)
            for h in range(SWA_HEADS):
                dve.wait_ge(swa_scored, h + 1)
                step(V.scalar_tensor_tensor(out=swaP[:, h], in0=psum[:, HEAD_BANKS[h], 0:3 * P], scalar=SCALE,
                                            in1=constant("band"), op0=ALU.mult, op1=ALU.add))
                V.tensor_reduce(swa_max[:, 2 * h:2 * h + 1], swaP[:, h, 0:P], AX_X, ALU.max)
                step(V.tensor_reduce(swa_max[:, 2 * h + 1:2 * h + 2], swaP[:, h, P:3 * P], AX_X, ALU.max))
                V.tensor_scalar(swa_neg[:, 2 * h:2 * h + 2], swa_max[:, 2 * h:2 * h + 2],
                                parameter("sinks")[:, h:h + 1], -1.0, ALU.max, ALU.mult).then_inc(swa_max_ready, 1)
            dve.wait_ge(decay_ready, RET_HEADS)
            for h in range(RET_HEADS):
                dve.wait_ge(ret_scored, h + 1)
                V.scalar_tensor_tensor(out=retP[:, h], in0=psum[:, RET_BANKS[h], 0:3 * P], scalar=SCALE,
                                       in1=decay[:, h], op0=ALU.mult, op1=ALU.mult).then_inc(retP_ready, 1)
            for h in range(SWA_HEADS):
                dve.wait_ge(swa_exp, 4 * h + 4)
                step(V.tensor_tensor(swa_inv[:, 2 * h:2 * h + 2], swa_sum[:, 2 * h:2 * h + 2],
                                     swa_sink[:, 2 * h:2 * h + 2], ALU.add))
                step(V.reciprocal(swa_inv[:, 2 * h:2 * h + 2], swa_inv[:, 2 * h:2 * h + 2]))
                for t, (lo, hi) in enumerate(((0, P), (P, 3 * P))):
                    V.tensor_scalar(swaP[:, h, lo:hi], swaP[:, h, lo:hi], swa_inv[:, 2 * h + t:2 * h + t + 1], None,
                                    ALU.mult).then_inc(swaP_ready, 1)
            for t in range(TILES):
                head_sums("ret", tmpA[:, t * N:(t + 1) * N], ss_ret[:, 4 * t:4 * t + 4], t + 1, 4)
            for t in range(TILES):
                dve.wait_ge(rstd["ret"], t + 1)
                o = tmpB[:, t * N:(t + 1) * N]
                step(V.tensor_tensor(heads(o, 4), heads(psum[:, RET_O_BANKS[t]], 4),
                                     per_head(rs_ret[:, 4 * t:4 * t + 4], 4, RET_DV), ALU.mult))
                V.tensor_tensor(o, o, rg[:, t], ALU.mult).then_inc(ret_gated, 1)
            dve.wait_ge(cat_ret, 2)
            V.memset(back, 0.0)
            V.memset(place, -FAR)
            V.memset(Y, 0.0).then_inc(y_ready, 2)
            def add_mixed(c):
                part = xy[:, c // 2, (c % 2) * N:(c % 2 + 1) * N]
                dve.wait_ge(mixed, c + 1)
                V.tensor_tensor(part, psum[:, MIXED_BANKS[c]], part, ALU.add).then_inc(x2_ready, 1)

            def take_h2(c):
                t, i = c // 2, c % 2
                dve.wait_ge(h2_turned, c + 1)
                turned_gain(hT[:, 4 * i:4 * i + 4, t * P:(t + 1) * P], psum[:, H2_BANKS[c]], 2 * KD, 4 * i, 4, P
                            ).then_inc(h2T_ready, 1)

            def choose(t):
                dve.wait_ge(routed, t + 1)
                dve.wait_ge(rstd["ffn"], t + 1)
                step(V.scalar_tensor_tensor(out=logits[:, t], in0=psum[:, ROUTE_BANKS[t], 0:E], scalar=rs_ffn[:, t:t + 1],
                                            in1=parameter("b_router"), op0=ALU.mult, op1=ALU.add))
                step(V.max(top_v[:, t], logits[:, t]))
                V.tensor_scalar(top_neg[:, t:t + 1], top_v[:, t, 0:1], -1.0, None, ALU.mult).then_inc(top_ready, 1)
                step(V.max_index(top_i[:, t], top_v[:, t], logits[:, t]))
                step(V.tensor_copy(top_x[:, t], top_i[:, t, 0:TOP_K]))
                step(V.tensor_tensor(hits[:, t], constant("iota")[:, 0:E].unsqueeze(1).to_broadcast([P, TOP_K, E]),
                                     top_x[:, t].unsqueeze(2).to_broadcast([P, TOP_K, E]), ALU.is_equal))
                V.tensor_reduce(chosen[:, t], hits[:, t].rearrange("p j e -> p e j"), AX_X, ALU.add
                                ).then_inc(chosen_ready, 1)

            def weigh(t):
                dve.wait_ge(top_exp, t + 1)
                step(V.reciprocal(top_inv[:, t:t + 1], top_sum[:, t:t + 1]))
                step(V.tensor_scalar(top_g[:, t], top_g[:, t], top_inv[:, t:t + 1], None, ALU.mult))
                step(V.tensor_tensor(hitg[:, t], hits[:, t], top_g[:, t].unsqueeze(2).to_broadcast([P, TOP_K, E]),
                                     ALU.mult))
                V.tensor_reduce(gates[:, t], hitg[:, t].rearrange("p j e -> p e j"), AX_X, ALU.add
                                ).then_inc(gates_ready, 1)

            def build_whose(p):
                V.tensor_scalar(whose[0:E, :], constant("half", E), constant("row", E)[:, bass.ds(p, 1)], None,
                                ALU.is_equal).then_inc(whose_ready, 1)

            build_whose(0)
            add_mixed(0)
            add_mixed(1)
            take_h2(0)
            add_mixed(2)
            take_h2(1)
            choose(0)
            add_mixed(3)
            take_h2(2)
            take_h2(3)
            weigh(0)
            choose(1)
            dve.wait_ge(placed, 1)
            step(V.scalar_tensor_tensor(out=logits, in0=psum[:, 5, 64:128].rearrange("p (t e) -> p t e", t=TILES),
                                        scalar=1.0, in1=chosen, op0=ALU.add, op1=ALU.mult))
            step(V.tensor_scalar(place[:, :, 0:E], logits, -1.0, None, ALU.add))

            def build_sel(q):
                for t in range(TILES):
                    for e in range(2):
                        last = V.tensor_scalar(sel[:, t, e * SLOTS:(e + 1) * SLOTS], constant("iota"),
                                               place[:, t, bass.ds(2 * q + e, 1)], None, ALU.is_equal)
                last.then_inc(sel_ready, 1)

            def build_gated(q, p):
                for t in range(TILES):
                    for e in range(2):
                        last = V.tensor_scalar(gated[:, t, e * SLOTS:(e + 1) * SLOTS], constant("iota"),
                                               place[:, t, bass.ds(2 * q + e, 1)], gates[:, t, bass.ds(2 * p + e, 1)],
                                               ALU.is_equal, ALU.mult)
                last.then_inc(gated_ready, 1)

            def take_gathered(q, i):
                dve.wait_ge(gathered, 2 * q + (i + 1))
                turned_gain(XT[:, 4 * i:4 * i + 4], psum[:, 6 + i], 2 * KD, 4 * i, 4, P).then_inc(xt_ready, 1)

            def add_combined(q, c, banks=(6, 7, 6, 7)):
                n, t = c // 2, c % 2
                dve.wait_ge(combined, 4 * q + (c + 1))
                part = xy[:, t, n * N:(n + 1) * N]
                V.tensor_tensor(part, psum[:, banks[c]], part, ALU.add).then_inc(y_added, 1)

            build_sel(0)
            for b in range(1, BLOCKS):
                V.tensor_scalar(place[:, :, b * E:(b + 1) * E], logits, -1.0 - b * SLOTS, None, ALU.add)
            step(V.tensor_reduce(count_f, psum[:, 5, 128:160], AX_X, ALU.max))
            V.tensor_copy(count_i[:], count_f[0:1]).then_inc(count_ready, 1)
            weigh(1)
            for i in range(2):
                take_gathered(0, i)

            def pair(q, p):
                dve.wait_ge(gathered, 2 * q + 2)
                build_sel(q + 1)
                dve.wait_ge(back_ready, q + 1)
                build_gated(q, p)
                dve.wait_ge(biased, q + 1)
                build_whose(p + 1)
                dve.wait_ge(slot_used, chunks_used(q, UP_CHUNKS))
                V.tensor_scalar(glu, psum[:, 0:2].rearrange("p b n -> p (b n)"), LIMIT, None, ALU.min
                                ).then_inc(glu_ready, 1)
                V.tensor_scalar(lin, psum[:, 2:4].rearrange("p b n -> p (b n)"), LIMIT, -LIMIT, ALU.min, ALU.max
                                ).then_inc(up_read, 1)
                for i in range(2):
                    take_gathered(q + 1, i)
                dve.wait_ge(glu_ready, q + 1)
                dve.wait_ge(up_read, q + 1)
                V.scalar_tensor_tensor(out=lin, in0=lin, scalar=1.0, in1=glu, op0=ALU.add, op1=ALU.mult
                                       ).then_inc(lin1_ready, 1)
                dve.wait_ge(lin1_ready, q + 1)
                dve.wait_ge(sig_ready, q + 1)
                V.tensor_tensor(sig, lin, sig, ALU.mult).then_inc(act_ready, 1)
                for c in range(4):
                    add_combined(q, c)

            with dve.Fori(0, PAIRS) as q:
                pair(q, q)
            with dve.If(overflowing(dve)):
                further_blocks(dve, pair)
                for c in range(4):
                    add_combined(BLOCKS * PAIRS, c, LAST_BANKS)
            with dve.Else():
                for c in range(4):
                    add_combined(PAIRS, c, LAST_BANKS)

        @block.tensor
        def _(pe):
            def turn(dst, src):
                n = src.shape[0]
                return pe.transpose(dst, src, ident[0:n, 0:n])

            pe.wait_ge(const_in, 16)
            pe.wait_ge(params_in, 32)
            turn(psum[:, 7, 0:3 * KD], norm_rows[:]).then_inc(params_spread, 1)
            pe.matmul(psum[:, 7, 64:64 + ROW_COLS], constant("ones", 1), param_row[:], start=True, stop=True
                      ).then_inc(params_spread, 1)

            def turn_rows(src, banks, arrived, done):
                for t in range(TILES):
                    pe.wait_ge(arrived[t], 16)
                    for k in range(KD):
                        c = (k % 2) * 256 + t * P
                        mm = turn(psum[:, banks[k // 2], c:c + P], src[:, t, k * P:(k + 1) * P])
                        if t == TILES - 1 and k % 2 == 1:
                            mm.then_inc(done, 1)

            turn_rows(xy, (3, 4, 5, 6), x_in, x_turned)
            pe.wait_ge(params_ready, 2)
            pe.wait_ge(landed[5], 16)
            for t in range(TILES):
                for k in range(KD):
                    if t == 0 and k % 2 == 0:
                        pe.wait_ge(hT_ready, k // 2 + 1)
                    mm = pe.matmul(psum[:, MQ_BANKS[t], 0:256], hT[:, k, t * P:(t + 1) * P], w_mq_sb[:, k],
                                   start=k == 0, stop=k == KD - 1)
                mm.then_inc(mq_done, 1)
            turn_rows(mem_sb, MEMT_BANKS, mem_in, mem_turned)
            pe.wait_ge(landed[0], 16)
            for t in range(TILES):
                for k in range(KD):
                    if t == 0:
                        pe.wait_ge(memT_ready, k + 1)
                    mm = pe.matmul(psum[:, 5 + t], memT[:, k, t * P:(t + 1) * P], w_mem_sb[:, k],
                                   start=k == 0, stop=k == KD - 1)
                mm.then_inc(mkv_done, 1)

            for k in range(KD):
                pe.wait_ge(landed[1 + k // 2], 16)
                for t in range(TILES):
                    mm = pe.matmul(psum[:, t], hT[:, k, t * P:(t + 1) * P], w_main_sb[k][:, 3 * N:4 * N],
                                   start=k == 0, stop=k == KD - 1)
                    if k == 0 and t == 0:
                        mm.then_inc(slot_used, 1)
                    if k == KD - 1:
                        mm.then_inc(swa_done, 1)

            def project(n, t, b, done):
                for k in range(KD):
                    mm = pe.matmul(psum[:, b], hT[:, k, t * P:(t + 1) * P], w_main_sb[k][:, n * N:(n + 1) * N],
                                   start=k == 0, stop=k == KD - 1)
                mm.then_inc(done, 1)

            project(0, 0, 3, rqk_done)
            project(0, 1, 4, rqk_done)
            for t in range(TILES):
                pe.wait_ge(mq_ready, t + 1)
                project(1, t, RV_BANKS[t], rv_done)

            def turn_heads(src, b, groups, done):
                for g in range(groups):
                    for t in range(TILES):
                        c = g * 256 + t * P
                        mm = turn(psum[:, b, c:c + P], src(t, g))
                mm.then_inc(done, 1)

            pe.wait_ge(mk_ready, 2)
            pe.wait_ge(mv_ready, 2)
            turn_heads(lambda t, g: mk[:, t, g * P:(g + 1) * P], 5, 2, turnedA)
            turn_heads(lambda t, g: mq[:, t, g * P:(g + 1) * P], 6, 2, turnedA)
            pe.wait_ge(swa_qk_ready, 2)
            pe.wait_ge(sv_ready, 2)
            turn_heads(lambda t, g: sqk[:, t, g * P:(g + 1) * P], 0, 2, turnedA)
            turn_heads(lambda t, g: sqk[:, t, 256:384], 1, 1, turnedA)
            pe.wait_ge(rqk_ready, 1)
            project(2, 0, 3, rg_done)
            pe.wait_ge(turnsA_ready, 4)
            for h in range(MEM_HEADS):
                r = DH * (h % 2)
                for t in range(TILES):
                    mm = pe.matmul(psum[:, HEAD_BANKS[h], t * 256:(t + 1) * 256], mqT[r:r + DH, h // 2, t * P:(t + 1) * P],
                                   mkT[r:r + DH, h // 2, :], start=True, stop=True)
                mm.then_inc(mem_scored, 1)
            pe.wait_ge(rqk_ready, 2)
            project(2, 1, 4, rg_done)
            pe.wait_ge(rv_ready, 2)
            turn(psum[:, 2, 0:P], rqk[:, 0, 0:P]).then_inc(slot_used, 5)
            turn_heads(lambda t, g: rqk[:, t, g * P:(g + 1) * P], 2, 2, turnedB)
            turn_heads(lambda t, g: rqk[:, t, (2 + g) * P:(3 + g) * P], 7, 2, turnedB)
            for h in range(SWA_HEADS):
                pe.wait_ge(mem_exp, 2 * h + 2)
                r = DH * (h // 2)
                for t in range(TILES):
                    mm = pe.matmul(psum[:, HEAD_BANKS[h], t * P:(2 * t + 1) * P], sqT[r:r + DH, h % 2, t * P:(t + 1) * P],
                                   skT[r:r + DH, 0:(t + 1) * P], start=True, stop=True)
                mm.then_inc(swa_scored, 1)
            pe.wait_ge(turnsB_ready, 2)
            pe.wait_ge(rg_ready, 2)
            for h in range(RET_HEADS):
                r = DH * (h % 2)
                pe.matmul(psum[:, RET_BANKS[h], 0:256], rkT[r:r + DH, h // 2, 0:P], rqT[r:r + DH, h // 2, :],
                          start=True, stop=True)
                pe.matmul(psum[:, RET_BANKS[h], 256:384], rkT[r:r + DH, h // 2, P:2 * P], rqT[r:r + DH, h // 2, P:2 * P],
                          start=True, stop=True).then_inc(ret_scored, 1)
            for h in range(MEM_HEADS):
                pe.wait_ge(memP_ready, 2 * h + 2)
                pe.wait_ge(swa_max_ready, h + 1)
                for b in range(2):
                    for t in range(TILES):
                        c = b * 256 + t * P
                        mm = turn(psum[:, HEAD_BANKS[h], c:c + P], memP[:, h, t, b * P:(b + 1) * P])
                mm.then_inc(memP_turned, 1)
            pe.wait_ge(retP_ready, 4)
            for h in range(RET_HEADS):
                mm = pe.matmul(psum[:, RET_O_BANKS[0], h * P:(h + 1) * P], retP[:, h, 0:P], rv[:, 0, h * P:(h + 1) * P],
                               start=True, stop=True)
            mm.then_inc(ret_read, 1)
            for h in range(RET_HEADS):
                pe.matmul(psum[:, RET_O_BANKS[1], h * P:(h + 1) * P], retP[:, h, P:2 * P], rv[:, 0, h * P:(h + 1) * P],
                          start=True, stop=False)
                mm = pe.matmul(psum[:, RET_O_BANKS[1], h * P:(h + 1) * P], retP[:, h, 2 * P:3 * P],
                               rv[:, 1, h * P:(h + 1) * P], start=False, stop=True)
            mm.then_inc(ret_read, 1)
            for g in range(2):
                pe.wait_ge(memPT_ready, 2 * g + 2)
                for b in range(2):
                    for r in range(2):
                        h = 2 * g + r
                        mm = pe.matmul(psum[r * DH:(r + 1) * DH, 3, g * 256:(g + 1) * 256], mv[:, b, h * DH:(h + 1) * DH],
                                       memPT[:, h, b], start=b == 0, stop=b == 1)
            mm.then_inc(mem_read, 1)
            for h in range(SWA_HEADS):
                pe.wait_ge(swaP_ready, 2 * h + 2)
                pe.wait_ge(memPT_ready, h + 1)
                for c in range(3):
                    mm = turn(psum[:, HEAD_BANKS[h], c * P:(c + 1) * P], swaP[:, h, c * P:(c + 1) * P])
                mm.then_inc(swaP_turned, 1)
            for g in range(2):
                pe.wait_ge(swaPT_ready, 2 * g + 2)
                for c, (t, b) in enumerate(((0, 0), (1, 0), (1, 1))):
                    for r in range(2):
                        h = 2 * g + r
                        first = g * 256 + t * P
                        mm = pe.matmul(psum[r * DH:(r + 1) * DH, 4, first:first + P], sv[:, b, g * DH:(g + 1) * DH],
                                       swaPT[:, h, c * P:(c + 1) * P], start=b == 0, stop=b == t)
            mm.then_inc(swa_read, 1)
            for t in range(TILES):
                pe.wait_ge(ret_gated, t + 1)
                for h in range(RET_HEADS):
                    c = t * N + h * P
                    mm = turn(psum[:, 5 + t, h * P:(h + 1) * P], tmpB[:, c:c + P])
                mm.then_inc(ret_turned, 1)

            def mix(c, steps):
                t, n = c // 2, c % 2
                for i in steps:
                    k = (4, 5, 6, 7, 0, 1, 2, 3)[i]
                    if i == 4 and n == 0:
                        pe.wait_ge(cat_ret, t + 1)
                    mm = pe.matmul(psum[:, MIXED_BANKS[c]], catT[:, k, t * P:(t + 1) * P],
                                   w_out_sb[k][:, n * N:(n + 1) * N], start=i == 0, stop=i == KD - 1)
                if i == KD - 1:
                    mm.then_inc(mixed, 1)

            def turn_h2(c):
                t, i = c // 2, c % 2
                pe.wait_ge(x2_ready, c + 1)
                for k in range(4):
                    first = (4 * i + k) * P
                    mm = turn(psum[:, H2_BANKS[c], k * P:(k + 1) * P], xy[:, t, first:first + P])
                    if c == 2 and k == 0:
                        mm.then_inc(slot_used, 2)
                mm.then_inc(h2_turned, 1)

            def route(t):
                for k in range(KD):
                    if k % 4 == 0:
                        pe.wait_ge(h2T_ready, 2 * t + k // 4 + 1)
                    mm = pe.matmul(psum[:, ROUTE_BANKS[t], 0:E], hT[:, k, t * P:(t + 1) * P], wr[:, k],
                                   start=k == 0, stop=k == KD - 1)
                mm.then_inc(routed, 1)

            pe.wait_ge(swaPT_ready, 4)
            pe.wait_ge(cat_mem, 1)
            pe.wait_ge(cat_swa, 1)
            pe.wait_ge(landed[0], 32)
            pe.wait_ge(landed[1], 32)
            pe.wait_ge(router_in, 16)
            mix(0, range(8))
            mix(1, range(8))
            turn_h2(0)
            mix(2, range(8))
            turn_h2(1)
            mix(3, range(4))
            route(0)
            mix(3, range(4, 8))
            turn_h2(2)
            turn_h2(3)
            route(1)

            def bias(p, banks):
                for n in banks:
                    mm = pe.matmul(psum[:, n], whose[0:E, :], bup_rows[0:E, n * N:(n + 1) * N], start=True, stop=False,
                                   skip_group_check=True)
                return mm

            def gather(q):
                pe.wait_ge(sel_ready, q + 1)
                for k in range(KD):
                    c = (k % 4) * P
                    for t in range(TILES):
                        mm = pe.matmul(psum[:, 6 + k // 4, c:c + P], xn[:, t, k * P:(k + 1) * P], sel[:, t],
                                       start=t == 0, stop=t == TILES - 1)
                    if k % 4 == 3:
                        mm.then_inc(gathered, 1)

            pe.wait_ge(bup_in, 16)
            pe.wait_ge(whose_ready, 1)
            bias(0, (0, 1))
            pe.wait_ge(chosen_ready, 2)
            pe.matmul(psum[:, 5, 64:96], constant("before"), chosen[:, 0], start=True, stop=True)
            pe.matmul(psum[:, 5, 96:128], constant("ones"), chosen[:, 0], start=True, stop=False)
            pe.matmul(psum[:, 5, 96:128], constant("before"), chosen[:, 1], start=False, stop=True)
            pe.matmul(psum[:, 5, 128:160], constant("ones"), chosen[:, 0], start=True, stop=False)
            pe.matmul(psum[:, 5, 128:160], constant("ones"), chosen[:, 1], start=False, stop=True).then_inc(placed, 1)
            bias(0, (2, 3)).then_inc(biased, 1)
            pe.wait_ge(xn2_ready, 2)
            gather(0)
            for t in range(TILES):
                pe.wait_ge(gates_ready, t + 1)
                mm = turn(psum[0:E, 4, t * P:(t + 1) * P], gates[:, t])
            mm.then_inc(gates_turned, 1)
            pe.wait_ge(bdown_in, 16)
            pe.wait_ge(count_ready, 1)

            def combine(q, c, banks=(6, 7, 6, 7)):
                n, t = c // 2, c % 2
                pe.matmul(psum[:, banks[c]], back[:, t], Y[:, n * N:(n + 1) * N], start=True, stop=True
                          ).then_inc(combined, 1)

            def pair(q, p, first=0):
                if not first:
                    pe.wait_ge(whose_ready, q + 1)
                    pe.wait_ge(up_read, q)
                    bias(p, range(4)).then_inc(biased, 1)
                for j in range(UP_CHUNKS):
                    if j % 4 == 0:
                        pe.wait_ge(xt_ready, 2 * q + (j // 4 + 1))
                    if j < first:
                        pe.wait_ge(extra_in[j], 16)
                        weights = extra[:, j].rearrange("p (e n) -> p e n", e=2)
                    else:
                        chunk_landed(pe, q, j)
                        weights = up_slot(j)
                    for n in range(4):
                        for e in range(2):
                            r = e * SLOTS
                            mm = pe.matmul(psum[r:r + SLOTS, n], XT[:, j, r:r + SLOTS], weights[:, e, n * N:(n + 1) * N],
                                           start=False, stop=j == KD - 1, skip_group_check=True)
                    if j >= first:
                        mm.then_inc(slot_used, 1)
                pe.wait_ge(y_ready, 2 * q + 2)
                gather(q + 1)
                pe.wait_ge(back_ready, q + 1)
                pe.wait_ge(xt_ready, 2 * q + 3)
                combine(q, 0)
                pe.wait_ge(xt_ready, 2 * q + 4)
                combine(q, 1)
                pe.wait_ge(y_added, 4 * q + 1)
                combine(q, 2)
                pe.wait_ge(y_added, 4 * q + 2)
                combine(q, 3)
                pe.wait_ge(gated_ready, q + 1)
                for t in range(TILES):
                    mm = turn(psum[:, 4, t * P:(t + 1) * P], gated[:, t])
                mm.then_inc(gated_turned, 1)
                pe.wait_ge(act_ready, q + 1)
                for i in range(2):
                    pe.wait_ge(y_added, 4 * q + (3 + i))
                    for k in range(4):
                        j = 4 * i + k
                        column = 256 * (j // 2) + j % 2
                        mm = turn(psum[:, 6 + i, k * P:(k + 1) * P], sig[:, column:column + 255:2])
                    mm.then_inc(act_turned, 1)
                pe.wait_ge(back_ready, q + 2)
                for i in range(DOWN_CHUNKS):
                    if i % 2 == 0:
                        pe.wait_ge(actT_ready, 2 * q + (i // 2 + 1))
                    chunk_landed(pe, q, UP_CHUNKS + i)
                    last = i == DOWN_CHUNKS - 1
                    for n in range(2):
                        for k in range(2):
                            for e in range(2):
                                r = e * SLOTS
                                mm = pe.matmul(psum[r:r + SLOTS, 4 + n], actT[:, 2 * i + k, r:r + SLOTS],
                                               down_slot(i)[:, e, k, n * N:(n + 1) * N],
                                               start=i == 0 and k == 0, stop=last and k == 1)
                        if last and n == 0:
                            mm.then_inc(down_half, 1)
                    mm.then_inc(slot_used, 1)

            def last_share(q_end):
                pe.wait_ge(back_ready, q_end + 1)
                for c in range(4):
                    pe.wait_ge(y_ready, 2 * q_end + (c // 2 + 1))
                    combine(q_end, c, LAST_BANKS)

            pair(0, 0, EXTRA)
            with pe.Fori(1, PAIRS) as q:
                pair(q, q)
            with pe.If(overflowing(pe)):
                further_blocks(pe, pair)
                last_share(BLOCKS * PAIRS)
            with pe.Else():
                last_share(PAIRS)


def kernel(**inputs):
    import concourse.bacc as bacc
    from concourse.bass_utils import run_bass_kernel_spmd

    nc = bacc.Bacc("TRN2", target_bir_lowering=False, num_devices=1)
    a = {name: np.asarray(value) for name, value in inputs.items()}
    gains = [a[name].reshape(-1, P) for name in ("g_mix", "g_mem", "g_ffn")]
    params = [a[name] for name in ("swa_q_gain", "swa_k_gain", "mem_q_gain", "mem_k_gain", "swa_sinks", "b_router")]
    arrays = {
        "x": a["x"], "mem": a["mem"], "positions": a["positions"].reshape(-1, P).T,
        "norm_gains": np.concatenate(gains, 0), "w_in": a["w_in"], "w_mem_kv": a["w_mem_kv"],
        "small_params": np.concatenate(params, 1), "w_out": a["w_out"], "w_router": a["w_router"],
        "w_up": a["w_up"], "b_up": a["b_up"], "w_down": a["w_down"], "b_down": a["b_down"],
        "constants": shape_constants(a["w_router"].shape[2]),
    }
    arrays = {name: np.ascontiguousarray(value) for name, value in arrays.items()}
    args = [nc.dram_tensor(f"in_{name}", a.shape, mybir.dt.from_np(a.dtype), kind="ExternalInput").ap()
            for name, a in arrays.items()]
    out = nc.dram_tensor("out_0", arrays["x"].shape, F32, kind="ExternalOutput").ap()
    layer_kernel(nc, *args, out)
    result = run_bass_kernel_spmd(nc, [{f"in_{name}": a for name, a in arrays.items()}], core_ids=[0])
    return result.results[0]["out_0"]
```

```python
from contextlib import ExitStack

import numpy as np

import concourse.bass as bass
from concourse import mybir

P = 128
CHUNK = 64
EPS = 1e-6
ROPE_THETA = 10000.0
RET_HEADS, RET_DV = 4, 128
SWA_HEADS, SWA_KV_HEADS = 4, 2
MEM_HEADS = 4
DH = 64
TOP_K = 4
LIMIT = 7.0
ALPHA = 1.702
SCALE = DH ** -0.5
MASKED = -1e30
FAR = 1e9

SLOTS = 64
RING = 8
SLOT_COLS = 4096

F32 = mybir.dt.float32
I32 = mybir.dt.int32
U32 = mybir.dt.uint32
ALU = mybir.AluOpType
ACT = mybir.ActivationFunctionType
AX_X = mybir.AxisListType.X

TWO_PI_HI = 6.28125
TWO_PI_MID = float(np.float32(np.round((2 * np.pi - TWO_PI_HI) * 2.0 ** 20) / 2.0 ** 20))
TWO_PI_LO = float(np.float32(2 * np.pi - TWO_PI_HI - TWO_PI_MID))
ROUND = 12582912.0
PI = float(np.float32(np.pi)) - 2.0 ** -22

CONST_WIDTHS = {"ident": P, "inv": DH // 2, "band": 6, "iota": SLOTS, "before": P, "half": 2, "row": 18, "dist": 3 * P}
CONST_FIRST = P + DH // 2
CONST_AT = {}
CONST_COLS = 0
for _name, _width in CONST_WIDTHS.items():
    CONST_AT[_name] = (CONST_COLS, CONST_COLS + _width)
    CONST_COLS += _width

DIST_AT = CONST_AT["dist"][0]

ROW_WIDTHS = {"swa_q": DH, "swa_k": DH, "mem_q": DH, "mem_k": DH, "sinks": SWA_HEADS, "b_router": 32}
ROW_AT = {}
ROW_COLS = 0
for _name, _width in ROW_WIDTHS.items():
    ROW_AT[_name] = (ROW_COLS, ROW_COLS + _width)
    ROW_COLS += _width


def shape_constants(n_experts):
    c = np.zeros((P, CONST_COLS), np.float32)

    def put(name, a):
        lo, hi = CONST_AT[name]
        c[:a.shape[0], lo:hi] = a

    p = np.arange(P)
    put("ident", np.eye(P))
    dist, band = [], []
    for key0, frame0, frames in ((0, 0, 2 * P), (P, P, P)):
        m, n = key0 + p[:, None], frame0 + np.arange(frames)[None, :]
        dist.append(np.where(m // CHUNK <= n // CHUNK, np.abs(n - m), FAR))
    put("dist", np.concatenate(dist, 1))
    for frame0, keys in ((0, P), (P, 2 * P)):
        n, m = frame0 + p[:, None], np.arange(0, keys, CHUNK)[None, :]
        ahead = n // CHUNK - m // CHUNK
        band.append(np.where((ahead >= 0) & (ahead <= 1), 0.0, MASKED))
    put("band", np.concatenate(band, 1))
    inv = np.float32(ROPE_THETA) ** (-np.arange(0, DH, 2, dtype=np.float32) / np.float32(DH))
    put("inv", np.broadcast_to(inv.astype(np.float32), (P, DH // 2)))
    put("iota", np.broadcast_to(np.arange(SLOTS), (P, SLOTS)))
    put("before", p[:, None] < p[None, :])
    put("half", np.broadcast_to(np.arange(2), (P, 2)))
    pair = np.arange(18) % (n_experts // 2)
    put("row", p[:, None] % n_experts - 2.0 * pair[None, :])
    return c


def layer_kernel(nc, x, mem, positions, norm_gains, w_in, w_mem_kv, small_params, w_out, w_router, w_up, b_up,
                 w_down, b_down, constants, out):
    _, S, D = x.shape
    E = w_router.shape[2]
    F = w_down.shape[2]
    TILES = S // P
    KD = D // P
    KF = F // P
    PAIRS = E // 2
    BLOCKS = S // SLOTS
    N = 512
    MQ_BANKS = RV_BANKS = RET_O_BANKS = (2, 7)
    MEMT_BANKS = MIXED_BANKS = (0, 1, 3, 4)
    HEAD_BANKS = (5, 6, 0, 1)
    RET_BANKS = (3, 2, 7, 4)
    H2_BANKS = (2, 7, 5, 6)
    ROUTE_BANKS = (2, 5)
    LAST_BANKS = (0, 1, 2, 3)
    assert (S, D, F, E) == (256, 1024, 1024, P // 4) and mem.shape[1] == S

    MIX_CHUNKS = 8
    UP_CHUNKS = KD
    DOWN_CHUNKS = KF // 2
    PAIR_CHUNKS = UP_CHUNKS + DOWN_CHUNKS
    assert 2 * PAIR_CHUNKS % RING == 0 and PAIRS % 2 == 0
    LAPS = 2 * PAIR_CHUNKS // RING
    MIX_SLOTS = RING - 2
    OUTSIDE_UP, OUTSIDE_DOWN = 0, UP_CHUNKS + 2
    BASE = MIX_CHUNKS - 2
    MIX_LOADS = (2, 2, 1, 1, 1, 1, 0, 0)

    with ExitStack() as ctx:
        def sb(name, shape, dt=F32):
            return ctx.enter_context(nc.sbuf_tensor(name, shape, dt))

        def sem(name):
            return ctx.enter_context(nc.semaphore(name))

        psum = ctx.enter_context(nc.psum_tensor("psum", [P, 8, N], F32))

        ring = sb("ring", [P, MIX_SLOTS, SLOT_COLS])
        xy = sb("xy", [P, TILES, D])
        const = sb("const", [P, DIST_AT])
        ones = sb("ones", [P, P])
        norm_gain = sb("norm_gain", [P, 3 * KD])
        param = sb("param", [P, ROW_COLS])
        wr = sb("wr", [P, KD, E])
        small = sb("small", [P, 224])
        pos_i = sb("pos_i", [P, TILES], I32)
        top_i = sb("top_i", [P, TILES, 8], U32)
        count_i = sb("count_i", [1, 1], I32)

        KIB = 256
        WORK_KIB = 88
        work = sb("work", [P, WORK_KIB * KIB])
        at = [0]

        def carve(cols):
            at[0] += cols
            assert at[0] <= WORK_KIB * KIB
            return work[:, at[0] - cols:at[0]]

        xn = carve(8 * KIB).rearrange("p (t d) -> p t d", t=TILES)
        late_start = at[0]
        hT = carve(8 * KIB).rearrange("p (k n) -> p k n", k=KD)
        memT = carve(8 * KIB).rearrange("p (k n) -> p k n", k=KD)
        catT = carve(8 * KIB).rearrange("p (k n) -> p k n", k=KD)
        cat_end = at[0]
        rqk = carve(4 * KIB).rearrange("p (t n) -> p t n", t=TILES)
        rv = carve(4 * KIB).rearrange("p (t n) -> p t n", t=TILES)
        shared_start = at[0]
        rg = carve(4 * KIB).rearrange("p (t n) -> p t n", t=TILES)
        sqk = carve(3 * KIB).rearrange("p (t n) -> p t n", t=TILES)
        sv = carve(1 * KIB).rearrange("p (t n) -> p t n", t=TILES)
        mq = carve(2 * KIB).rearrange("p (t n) -> p t n", t=TILES)
        mk = carve(2 * KIB).rearrange("p (t n) -> p t n", t=TILES)
        mv = carve(2 * KIB).rearrange("p (t n) -> p t n", t=TILES)
        sqT = carve(2 * KIB).rearrange("p (g n) -> p g n", g=2)
        mqT = carve(2 * KIB).rearrange("p (g n) -> p g n", g=2)
        mkT = carve(2 * KIB).rearrange("p (g n) -> p g n", g=2)
        decay = carve(6 * KIB).rearrange("p (h n) -> p h n", h=RET_HEADS)
        swaP = carve(6 * KIB).rearrange("p (h n) -> p h n", h=SWA_HEADS)
        memP = carve(8 * KIB).rearrange("p (h t n) -> p h t n", h=MEM_HEADS, t=TILES)
        tmpA = carve(4 * KIB)
        tmpB = carve(4 * KIB)
        start_cols = rg.rearrange("p t n -> p (t n)")
        norm_rows = start_cols[0:3 * KD, 0:P]
        param_row = start_cols[0:1, P:P + ROW_COLS]
        turns = start_cols[:, 512:512 + 2 * TILES * (DH // 2)].rearrange("p (a t n) -> p a t n", a=2, t=TILES)
        retP = xn.rearrange("p t d -> p (t d)")[:, 0:1536].rearrange("p (h n) -> p h n", h=RET_HEADS)
        rope_r = xn.rearrange("p t d -> p (t d)")[:, 0:1024].rearrange("p (t n) -> p t n", t=TILES)
        rkT = xn.rearrange("p t d -> p (t d)")[:, 1536:2048].rearrange("p (g n) -> p g n", g=2)
        rqT = mq.rearrange("p t n -> p (t n)").rearrange("p (g n) -> p g n", g=2)
        skT = tmpB[:, 768:1024]
        rope_s = swaP.rearrange("p h n -> p (h n)")[:, 0:768].rearrange("p (t n) -> p t n", t=TILES)
        swaPT = hT.rearrange("p k n -> p (k n)")[:, 0:1536].rearrange("p (h n) -> p h n", h=SWA_HEADS)
        memPT = memT.rearrange("p (h b) n -> p h b n", b=2)

        at[0] = late_start
        glu = carve(4 * KIB)
        lin = carve(4 * KIB)
        XT = carve(4 * KIB).rearrange("p (k s) -> p k s", k=KD)
        act_start = at[0]
        actT = carve(4 * KIB).rearrange("p (k s) -> p k s", k=KF)
        sig = carve(4 * KIB)
        sel = carve(1 * KIB).rearrange("p (t s) -> p t s", t=TILES)
        gated = carve(1 * KIB).rearrange("p (t s) -> p t s", t=TILES)
        place = carve(TILES * (BLOCKS * E + 2)).rearrange("p (t c) -> p t c", t=TILES)
        assert at[0] <= cat_end
        at[0] = cat_end
        Y = carve(4 * KIB)
        back = carve(1 * KIB).rearrange("p (t n) -> p t n", t=TILES)
        whose = carve(KIB // 2)
        bup_rows = carve(2 * KIB)
        gates = carve(TILES * E).rearrange("p (t e) -> p t e", t=TILES)
        assert at[0] <= shared_start
        at[0] = shared_start
        slots = [ring[:, s, :] for s in range(MIX_SLOTS)] + [carve(SLOT_COLS), carve(SLOT_COLS)]
        outside_down = carve(SLOT_COLS)
        outside_up = [work[:, start:start + 2 * F] for start in (late_start, act_start)]
        router = sb("router", [P, TILES * E * (2 + 2 * TOP_K)])
        logits, chosen = (router[:, i * TILES * E:(i + 1) * TILES * E].rearrange("p (t e) -> p t e", t=TILES)
                          for i in range(2))
        hits, hitg = (router[:, i * TILES * E:(i + TOP_K) * TILES * E].rearrange("p (t j e) -> p t j e", t=TILES, j=TOP_K)
                      for i in (2, 2 + TOP_K))

        used = [0]

        def cols(n):
            used[0] += n
            assert used[0] <= small.shape[1]
            return small[:, used[0] - n:used[0]]

        ss_mem, rs_mem = cols(TILES), cols(TILES)
        ss_x, rs_x = cols(TILES), cols(TILES)
        ss_mk, rs_mk = cols(8), cols(8)
        ss_mq, rs_mq = cols(8), cols(8)
        ss_s, rs_s = cols(12), cols(12)
        ss_ret, rs_ret = cols(8), cols(8)
        ss_ffn, rs_ffn = cols(TILES), cols(TILES)
        mem_max, mem_neg, mem_sum, mem_inv = cols(8), cols(8), cols(8), cols(8)
        swa_max, swa_neg, swa_sum, swa_sink, swa_inv = cols(8), cols(8), cols(8), cols(8), cols(8)
        minus_half = cols(16)
        posf = cols(TILES)
        top_v = cols(16).rearrange("p (t j) -> p t j", t=TILES)
        top_x = cols(8).rearrange("p (t j) -> p t j", t=TILES)
        top_neg, top_sum, top_inv = cols(TILES), cols(TILES), cols(TILES)
        top_g = cols(8).rearrange("p (t j) -> p t j", t=TILES)
        count_f = cols(1)
        dist = sb("dist", [P, 3 * P])
        angle = sb("angle", [P, 4, TILES, DH // 2])
        cos2 = sb("cos2", [P, TILES, DH])
        sin2 = sb("sin2", [P, TILES, DH])
        cosr = sb("cosr", [P, TILES, DH])
        sinr = sb("sinr", [P, TILES, DH])
        swa_gain = sb("swa_gain", [P, 6, DH])

        def constant(name):
            lo, hi = CONST_AT[name]
            return const[:, lo:hi]

        def parameter(name):
            lo, hi = ROW_AT[name]
            return param[:, lo:hi]

        ident = constant("ident")

        ones_ready = sem("ones_ready")
        const_in, tables_in, x_in, mem_in = (
            sem("const_in"), sem("tables_in"), [sem("x_in0"), sem("x_in1")], [sem("mem_in0"), sem("mem_in1")])
        pos_in, params_in, router_in = sem("pos_in"), sem("params_in"), sem("router_in")
        bup_in, bdown_in, out_written = sem("bup_in"), sem("bdown_in"), sem("out_written")
        outside_up_in, outside_down_in = sem("outside_up_in"), sem("outside_down_in")
        last_half_in = sem("last_half_in")
        landed = [sem(f"landed{i}") for i in range(RING)]
        slot_used = sem("slot_used")
        dve_step, pool_step = sem("dve_step"), sem("pool_step")
        squares = {n: sem(f"squares_{n}") for n in ("mem", "x", "mk", "mq", "swa", "ret", "ffn")}
        sums = {n: sem(f"sums_{n}") for n in ("mk", "mq", "swa", "ret")}
        rstd = {n: sem(f"rstd_{n}") for n in ("mem", "x", "mk", "mq", "swa", "ret", "ffn")}
        params_spread, params_ready = sem("params_spread"), sem("params_ready")
        angles_ready, trig_ready, decay_ready = sem("angles_ready"), sem("trig_ready"), sem("decay_ready")
        rotation_ready = sem("rotation_ready")
        mem_turned, memT_ready = sem("mem_turned"), sem("memT_ready")
        x_turned, hT_ready = sem("x_turned"), sem("hT_ready")
        mkv_done, mv_ready, mk_ready = sem("mkv_done"), sem("mv_ready"), sem("mk_ready")
        mq_done, mq_ready = sem("mq_done"), sem("mq_ready")
        swa_done, swa_qk_ready, sv_ready = sem("swa_done"), sem("swa_qk_ready"), sem("sv_ready")
        rqk_done, rqk_ready = sem("rqk_done"), sem("rqk_ready")
        rv_done, rv_ready = sem("rv_done"), sem("rv_ready")
        rg_done, rg_sig, rg_ready = sem("rg_done"), sem("rg_sig"), sem("rg_ready")
        turnedA, turnsA_ready = sem("turnedA"), sem("turnsA_ready")
        turnedB, turnsB_ready = sem("turnedB"), sem("turnsB_ready")
        mem_scored, mem_max_ready, mem_exp, memP_ready = (
            sem("mem_scored"), sem("mem_max_ready"), sem("mem_exp"), sem("memP_ready"))
        swa_scored, swa_max_ready, swa_exp, swaP_ready = (
            sem("swa_scored"), sem("swa_max_ready"), sem("swa_exp"), sem("swaP_ready"))
        ret_scored, retP_ready = sem("ret_scored"), sem("retP_ready")
        memP_turned, memPT_ready = sem("memP_turned"), sem("memPT_ready")
        swaP_turned, swaPT_ready = sem("swaP_turned"), sem("swaPT_ready")
        mem_read, swa_read, ret_read = sem("mem_read"), sem("swa_read"), sem("ret_read")
        cat_mem, cat_swa, ret_gated, ret_turned, cat_ret = (
            sem("cat_mem"), sem("cat_swa"), sem("ret_gated"), sem("ret_turned"), sem("cat_ret"))
        mixed, x2_ready, xn2_ready = sem("mixed"), sem("x2_ready"), sem("xn2_ready")
        h2_turned, h2T_ready, routed, top_ready, top_exp = (
            sem("h2_turned"), sem("h2T_ready"), sem("routed"), sem("top_ready"), sem("top_exp"))
        chosen_ready, gates_ready, placed, count_ready = (
            sem("chosen_ready"), sem("gates_ready"), sem("placed"), sem("count_ready"))
        gates_turned, counted = sem("gates_turned"), sem("counted")
        sel_ready, gated_ready, whose_ready = sem("sel_ready"), sem("gated_ready"), sem("whose_ready")
        biased, gathered, xt_ready = sem("biased"), sem("gathered"), sem("xt_ready")
        glu_ready, lin1_ready = sem("glu_ready"), sem("lin1_ready")
        sig_ready, act_ready = sem("sig_ready"), sem("act_ready")
        up_done = sem("up_done")
        up_read = sem("up_read")
        gated_turned, back_ready = sem("gated_turned"), sem("back_ready")
        act_turned, actT_ready = sem("act_turned"), sem("actT_ready")
        down_half, y_ready, combined, y_added = sem("down_half"), sem("y_ready"), sem("combined"), sem("y_added")

        w_mem_sb = ring[:, 0, :].rearrange("p (k n) -> p k n", k=KD)
        w_mq_sb = ring[:, 2, 0:2048].rearrange("p (k n) -> p k n", k=KD)
        mem_sb = ring[:, 2, 2048:4096].rearrange("p (t d) -> p t d", t=TILES)
        GROUP_SLOTS = (3, 4, 5, 1)
        w_group_sb = [ring[:, s, :].rearrange("p (k n) -> p k n", k=KD) for s in GROUP_SLOTS]
        w_out_sb = [ring[:, n, :].rearrange("p (k n) -> p k n", k=KD) for n in range(2)]

        def in_ring(u, j, first=False):
            g = BASE + u * PAIR_CHUNKS + j + (first and j < OUTSIDE_DOWN)
            return (g + 2) % RING, g // RING - 1

        def chunk_landed(eng, h, u, j, first=False):
            s, lap = in_ring(u, j, first)
            eng.wait_ge(landed[s], h * (16 * LAPS) + 16 * (MIX_LOADS[s] + lap + 1))
            return slots[s]

        def chunks_used(q, j):
            return q * PAIR_CHUNKS + (BASE + j)

        block = ctx.enter_context(nc.Block())

        def overflowing(eng):
            eng.wait_ge(count_ready, 1)
            return eng.value_load(count_i[0:1, 0:1], min_val=0, max_val=S) > SLOTS

        def further_blocks(eng, pair):
            with eng.Fori(1, BLOCKS) as b:
                with eng.Fori(0, PAIRS) as p:
                    pair(b * PAIRS + p, p)

        def further_twos(eng, pair):
            with eng.Fori(1, BLOCKS) as b:
                with eng.Fori(0, PAIRS // 2) as h:
                    for u in range(2):
                        pair(b * (PAIRS // 2) + h, h, u)

        @block.sync
        def _(sp):
            sp.dma_start(const[:, 0:CONST_FIRST], constants[:, 0:CONST_FIRST]).then_inc(const_in, 16)
            for t in range(TILES):
                sp.dma_start(xy[:, t], x[0, t * P:(t + 1) * P, :]).then_inc(x_in[t], 16)
            sp.dma_start(w_mq_sb, w_in[0, :, 2048:2304].rearrange("(k p) n -> p k n", p=P)).then_inc(landed[2], 16)
            for t in range(TILES):
                sp.dma_start(mem_sb[:, t], mem[0, t * P:(t + 1) * P, :]).then_inc(mem_in[t], 16)
            sp.dma_start(w_mem_sb, w_mem_kv[0].rearrange("(k p) n -> p k n", p=P)).then_inc(landed[0], 16)
            sp.dma_start(const[:, CONST_FIRST:], constants[:, CONST_FIRST:DIST_AT]).then_inc(tables_in, 16)
            sp.dma_start(dist[:], constants[:, DIST_AT:]).then_inc(tables_in, 16)
            for n in (3, 0, 1, 2):
                sp.dma_start(w_group_sb[n], w_in[0, :, n * N:(n + 1) * N].rearrange("(k p) n -> p k n", p=P)
                             ).then_inc(landed[GROUP_SLOTS[n]], 16)
            sp.dma_start(wr[:], w_router[0].rearrange("(k p) e -> p k e", p=P)).then_inc(router_in, 16)
            for s in range(2):
                sp.wait_ge(slot_used, s + 2)
                sp.dma_start(w_out_sb[s], w_out[0, :, s * N:(s + 1) * N].rearrange("(k p) n -> p k n", p=P)
                             ).then_inc(landed[s], 16)

            def load(s, p, j):
                if j < UP_CHUNKS:
                    src = w_up[0, bass.ds(2 * p, 2), j * P:(j + 1) * P, :].rearrange("e r n -> r e n")
                    sp.dma_start(slots[s].rearrange("r (e n) -> r e n", e=2), src).then_inc(landed[s], 16)
                    return
                i = j - UP_CHUNKS
                src = w_down[0, bass.ds(2 * p, 2), 2 * i * P:(2 * i + 2) * P, :]
                if i < DOWN_CHUNKS - 1:
                    sp.dma_start(slots[s].rearrange("r (e n) -> r e n", e=2), src.rearrange("e (r k) n -> r e (k n)", k=2)
                                 ).then_inc(landed[s], 16)
                    return
                src = src.rearrange("e (r k) n -> r e k n", k=2)
                dst = slots[s].rearrange("r (e k n) -> r e k n", e=2, k=2)
                for k, done in ((0, last_half_in), (1, landed[s])):
                    sp.dma_start(dst[:, :, k], src[:, :, k]).then_inc(done, 16)

            def pair(h, expert_h, u):
                for j in range(PAIR_CHUNKS):
                    sp.wait_ge(slot_used, h * (2 * PAIR_CHUNKS) + (BASE + u * PAIR_CHUNKS + j - RING + 1))
                    load(in_ring(u, j)[0], expert_h * 2 + u, j)

            def first_pair():
                ring_chunks = [j for j in range(PAIR_CHUNKS) if j not in (OUTSIDE_UP, OUTSIDE_DOWN)]
                for c, j in enumerate(ring_chunks):
                    s, _ = in_ring(0, j, True)
                    if c < 4:
                        sp.wait_ge(slot_used, c + 3)
                    elif c < 6:
                        sp.wait_ge(ret_turned, TILES)
                    else:
                        sp.wait_ge(slot_used, c + 1)
                    load(s, 0, j)
                    if c == 5:
                        i = OUTSIDE_DOWN - UP_CHUNKS
                        sp.dma_start(outside_down.rearrange("r (e n) -> r e n", e=2),
                                     w_down[0, 0:2, 2 * i * P:(2 * i + 2) * P, :].rearrange("e (r k) n -> r e (k n)", k=2)
                                     ).then_inc(outside_down_in, 16)
                    elif c == 7:
                        sp.wait_ge(slot_used, MIX_CHUNKS)
                        sp.wait_ge(routed, TILES)
                        for e in range(2):
                            sp.dma_start(outside_up[e], w_up[0, e, OUTSIDE_UP * P:(OUTSIDE_UP + 1) * P, :]
                                         ).then_inc(outside_up_in, 16)

            def store_result(q_end):
                for n in range(2):
                    for t in range(TILES):
                        sp.wait_ge(y_added, 4 * q_end + 2 * n + t + 1)
                        sp.dma_start(out[0, t * P:(t + 1) * P, n * N:(n + 1) * N], xy[:, t, n * N:(n + 1) * N]
                                     ).then_inc(out_written, 16)

            first_pair()
            pair(0, 0, 1)
            with sp.Fori(1, PAIRS // 2) as h:
                for u in range(2):
                    pair(h, h, u)
            with sp.If(overflowing(sp)):
                further_twos(sp, pair)
                store_result(BLOCKS * PAIRS)
            with sp.Else():
                store_result(PAIRS)
            sp.wait_ge(out_written, 16 * 4)

        @block.gpsimd
        def _(pool):
            count = [0]

            def step(ins):
                count[0] += 1
                ins.then_inc(pool_step, 1)
                pool.wait_ge(pool_step, count[0])

            nc.gpsimd.memset(ones[:], 1.0).then_inc(ones_ready, 1)
            step(nc.gpsimd.memset(minus_half, -0.5))

            def root(name, summed, done, ss, rs, width):
                n = ss.shape[1]
                pool.wait_ge(summed, done)
                step(nc.gpsimd.tensor_scalar(ss, ss, 1.0 / width, EPS, ALU.mult, ALU.add))
                nc.gpsimd.tensor_tensor(rs, ss, minus_half[:, 0:n], ALU.pow).then_inc(rstd[name], 1)

            root("x", squares["x"], TILES, ss_x, rs_x, D)
            root("mem", squares["mem"], TILES, ss_mem, rs_mem, D)
            root("mq", sums["mq"], 1, ss_mq, rs_mq, DH)
            root("mk", sums["mk"], 1, ss_mk, rs_mk, DH)
            root("swa", sums["swa"], 1, ss_s, rs_s, DH)
            for t in range(TILES):
                root("ret", sums["ret"], t + 1, ss_ret[:, 4 * t:4 * t + 4], rs_ret[:, 4 * t:4 * t + 4], RET_DV)
            for t in range(TILES):
                root("ffn", squares["ffn"], t + 1, ss_ffn[:, t:t + 1], rs_ffn[:, t:t + 1], D)

        @block.scalar
        def _(act):
            act.dma_start(norm_rows, norm_gains).then_inc(params_in, 16)
            act.dma_start(param_row, small_params).then_inc(params_in, 16)
            act.dma_start(pos_i[:], positions).then_inc(pos_in, 16)

            def row_squares(name, src, ss, arrived, other):
                for t in range(TILES):
                    act.wait_ge(arrived[t], 16)
                    if t > 0:
                        act.wait_ge(squares[name], t)
                    nc.scalar.activation(other, src[:, t], ACT.Square, accum_out=ss[:, t:t + 1]
                                         ).then_inc(squares[name], 1)

            row_squares("x", xy, ss_x, x_in, tmpB)
            row_squares("mem", mem_sb, ss_mem, mem_in, tmpA)
            act.wait_ge(params_ready, 2)
            for k in range(KD):
                if k % 2 == 0:
                    act.wait_ge(mem_turned, k // 2 + 1)
                nc.scalar.activation(memT[:, k], psum[:, MEMT_BANKS[k // 2], (k % 2) * 256:(k % 2 + 1) * 256], ACT.Copy,
                                     scale=norm_gain[:, KD + k:KD + k + 1]).then_inc(memT_ready, 1)
            act.wait_ge(rstd["x"], 1)
            act.wait_ge(squares["mem"], TILES)
            for t in range(TILES):
                act.wait_ge(mq_done, t + 1)
                nc.scalar.activation(tmpA[:, 512 + t * 256:768 + t * 256], psum[:, MQ_BANKS[t], 0:256], ACT.Square,
                                     scale=rs_x[:, t:t + 1]).then_inc(squares["mq"], 1)
            act.wait_ge(angles_ready, 1)
            nc.scalar.activation(angle[:, 2:4], angle[:, 0:2], ACT.Sin).then_inc(trig_ready, 1)
            act.wait_ge(tables_in, 32)
            for h in range(RET_HEADS):
                nc.scalar.activation(decay[:, h], dist[:], ACT.Exp,
                                     scale=float(np.log1p(-(2.0 ** (-5.0 - h))))).then_inc(decay_ready, 1)
            act.wait_ge(rstd["mem"], 1)
            for t in range(TILES):
                act.wait_ge(mkv_done, t + 1)
                nc.scalar.activation(tmpA[:, t * 256:(t + 1) * 256], psum[:, 5 + t, 0:256], ACT.Square,
                                     scale=rs_mem[:, t:t + 1]).then_inc(squares["mk"], 1)
                nc.scalar.activation(mv[:, t], psum[:, 5 + t, 256:512], ACT.Copy, scale=rs_mem[:, t:t + 1]
                                     ).then_inc(mv_ready, 1)
            for t in range(TILES):
                act.wait_ge(swa_done, t + 1)
                nc.scalar.activation(tmpB[:, t * 384:(t + 1) * 384], psum[:, t, 0:384], ACT.Square,
                                     scale=rs_x[:, t:t + 1]).then_inc(squares["swa"], 1)
                nc.scalar.activation(sv[:, t], psum[:, t, 384:512], ACT.Copy, scale=rs_x[:, t:t + 1]
                                     ).then_inc(sv_ready, 1)
            for t in range(TILES):
                act.wait_ge(rv_done, t + 1)
                nc.scalar.activation(rv[:, t], psum[:, RV_BANKS[t]], ACT.Copy, scale=rs_x[:, t:t + 1]
                                     ).then_inc(rv_ready, 1)
            for n, (dst, b) in enumerate(((mkT, 5), (mqT, 6), (sqT, 0))):
                act.wait_ge(turnedA, n + 1)
                nc.scalar.activation(dst, psum[:, b].rearrange("p (g n) -> p g n", g=2), ACT.Copy
                                     ).then_inc(turnsA_ready, 1)
            act.wait_ge(turnedA, 4)
            nc.scalar.activation(skT, psum[:, 1, 0:256], ACT.Copy).then_inc(turnsA_ready, 1)

            def gate_sigmoid(t):
                act.wait_ge(rg_done, t + 1)
                nc.scalar.activation(rg[:, t], psum[:, 3 + t], ACT.Sigmoid, scale=rs_x[:, t:t + 1]).then_inc(rg_sig, 1)

            act.wait_ge(rotation_ready, 1)
            gate_sigmoid(0)
            for h in range(MEM_HEADS):
                act.wait_ge(mem_max_ready, h + 1)
                for t in range(TILES):
                    c = 2 * h + t
                    nc.scalar.activation(memP[:, h, t], psum[:, HEAD_BANKS[h], t * 256:(t + 1) * 256], ACT.Exp, scale=SCALE,
                                         bias=mem_neg[:, c:c + 1], accum_out=mem_sum[:, c:c + 1]).then_inc(mem_exp, 1)
            for n, (dst, b) in enumerate(((rqT, 2), (rkT, 7))):
                act.wait_ge(turnedB, n + 1)
                nc.scalar.activation(dst, psum[:, b].rearrange("p (g n) -> p g n", g=2), ACT.Copy
                                     ).then_inc(turnsB_ready, 1)
            for h in range(SWA_HEADS):
                act.wait_ge(swa_max_ready, h + 1)
                for t, (lo, hi) in enumerate(((0, P), (P, 3 * P))):
                    c = 2 * h + t
                    nc.scalar.activation(swaP[:, h, lo:hi], swaP[:, h, lo:hi], ACT.Exp, bias=swa_neg[:, c:c + 1],
                                         accum_out=swa_sum[:, c:c + 1]).then_inc(swa_exp, 1)
                    nc.scalar.activation(swa_sink[:, c:c + 1], parameter("sinks")[:, h:h + 1], ACT.Exp,
                                         bias=swa_neg[:, c:c + 1]).then_inc(swa_exp, 1)
                if h == 2:
                    gate_sigmoid(1)
            for h in range(MEM_HEADS):
                act.wait_ge(memP_turned, h + 1)
                nc.scalar.activation(memPT[:, h], psum[:, HEAD_BANKS[h]].rearrange("p (b n) -> p b n", b=2), ACT.Copy
                                     ).then_inc(memPT_ready, 1)
            for t in range(TILES):
                act.wait_ge(ret_read, t + 1)
                nc.scalar.activation(tmpA[:, t * N:(t + 1) * N], psum[:, RET_O_BANKS[t]], ACT.Square
                                     ).then_inc(squares["ret"], 1)
            for h in range(SWA_HEADS):
                act.wait_ge(swaP_turned, h + 1)
                nc.scalar.activation(swaPT[:, h], psum[:, HEAD_BANKS[h], 0:3 * P], ACT.Copy).then_inc(swaPT_ready, 1)
            act.wait_ge(mem_read, 1)
            nc.scalar.activation(catT[:, 6:8], psum[:, 3].rearrange("p (g n) -> p g n", g=2), ACT.Copy
                                 ).then_inc(cat_mem, 1)
            for n in range(4):
                act.dma_start(bup_rows[n * E:(n + 1) * E, :], b_up[0, :, n * N:(n + 1) * N]).then_inc(bup_in, 16)
            act.wait_ge(swa_read, 1)
            nc.scalar.activation(catT[:, 4:6], psum[:, 4].rearrange("p (g n) -> p g n", g=2), ACT.Copy
                                 ).then_inc(cat_swa, 1)
            for t in range(TILES):
                act.wait_ge(ret_turned, t + 1)
                nc.scalar.activation(catT[:, 0:4, t * P:(t + 1) * P], psum[:, 5 + t].rearrange("p (h n) -> p h n", h=4),
                                     ACT.Copy).then_inc(cat_ret, 1)
            act.wait_ge(y_ready, 2)
            act.dma_start(Y[0:E, :], b_down[0]).then_inc(bdown_in, 16)
            for t in range(TILES):
                act.wait_ge(x2_ready, t + 3)
                nc.scalar.activation(XT.rearrange("p k s -> p (k s)"), xy[:, t], ACT.Square,
                                     accum_out=ss_ffn[:, t:t + 1]).then_inc(squares["ffn"], 1)
                act.wait_ge(rstd["ffn"], t + 1)
                nc.scalar.activation(xn[:, t], xy[:, t], ACT.Copy, scale=rs_ffn[:, t:t + 1]).then_inc(xn2_ready, 1)
                act.wait_ge(top_ready, t + 1)
                nc.scalar.activation(top_g[:, t], top_v[:, t, 0:TOP_K], ACT.Exp, bias=top_neg[:, t:t + 1],
                                     accum_out=top_sum[:, t:t + 1]).then_inc(top_exp, 1)
            act.wait_ge(gates_turned, 1)
            nc.scalar.activation(back[0:E], psum[0:E, 4, 0:256].rearrange("p (t n) -> p t n", t=TILES), ACT.Copy
                                 ).then_inc(back_ready, 1)

            def pair(q, p):
                for i in range(2):
                    act.wait_ge(glu_ready, 2 * q + (i + 1))
                    nc.scalar.activation(sig[:, i * N:(i + 1) * N], glu[:, i * N:(i + 1) * N], ACT.Sigmoid, scale=ALPHA
                                         ).then_inc(sig_ready, 1)
                act.wait_ge(gated_turned, q + 1)
                nc.scalar.activation(back, psum[:, 4, 0:256].rearrange("p (t n) -> p t n", t=TILES), ACT.Copy
                                     ).then_inc(back_ready, 1)
                for i in range(2):
                    act.wait_ge(act_turned, 2 * q + (i + 1))
                    nc.scalar.activation(actT[:, 4 * i:4 * i + 4], psum[:, i].rearrange("p (k s) -> p k s", k=4),
                                         ACT.Copy).then_inc(actT_ready, 1)
                for n in range(2):
                    if n == 0:
                        act.wait_ge(down_half, q + 1)
                    else:
                        act.wait_ge(slot_used, chunks_used(q, PAIR_CHUNKS))
                    nc.scalar.activation(Y[:, n * N:(n + 1) * N], psum[:, 4 + n], ACT.Copy).then_inc(y_ready, 1)

            with act.Fori(0, PAIRS) as q:
                pair(q, q)
            with act.If(overflowing(act)):
                further_blocks(act, pair)

        @block.vector
        def _(dve):
            V = nc.vector
            count = [0]

            def step(ins):
                count[0] += 1
                ins.then_inc(dve_step, 1)
                dve.wait_ge(dve_step, count[0])

            dve.wait_ge(params_spread, 2)
            V.tensor_copy(norm_gain[:], psum[:, 7, 0:3 * KD]).then_inc(params_ready, 1)
            V.tensor_copy(param[:], psum[:, 7, 64:64 + ROW_COLS]).then_inc(params_ready, 1)

            def turned_gain(dst, src, gain0, k0, kn, n):
                g = norm_gain[:, gain0 + k0:gain0 + k0 + kn].unsqueeze(2).to_broadcast([P, kn, n])
                return V.tensor_tensor(dst, src.rearrange("p (k n) -> p k n", k=kn), g, ALU.mult)

            dve.wait_ge(params_ready, 2)
            for i in range(4):
                dve.wait_ge(x_turned, i + 1)
                turned_gain(hT[:, 2 * i:2 * i + 2], psum[:, 3 + i], 0, 2 * i, 2, 256).then_inc(hT_ready, 1)

            dve.wait_ge(pos_in, 16)
            step(V.tensor_copy(posf, pos_i[:]))
            for t in range(TILES):
                step(V.tensor_scalar(angle[:, 0, t], constant("inv"), posf[:, t:t + 1], None, ALU.mult))
            step(V.tensor_scalar(turns[:, 0], angle[:, 0], float(1 / (2 * np.pi)), ROUND, ALU.mult, ALU.add))
            step(V.tensor_scalar(turns[:, 1], angle[:, 0], float(1 / (2 * np.pi)), 0.25, ALU.mult, ALU.add))
            step(V.tensor_scalar(turns[:, 1], turns[:, 1], ROUND, None, ALU.add))
            step(V.tensor_scalar(turns[:], turns[:], ROUND, None, ALU.subtract))
            step(V.tensor_copy(angle[:, 1], angle[:, 0]))
            for part in (TWO_PI_HI, TWO_PI_MID, TWO_PI_LO):
                step(V.scalar_tensor_tensor(out=angle[:, 0:2], in0=turns[:], scalar=-part, in1=angle[:, 0:2],
                                            op0=ALU.mult, op1=ALU.add))
            step(V.tensor_scalar(angle[:, 1], angle[:, 1], float(np.pi / 2), None, ALU.add))
            V.tensor_scalar(angle[:, 0:2], angle[:, 0:2], PI, -PI, ALU.min, ALU.max).then_inc(angles_ready, 1)

            dve.wait_ge(trig_ready, 1)
            V.tensor_copy(cos2[:, :, 0:32], angle[:, 3])
            V.tensor_copy(cos2[:, :, 32:64], angle[:, 3])
            V.tensor_scalar(sin2[:, :, 0:32], angle[:, 2], -1.0, None, ALU.mult)
            V.tensor_copy(sin2[:, :, 32:64], angle[:, 2])
            V.tensor_copy(swa_gain[:, 0:4], parameter("swa_q").unsqueeze(1).to_broadcast([P, 4, DH]))
            step(V.tensor_copy(swa_gain[:, 4:6], parameter("swa_k").unsqueeze(1).to_broadcast([P, 2, DH])))
            dve.wait_ge(rstd["x"], 1)
            for t in range(TILES):
                V.tensor_scalar(cosr[:, t], cos2[:, t], rs_x[:, t:t + 1], None, ALU.mult)
                last = V.tensor_scalar(sinr[:, t], sin2[:, t], rs_x[:, t:t + 1], None, ALU.mult)
            last.then_inc(rotation_ready, 1)

            def heads(a, n):
                return a.rearrange("p (h d) -> p h d", h=n)

            def per_head(a, n, width=DH):
                return a.unsqueeze(2).to_broadcast([P, n, width])

            def over_heads(a, n):
                return a.unsqueeze(1).to_broadcast([P, n, a.shape[1]])

            def head_sums(name, src, ss, done, n):
                dve.wait_ge(squares[name], done)
                V.tensor_reduce(ss, heads(src, n), AX_X, ALU.add).then_inc(sums[name], 1)

            def normed(dst, src, rs, row_rs, n):
                step(V.tensor_scalar(rs, rs, row_rs, None, ALU.mult))
                return V.tensor_tensor(heads(dst, n), heads(src, n), per_head(rs, n), ALU.mult)

            head_sums("mq", tmpA[:, 512:1024], ss_mq, 2, 8)
            dve.wait_ge(rstd["mq"], 1)
            for t in range(TILES):
                step(normed(mq[:, t], psum[:, MQ_BANKS[t], 0:256], rs_mq[:, 4 * t:4 * t + 4], rs_x[:, t:t + 1], 4))
                V.tensor_tensor(heads(mq[:, t], 4), heads(mq[:, t], 4), over_heads(parameter("mem_q"), 4), ALU.mult
                                ).then_inc(mq_ready, 1)
            head_sums("mk", tmpA[:, 0:512], ss_mk, 2, 8)
            dve.wait_ge(rstd["mk"], 1)
            dve.wait_ge(mv_ready, 2)
            for t in range(TILES):
                step(normed(mk[:, t], psum[:, 5 + t, 0:256], rs_mk[:, 4 * t:4 * t + 4], rs_mem[:, t:t + 1], 4))
                V.tensor_tensor(heads(mk[:, t], 4), heads(mk[:, t], 4), over_heads(parameter("mem_k"), 4), ALU.mult
                                ).then_inc(mk_ready, 1)

            def rotate(dst, src, swapped, cos, sin, n):
                src, dst, swapped = heads(src, n), heads(dst, n), heads(swapped, n)
                for lo, hi in ((0, 32), (32, 64)):
                    last = V.tensor_tensor(swapped[:, :, lo:hi], src[:, :, 32 - lo:64 - lo],
                                           over_heads(sin[:, lo:hi], n), ALU.mult)
                step(last)
                step(V.tensor_tensor(dst, src, over_heads(cos, n), ALU.mult))
                return V.tensor_tensor(dst, dst, swapped, ALU.add)

            head_sums("swa", tmpB[:, 0:768], ss_s, 2, 12)
            dve.wait_ge(rstd["swa"], 1)
            dve.wait_ge(sv_ready, 2)
            for t in range(TILES):
                rs = rs_s[:, 6 * t:6 * t + 6]
                step(V.tensor_scalar(rs, rs, rs_x[:, t:t + 1], None, ALU.mult))
                V.tensor_tensor(sqk[:, t, 0:256].rearrange("p (b a d) -> p a b d", a=2, b=2),
                                psum[:, t, 0:256].rearrange("p (a b d) -> p a b d", a=2, b=2),
                                rs[:, 0:4].rearrange("p (a b) -> p a b", a=2).unsqueeze(3).to_broadcast([P, 2, 2, DH]),
                                ALU.mult)
                step(V.tensor_tensor(heads(sqk[:, t, 256:384], 2), heads(psum[:, t, 256:384], 2),
                                     per_head(rs[:, 4:6], 2), ALU.mult))
                step(V.tensor_tensor(heads(sqk[:, t], 6), heads(sqk[:, t], 6), swa_gain[:], ALU.mult))
                rotate(sqk[:, t], sqk[:, t], rope_s[:, t], cos2[:, t], sin2[:, t], 6).then_inc(swa_qk_ready, 1)
            dve.wait_ge(rotation_ready, 1)
            for t in range(TILES):
                dve.wait_ge(rqk_done, t + 1)
                rotate(rqk[:, t], psum[:, 3 + t], rope_r[:, t], cosr[:, t], sinr[:, t], 8).then_inc(rqk_ready, 1)

            def gate(t):
                dve.wait_ge(rg_sig, t + 1)
                V.scalar_tensor_tensor(out=rg[:, t], in0=psum[:, 3 + t], scalar=rs_x[:, t:t + 1], in1=rg[:, t],
                                       op0=ALU.mult, op1=ALU.mult).then_inc(rg_ready, 1)

            gate(0)
            for h in range(MEM_HEADS):
                dve.wait_ge(mem_scored, h + 1)
                step(V.tensor_reduce(mem_max[:, 2 * h:2 * h + 2], psum[:, HEAD_BANKS[h]].rearrange("p (t n) -> p t n", t=2),
                                     AX_X, ALU.max))
                V.tensor_scalar(mem_neg[:, 2 * h:2 * h + 2], mem_max[:, 2 * h:2 * h + 2], -SCALE, None, ALU.mult
                                ).then_inc(mem_max_ready, 1)
            for h in range(MEM_HEADS):
                dve.wait_ge(mem_exp, 2 * h + 2)
                step(V.reciprocal(mem_inv[:, 2 * h:2 * h + 2], mem_sum[:, 2 * h:2 * h + 2]))
                for t in range(TILES):
                    V.tensor_scalar(memP[:, h, t], memP[:, h, t], mem_inv[:, 2 * h + t:2 * h + t + 1], None, ALU.mult
                                    ).then_inc(memP_ready, 1)
            def by_chunk(a):
                return a.rearrange("p (c m) -> p c m", m=CHUNK)

            for h in range(SWA_HEADS):
                dve.wait_ge(swa_scored, h + 1)
                step(V.scalar_tensor_tensor(out=by_chunk(swaP[:, h]), in0=by_chunk(psum[:, HEAD_BANKS[h], 0:3 * P]),
                                            scalar=SCALE, in1=constant("band").unsqueeze(2).to_broadcast([P, 6, CHUNK]),
                                            op0=ALU.mult, op1=ALU.add))
                V.tensor_reduce(swa_max[:, 2 * h:2 * h + 1], swaP[:, h, 0:P], AX_X, ALU.max)
                step(V.tensor_reduce(swa_max[:, 2 * h + 1:2 * h + 2], swaP[:, h, P:3 * P], AX_X, ALU.max))
                V.tensor_scalar(swa_neg[:, 2 * h:2 * h + 2], swa_max[:, 2 * h:2 * h + 2],
                                parameter("sinks")[:, h:h + 1], -1.0, ALU.max, ALU.mult).then_inc(swa_max_ready, 1)
            dve.wait_ge(decay_ready, RET_HEADS)
            for h in range(RET_HEADS):
                if h == 2:
                    gate(1)
                dve.wait_ge(ret_scored, h + 1)
                V.scalar_tensor_tensor(out=retP[:, h], in0=psum[:, RET_BANKS[h], 0:3 * P], scalar=SCALE,
                                       in1=decay[:, h], op0=ALU.mult, op1=ALU.mult).then_inc(retP_ready, 1)
            for h in range(SWA_HEADS):
                dve.wait_ge(swa_exp, 4 * h + 4)
                step(V.tensor_tensor(swa_inv[:, 2 * h:2 * h + 2], swa_sum[:, 2 * h:2 * h + 2],
                                     swa_sink[:, 2 * h:2 * h + 2], ALU.add))
                step(V.reciprocal(swa_inv[:, 2 * h:2 * h + 2], swa_inv[:, 2 * h:2 * h + 2]))
                for t, (lo, hi) in enumerate(((0, P), (P, 3 * P))):
                    V.tensor_scalar(swaP[:, h, lo:hi], swaP[:, h, lo:hi], swa_inv[:, 2 * h + t:2 * h + t + 1], None,
                                    ALU.mult).then_inc(swaP_ready, 1)
            for t in range(TILES):
                head_sums("ret", tmpA[:, t * N:(t + 1) * N], ss_ret[:, 4 * t:4 * t + 4], t + 1, 4)
            for t in range(TILES):
                dve.wait_ge(rstd["ret"], t + 1)
                o = tmpB[:, t * N:(t + 1) * N]
                step(V.tensor_tensor(heads(o, 4), heads(psum[:, RET_O_BANKS[t]], 4),
                                     per_head(rs_ret[:, 4 * t:4 * t + 4], 4, RET_DV), ALU.mult))
                V.tensor_tensor(o, o, rg[:, t], ALU.mult).then_inc(ret_gated, 1)
            dve.wait_ge(cat_ret, 2)
            V.memset(back, 0.0)
            V.memset(Y, 0.0).then_inc(y_ready, 2)
            def add_mixed(c):
                n, t = c // 2, c % 2
                part = xy[:, t, n * N:(n + 1) * N]
                dve.wait_ge(mixed, c + 1)
                V.tensor_tensor(part, psum[:, MIXED_BANKS[c]], part, ALU.add).then_inc(x2_ready, 1)

            def take_h2(c):
                i, t = c // 2, c % 2
                dve.wait_ge(h2_turned, c + 1)
                turned_gain(hT[:, 4 * i:4 * i + 4, t * P:(t + 1) * P], psum[:, H2_BANKS[c]], 2 * KD, 4 * i, 4, P
                            ).then_inc(h2T_ready, 1)

            def choose(t):
                dve.wait_ge(routed, t + 1)
                dve.wait_ge(rstd["ffn"], t + 1)
                step(V.scalar_tensor_tensor(out=logits[:, t], in0=psum[:, ROUTE_BANKS[t], 0:E], scalar=rs_ffn[:, t:t + 1],
                                            in1=parameter("b_router"), op0=ALU.mult, op1=ALU.add))
                step(V.max(top_v[:, t], logits[:, t]))
                V.tensor_scalar(top_neg[:, t:t + 1], top_v[:, t, 0:1], -1.0, None, ALU.mult).then_inc(top_ready, 1)
                step(V.max_index(top_i[:, t], top_v[:, t], logits[:, t]))
                step(V.tensor_copy(top_x[:, t], top_i[:, t, 0:TOP_K]))
                step(V.tensor_tensor(hits[:, t], constant("iota")[:, 0:E].unsqueeze(1).to_broadcast([P, TOP_K, E]),
                                     top_x[:, t].unsqueeze(2).to_broadcast([P, TOP_K, E]), ALU.is_equal))
                V.tensor_reduce(chosen[:, t], hits[:, t].rearrange("p j e -> p e j"), AX_X, ALU.add
                                ).then_inc(chosen_ready, 1)

            def weigh(t):
                dve.wait_ge(top_exp, t + 1)
                step(V.reciprocal(top_inv[:, t:t + 1], top_sum[:, t:t + 1]))
                step(V.tensor_scalar(top_g[:, t], top_g[:, t], top_inv[:, t:t + 1], None, ALU.mult))
                step(V.tensor_tensor(hitg[:, t], hits[:, t], top_g[:, t].unsqueeze(2).to_broadcast([P, TOP_K, E]),
                                     ALU.mult))
                V.tensor_reduce(gates[:, t], hitg[:, t].rearrange("p j e -> p e j"), AX_X, ALU.add
                                ).then_inc(gates_ready, 1)

            def build_whose(p):
                V.tensor_scalar(whose.rearrange("p (e s) -> p e s", e=2),
                                constant("half").unsqueeze(2).to_broadcast([P, 2, SLOTS]), constant("row")[:, bass.ds(p, 1)], None,
                                ALU.is_equal).then_inc(whose_ready, 1)

            build_whose(0)
            add_mixed(0)
            add_mixed(1)
            take_h2(0)
            take_h2(1)
            add_mixed(2)
            take_h2(2)
            choose(0)
            add_mixed(3)
            take_h2(3)
            weigh(0)
            V.memset(place[:, :, BLOCKS * E:], -FAR)
            choose(1)
            dve.wait_ge(placed, 1)
            step(V.scalar_tensor_tensor(out=logits, in0=psum[:, 5, 64:128].rearrange("p (t e) -> p t e", t=TILES),
                                        scalar=1.0, in1=chosen, op0=ALU.add, op1=ALU.mult))
            step(V.tensor_scalar(place[:, :, 0:E], logits, -1.0, None, ALU.add))

            def build_sel(q):
                for t in range(TILES):
                    for e in range(2):
                        last = V.tensor_scalar(sel[:, t, e * SLOTS:(e + 1) * SLOTS], constant("iota"),
                                               place[:, t, bass.ds(2 * q + e, 1)], None, ALU.is_equal)
                last.then_inc(sel_ready, 1)

            def build_gated(q, p):
                for t in range(TILES):
                    for e in range(2):
                        last = V.tensor_scalar(gated[:, t, e * SLOTS:(e + 1) * SLOTS], constant("iota"),
                                               place[:, t, bass.ds(2 * q + e, 1)], gates[:, t, bass.ds(2 * p + e, 1)],
                                               ALU.is_equal, ALU.mult)
                last.then_inc(gated_ready, 1)

            def take_gathered(q, i):
                dve.wait_ge(gathered, 2 * q + (i + 1))
                turned_gain(XT[:, 4 * i:4 * i + 4], psum[:, 6 + i], 2 * KD, 4 * i, 4, P).then_inc(xt_ready, 1)

            def add_combined(q, c, banks=(6, 7, 6, 7)):
                n, t = c // 2, c % 2
                dve.wait_ge(combined, 4 * q + (c + 1))
                part = xy[:, t, n * N:(n + 1) * N]
                V.tensor_tensor(part, psum[:, banks[c]], part, ALU.add).then_inc(y_added, 1)

            build_sel(0)
            for b in range(1, BLOCKS):
                V.tensor_scalar(place[:, :, b * E:(b + 1) * E], logits, -1.0 - b * SLOTS, None, ALU.add)
            weigh(1)
            take_gathered(0, 0)
            dve.wait_ge(counted, 1)
            step(V.tensor_reduce(count_f, psum[:, 4, 256:256 + E], AX_X, ALU.max))
            V.tensor_copy(count_i[:], count_f[0:1]).then_inc(count_ready, 1)
            take_gathered(0, 1)

            def lin_times_glu(part):
                V.scalar_tensor_tensor(out=lin[:, part], in0=lin[:, part], scalar=1.0, in1=glu[:, part],
                                       op0=ALU.add, op1=ALU.mult).then_inc(lin1_ready, 1)

            def pair(q, p):
                dve.wait_ge(gathered, 2 * q + 2)
                build_sel(q + 1)
                dve.wait_ge(back_ready, q + 1)
                build_gated(q, p)
                dve.wait_ge(biased, q + 1)
                build_whose(p + 1)
                for c in range(4):
                    add_combined(q, c)
                parts = [slice(i * N, (i + 1) * N) for i in range(2)]
                for i, part in enumerate(parts):
                    dve.wait_ge(up_done, 4 * q + (2 * i + 1))
                    V.tensor_scalar(glu[:, part], psum[:, i], LIMIT, None, ALU.min).then_inc(glu_ready, 1)
                    dve.wait_ge(up_done, 4 * q + (2 * i + 2))
                    V.tensor_scalar(lin[:, part], psum[:, 2 + i], LIMIT, -LIMIT, ALU.min, ALU.max).then_inc(up_read, 1)
                    if i == 0:
                        dve.wait_ge(up_read, 2 * q + 1)
                        lin_times_glu(parts[0])
                dve.wait_ge(lin1_ready, 2 * q + 1)
                dve.wait_ge(sig_ready, 2 * q + 1)
                V.tensor_tensor(sig[:, parts[0]], lin[:, parts[0]], sig[:, parts[0]], ALU.mult).then_inc(act_ready, 1)
                dve.wait_ge(up_read, 2 * q + 2)
                lin_times_glu(parts[1])
                dve.wait_ge(lin1_ready, 2 * q + 2)
                dve.wait_ge(sig_ready, 2 * q + 2)
                V.tensor_tensor(sig[:, parts[1]], lin[:, parts[1]], sig[:, parts[1]], ALU.mult).then_inc(act_ready, 1)
                for i in range(2):
                    take_gathered(q + 1, i)

            with dve.Fori(0, PAIRS) as q:
                pair(q, q)
            with dve.If(overflowing(dve)):
                further_blocks(dve, pair)
                for c in range(4):
                    add_combined(BLOCKS * PAIRS, c, LAST_BANKS)
            with dve.Else():
                for c in range(4):
                    add_combined(PAIRS, c, LAST_BANKS)

        @block.tensor
        def _(pe):
            def turn(dst, src):
                n = src.shape[0]
                return pe.transpose(dst, src, ident[0:n, 0:n])

            pe.wait_ge(const_in, 16)
            pe.wait_ge(ones_ready, 1)
            pe.wait_ge(params_in, 32)
            turn(psum[:, 7, 0:3 * KD], norm_rows).then_inc(params_spread, 1)
            pe.matmul(psum[:, 7, 64:64 + ROW_COLS], ones[0:1, :], param_row, start=True, stop=True
                      ).then_inc(params_spread, 1)

            def turn_rows(src, banks, arrived, done):
                for t in range(TILES):
                    pe.wait_ge(arrived[t], 16)
                    for k in range(KD):
                        c = (k % 2) * 256 + t * P
                        mm = turn(psum[:, banks[k // 2], c:c + P], src[:, t, k * P:(k + 1) * P])
                        if t == TILES - 1 and k % 2 == 1:
                            mm.then_inc(done, 1)

            turn_rows(xy, (3, 4, 5, 6), x_in, x_turned)
            pe.wait_ge(params_ready, 2)
            pe.wait_ge(landed[2], 16)
            for t in range(TILES):
                for k in range(KD):
                    if t == 0 and k % 2 == 0:
                        pe.wait_ge(hT_ready, k // 2 + 1)
                    mm = pe.matmul(psum[:, MQ_BANKS[t], 0:256], hT[:, k, t * P:(t + 1) * P], w_mq_sb[:, k],
                                   start=k == 0, stop=k == KD - 1)
                mm.then_inc(mq_done, 1)
            turn_rows(mem_sb, MEMT_BANKS, mem_in, mem_turned)
            pe.wait_ge(landed[0], 16)
            for t in range(TILES):
                for k in range(KD):
                    if t == 0:
                        pe.wait_ge(memT_ready, k + 1)
                    mm = pe.matmul(psum[:, 5 + t], memT[:, k, t * P:(t + 1) * P], w_mem_sb[:, k],
                                   start=k == 0, stop=k == KD - 1)
                mm.then_inc(mkv_done, 1)

            def project(n, t, b, done, steps=range(KD), used=0):
                pe.wait_ge(landed[GROUP_SLOTS[n]], 16)
                for k in steps:
                    mm = pe.matmul(psum[:, b], hT[:, k, t * P:(t + 1) * P], w_group_sb[n][:, k],
                                   start=k == 0, stop=k == KD - 1)
                    if used and k == steps[0]:
                        mm.then_inc(slot_used, used)
                if k == KD - 1:
                    mm.then_inc(done, 1)

            project(3, 0, 0, swa_done, used=2)
            project(3, 1, 1, swa_done)
            project(0, 0, 3, rqk_done, used=1)
            project(0, 1, 4, rqk_done)
            for t in range(TILES):
                pe.wait_ge(mq_ready, t + 1)
                project(1, t, RV_BANKS[t], rv_done, used=1 - t)

            def turn_heads(src, b, groups, done):
                for g in range(groups):
                    for t in range(TILES):
                        c = g * 256 + t * P
                        mm = turn(psum[:, b, c:c + P], src(t, g))
                mm.then_inc(done, 1)

            pe.wait_ge(mk_ready, 2)
            pe.wait_ge(mv_ready, 2)
            turn_heads(lambda t, g: mk[:, t, g * P:(g + 1) * P], 5, 2, turnedA)
            turn_heads(lambda t, g: mq[:, t, g * P:(g + 1) * P], 6, 2, turnedA)
            pe.wait_ge(swa_qk_ready, 2)
            pe.wait_ge(sv_ready, 2)
            turn_heads(lambda t, g: sqk[:, t, g * P:(g + 1) * P], 0, 2, turnedA)
            turn_heads(lambda t, g: sqk[:, t, 256:384], 1, 1, turnedA)
            pe.wait_ge(rqk_ready, 1)
            project(2, 0, 3, rg_done, used=1)
            pe.wait_ge(turnsA_ready, 4)
            for h in range(MEM_HEADS):
                r = DH * (h % 2)
                for t in range(TILES):
                    mm = pe.matmul(psum[:, HEAD_BANKS[h], t * 256:(t + 1) * 256], mqT[r:r + DH, h // 2, t * P:(t + 1) * P],
                                   mkT[r:r + DH, h // 2, :], start=True, stop=True)
                mm.then_inc(mem_scored, 1)
            pe.wait_ge(rqk_ready, 2)
            project(2, 1, 4, rg_done, range(4))
            pe.wait_ge(rv_ready, 2)
            turn_heads(lambda t, g: rqk[:, t, g * P:(g + 1) * P], 2, 2, turnedB)
            turn_heads(lambda t, g: rqk[:, t, (2 + g) * P:(3 + g) * P], 7, 2, turnedB)
            for h in range(SWA_HEADS):
                pe.wait_ge(mem_exp, 2 * h + 2)
                r = DH * (h // 2)
                for t in range(TILES):
                    mm = pe.matmul(psum[:, HEAD_BANKS[h], t * P:(2 * t + 1) * P], sqT[r:r + DH, h % 2, t * P:(t + 1) * P],
                                   skT[r:r + DH, 0:(t + 1) * P], start=True, stop=True)
                mm.then_inc(swa_scored, 1)
            project(2, 1, 4, rg_done, range(4, KD))
            def score_ret(h):
                r = DH * (h % 2)
                mm = pe.matmul(psum[:, RET_BANKS[h], 0:256], rkT[r:r + DH, h // 2, 0:P], rqT[r:r + DH, h // 2, :],
                               start=True, stop=True)
                if h == 0:
                    mm.then_inc(slot_used, 1)
                pe.matmul(psum[:, RET_BANKS[h], 256:384], rkT[r:r + DH, h // 2, P:2 * P], rqT[r:r + DH, h // 2, P:2 * P],
                          start=True, stop=True).then_inc(ret_scored, 1)

            pe.wait_ge(turnsB_ready, 2)
            pe.wait_ge(rg_ready, 1)
            for h in range(3):
                score_ret(h)
            for h in range(MEM_HEADS):
                pe.wait_ge(memP_ready, 2 * h + 2)
                pe.wait_ge(swa_max_ready, h + 1)
                for b in range(2):
                    for t in range(TILES):
                        c = b * 256 + t * P
                        mm = turn(psum[:, HEAD_BANKS[h], c:c + P], memP[:, h, t, b * P:(b + 1) * P])
                mm.then_inc(memP_turned, 1)
            pe.wait_ge(rg_ready, 2)
            score_ret(3)
            pe.wait_ge(retP_ready, 4)
            for h in range(RET_HEADS):
                mm = pe.matmul(psum[:, RET_O_BANKS[0], h * P:(h + 1) * P], retP[:, h, 0:P], rv[:, 0, h * P:(h + 1) * P],
                               start=True, stop=True)
            mm.then_inc(ret_read, 1)
            for h in range(RET_HEADS):
                pe.matmul(psum[:, RET_O_BANKS[1], h * P:(h + 1) * P], retP[:, h, P:2 * P], rv[:, 0, h * P:(h + 1) * P],
                          start=True, stop=False)
                mm = pe.matmul(psum[:, RET_O_BANKS[1], h * P:(h + 1) * P], retP[:, h, 2 * P:3 * P],
                               rv[:, 1, h * P:(h + 1) * P], start=False, stop=True)
            mm.then_inc(ret_read, 1)
            for g in range(2):
                pe.wait_ge(memPT_ready, 2 * g + 2)
                for b in range(2):
                    for r in range(2):
                        h = 2 * g + r
                        mm = pe.matmul(psum[r * DH:(r + 1) * DH, 3, g * 256:(g + 1) * 256], mv[:, b, h * DH:(h + 1) * DH],
                                       memPT[:, h, b], start=b == 0, stop=b == 1)
            mm.then_inc(mem_read, 1)
            for h in range(SWA_HEADS):
                pe.wait_ge(swaP_ready, 2 * h + 2)
                pe.wait_ge(memPT_ready, h + 1)
                for c in range(3):
                    mm = turn(psum[:, HEAD_BANKS[h], c * P:(c + 1) * P], swaP[:, h, c * P:(c + 1) * P])
                mm.then_inc(swaP_turned, 1)
            for g in range(2):
                pe.wait_ge(swaPT_ready, 2 * g + 2)
                for c, (t, b) in enumerate(((0, 0), (1, 0), (1, 1))):
                    for r in range(2):
                        h = 2 * g + r
                        first = g * 256 + t * P
                        mm = pe.matmul(psum[r * DH:(r + 1) * DH, 4, first:first + P], sv[:, b, g * DH:(g + 1) * DH],
                                       swaPT[:, h, c * P:(c + 1) * P], start=b == 0, stop=b == t)
            mm.then_inc(swa_read, 1)
            def mix(c, steps):
                n, t = c // 2, c % 2
                for i in steps:
                    k = (6, 7, 4, 5, 0, 1, 2, 3)[i]
                    if i == 4 and n == 0:
                        pe.wait_ge(cat_ret, t + 1)
                    mm = pe.matmul(psum[:, MIXED_BANKS[c]], catT[:, k, t * P:(t + 1) * P],
                                   w_out_sb[n][:, k], start=i == 0, stop=i == KD - 1)
                if i == KD - 1:
                    mm.then_inc(mixed, 1)

            def turn_h2(c):
                i, t = c // 2, c % 2
                pe.wait_ge(x2_ready, c + 1)
                for k in range(4):
                    first = (4 * i + k) * P
                    mm = turn(psum[:, H2_BANKS[c], k * P:(k + 1) * P], xy[:, t, first:first + P])
                    if k == 0 and c in (1, 3):
                        mm.then_inc(slot_used, 1)
                mm.then_inc(h2_turned, 1)

            def route(t):
                for k in range(KD):
                    if k % 4 == 0:
                        pe.wait_ge(h2T_ready, 2 * (k // 4) + t + 1)
                    mm = pe.matmul(psum[:, ROUTE_BANKS[t], 0:E], hT[:, k, t * P:(t + 1) * P], wr[:, k],
                                   start=k == 0, stop=k == KD - 1)
                mm.then_inc(routed, 1)

            pe.wait_ge(swaPT_ready, 4)
            pe.wait_ge(landed[0], 32)
            pe.wait_ge(cat_mem, 1)
            mix(0, range(2))
            for t in range(TILES):
                pe.wait_ge(ret_gated, t + 1)
                for h in range(RET_HEADS):
                    c = t * N + h * P
                    mm = turn(psum[:, 5 + t, h * P:(h + 1) * P], tmpB[:, c:c + P])
                mm.then_inc(ret_turned, 1)
            pe.wait_ge(cat_swa, 1)
            pe.wait_ge(router_in, 16)
            mix(0, range(2, 8))
            mix(1, range(8))
            pe.wait_ge(landed[1], 32)
            turn_h2(0)
            mix(2, range(2))
            turn_h2(1)
            mix(2, range(2, 8))
            mix(3, range(2))
            turn_h2(2)
            mix(3, range(2, 5))
            route(0)
            mix(3, range(5, 8))
            turn_h2(3)
            route(1)

            def bias(p, banks, start=False):
                for n in banks:
                    rows = slice(n * E, (n + 1) * E)
                    mm = pe.matmul(psum[:, n], whose[rows, :], bup_rows[rows, :], start=start, stop=False,
                                   skip_group_check=True)
                return mm

            def gather(q, ks=range(KD)):
                pe.wait_ge(sel_ready, q + 1)
                for k in ks:
                    c = (k % 4) * P
                    for t in range(TILES):
                        mm = pe.matmul(psum[:, 6 + k // 4, c:c + P], xn[:, t, k * P:(k + 1) * P], sel[:, t],
                                       start=t == 0, stop=t == TILES - 1)
                    if k % 4 == 3:
                        mm.then_inc(gathered, 1)

            pe.wait_ge(bup_in, 16 * 4)
            pe.wait_ge(whose_ready, 1)
            bias(0, (0, 1), start=True)
            pe.wait_ge(chosen_ready, 2)
            pe.matmul(psum[:, 5, 64:128], constant("before"), chosen.rearrange("p t e -> p (t e)"), start=True, stop=False)
            pe.matmul(psum[:, 5, 96:128], ones[:], chosen[:, 0], start=False, stop=True).then_inc(placed, 1)
            bias(0, (2, 3), start=True).then_inc(biased, 1)
            pe.wait_ge(xn2_ready, 2)
            gather(0, range(KD // 2))
            pe.matmul(psum[:, 4, 256:256 + E], ones[:], chosen[:, 0], start=True, stop=False)
            pe.matmul(psum[:, 4, 256:256 + E], ones[:], chosen[:, 1], start=False, stop=True).then_inc(counted, 1)

            def turn_gates():
                pe.wait_ge(count_ready, 1)
                pe.wait_ge(gates_ready, TILES)
                for t in range(TILES):
                    mm = turn(psum[0:E, 4, t * P:(t + 1) * P], gates[:, t])
                mm.then_inc(gates_turned, 1)

            def combine(q, c, banks=(6, 7, 6, 7)):
                n, t = c // 2, c % 2
                pe.matmul(psum[:, banks[c]], back[:, t], Y[:, n * N:(n + 1) * N], start=True, stop=True
                          ).then_inc(combined, 1)

            def pair(h, expert_h, u, first=False):
                q = h * 2 + u
                p = expert_h * 2 + u
                if not first:
                    pe.wait_ge(up_read, 2 * q)
                order = list(range(UP_CHUNKS))
                if first:
                    order.remove(OUTSIDE_UP)
                    order.insert(UP_CHUNKS - 2, OUTSIDE_UP)
                for i, j in enumerate(order):
                    if i == 0:
                        pe.wait_ge(xt_ready, 2 * q + 1)
                    elif j == UP_CHUNKS // 2:
                        pe.wait_ge(xt_ready, 2 * q + 2)
                    if first and i == 1:
                        gather(0, range(KD // 2, KD))
                        turn_gates()
                    if i == 2 and not first:
                        pe.wait_ge(whose_ready, q + 1)
                        bias(p, range(4)).then_inc(biased, 1)
                    elif i == 4:
                        pe.wait_ge(xt_ready, 2 * q + 2)
                        pe.wait_ge(y_ready, 2 * q + 2)
                        pe.wait_ge(back_ready, q + 1)
                        if first:
                            pe.wait_ge(bdown_in, 16)
                        combine(q, 0)
                        combine(q, 1)
                    elif i == 5:
                        for c in (2, 3):
                            pe.wait_ge(y_added, 4 * q + (c - 1))
                            combine(q, c)
                    if first and j == OUTSIDE_UP:
                        pe.wait_ge(outside_up_in, 16 * 2)
                        weights = outside_up
                    else:
                        slot = chunk_landed(pe, h, u, j, first)
                        weights = [slot[:, e * 2 * F:(e + 1) * 2 * F] for e in range(2)]
                    last = i == UP_CHUNKS - 1
                    for n in (0, 2, 1, 3):
                        for e in range(2):
                            r = e * SLOTS
                            mm = pe.matmul(psum[r:r + SLOTS, n], XT[:, j, r:r + SLOTS], weights[e][:, n * N:(n + 1) * N],
                                           start=i == 0 and not first, stop=last, skip_group_check=True)
                        if last:
                            mm.then_inc(up_done, 1)
                    if not last and not (first and j == OUTSIDE_UP):
                        mm.then_inc(slot_used, 1)
                pe.wait_ge(gated_ready, q + 1)
                turn(psum[:, 4, 0:P], gated[:, 0]).then_inc(slot_used, 1)
                turn(psum[:, 4, P:2 * P], gated[:, 1]).then_inc(gated_turned, 1)
                pe.wait_ge(y_added, 4 * q + 4)
                gather(q + 1)
                for i in range(2):
                    pe.wait_ge(act_ready, 2 * q + (i + 1))
                    for k in range(4):
                        j = 4 * i + k
                        column = 256 * (j // 2) + j % 2
                        mm = turn(psum[:, i, k * P:(k + 1) * P], sig[:, column:column + 255:2])
                    mm.then_inc(act_turned, 1)
                pe.wait_ge(back_ready, q + 2)
                for i in range(DOWN_CHUNKS):
                    if i % 2 == 0:
                        pe.wait_ge(actT_ready, 2 * q + (i // 2 + 1))
                    outside = first and UP_CHUNKS + i == OUTSIDE_DOWN
                    last = i == DOWN_CHUNKS - 1
                    slot = slots[in_ring(u, UP_CHUNKS + i, first)[0]]
                    if outside:
                        pe.wait_ge(outside_down_in, 16)
                        slot = outside_down
                    elif last:
                        pe.wait_ge(last_half_in, 16 * q + 16)
                    else:
                        chunk_landed(pe, h, u, UP_CHUNKS + i, first)
                    weights = [slot[:, e * 2 * F:(e + 1) * 2 * F] for e in range(2)]
                    for k in range(2):
                        if last and k == 1:
                            chunk_landed(pe, h, u, UP_CHUNKS + i, first)
                        for n in range(2):
                            for e in range(2):
                                r = e * SLOTS
                                mm = pe.matmul(psum[r:r + SLOTS, 4 + n], actT[:, 2 * i + k, r:r + SLOTS],
                                               weights[e][:, k * D + n * N:k * D + (n + 1) * N],
                                               start=i == 0 and k == 0, stop=last and k == 1)
                            if last and k == 1 and n == 0:
                                mm.then_inc(down_half, 1)
                    if not outside:
                        mm.then_inc(slot_used, 1)

            def last_share(q_end):
                pe.wait_ge(back_ready, q_end + 1)
                for c in range(4):
                    pe.wait_ge(y_ready, 2 * q_end + (c // 2 + 1))
                    combine(q_end, c, LAST_BANKS)

            pair(0, 0, 0, True)
            pair(0, 0, 1)
            with pe.Fori(1, PAIRS // 2) as h:
                for u in range(2):
                    pair(h, h, u)
            with pe.If(overflowing(pe)):
                further_twos(pe, pair)
                last_share(BLOCKS * PAIRS)
            with pe.Else():
                last_share(PAIRS)


def kernel(**inputs):
    import concourse.bacc as bacc
    from concourse.bass_utils import run_bass_kernel_spmd

    nc = bacc.Bacc("TRN2", target_bir_lowering=False, num_devices=1)
    a = {name: np.asarray(value) for name, value in inputs.items()}
    gains = [a[name].reshape(-1, P) for name in ("g_mix", "g_mem", "g_ffn")]
    params = [a[name] for name in ("swa_q_gain", "swa_k_gain", "mem_q_gain", "mem_k_gain", "swa_sinks", "b_router")]
    arrays = {
        "x": a["x"], "mem": a["mem"], "positions": a["positions"].reshape(-1, P).T,
        "norm_gains": np.concatenate(gains, 0), "w_in": a["w_in"], "w_mem_kv": a["w_mem_kv"],
        "small_params": np.concatenate(params, 1), "w_out": a["w_out"], "w_router": a["w_router"],
        "w_up": a["w_up"], "b_up": a["b_up"], "w_down": a["w_down"], "b_down": a["b_down"],
        "constants": shape_constants(a["w_router"].shape[2]),
    }
    arrays = {name: np.ascontiguousarray(value) for name, value in arrays.items()}
    args = [nc.dram_tensor(f"in_{name}", a.shape, mybir.dt.from_np(a.dtype), kind="ExternalInput").ap()
            for name, a in arrays.items()]
    out = nc.dram_tensor("out_0", arrays["x"].shape, F32, kind="ExternalOutput").ap()
    layer_kernel(nc, *args, out)
    result = run_bass_kernel_spmd(nc, [{f"in_{name}": a for name, a in arrays.items()}], core_ids=[0])
    return result.results[0]["out_0"]
```
